# Optimizing a Trainium2 kernel written in Bass

```python
import jax, jax.numpy as jnp
from jax import lax
import numpy as np
import jax
import jax.numpy as jnp

D_MODEL = 1024
BATCH = 1
SEQ = 512
DEPTH = 1

M_HEADS = 4
M_HEAD_DIM = 128
M_WIDTH = M_HEADS * M_HEAD_DIM
CONV_W = 4
CHUNK = 128
A_HEADS = 8
A_HEAD_DIM = 64
A_WIDTH = A_HEADS * A_HEAD_DIM
DIL_PATTERNS = ((128, 1), (512, 4), (2048, 16))
N_BUCKETS = 32
MAX_DISTANCE = 2048
MIX_WIDTH = M_WIDTH + A_WIDTH
IN_SIZES = (M_WIDTH, M_WIDTH, M_WIDTH, M_HEADS, M_HEADS, A_WIDTH, A_WIDTH, A_WIDTH)
IN_COLS = 3 * M_WIDTH + 2 * M_HEADS + 3 * A_WIDTH
PEER_HEADS = 8
N_KEYS = 128
N_EXPERTS = N_KEYS * N_KEYS
PEER_QDIM = 256
PEER_TOPK = 16
PEER_BLOCK = 128
EPS = 1e-6


def rms_norm(x, g):
    xf = x.astype(jnp.float32)
    y = xf * lax.rsqrt(jnp.mean(xf * xf, axis=-1, keepdims=True) + EPS)
    return (y * g).astype(x.dtype)

def t5_bucket(dist):
    max_exact = N_BUCKETS // 2
    nf = jnp.maximum(dist, 1).astype(jnp.float32)
    large = max_exact + (jnp.log(nf / max_exact) / np.log(MAX_DISTANCE / max_exact)
                         * (N_BUCKETS - max_exact)).astype(jnp.int32)
    large = jnp.minimum(large, N_BUCKETS - 1)
    return jnp.where(dist < max_exact, dist, large)

def causal_short_conv(u, w, b):
    y = lax.conv_general_dilated(u, w[:, None, :], window_strides=(1,),
                                 padding=[(CONV_W - 1, 0)],
                                 dimension_numbers=('NWC', 'WIO', 'NWC'),
                                 feature_group_count=u.shape[-1])
    return y + b

def mlstm_chunkwise(q, k, v, ipre, fpre):
    B, H, S, Dh = q.shape
    nc = S // CHUNK
    q = q.reshape(B, H, nc, CHUNK, Dh)
    k = k.reshape(B, H, nc, CHUNK, Dh)
    v = v.reshape(B, H, nc, CHUNK, Dh)
    logi = ipre.reshape(B, H, nc, CHUNK)
    b = jnp.cumsum(jax.nn.log_sigmoid(fpre).reshape(B, H, nc, CHUNK), axis=-1)
    b_last = b[..., -1]
    g = b_last[..., None] - b + logi
    m_loc = jnp.max(g, axis=-1)
    wts = jnp.exp(g - m_loc[..., None])
    c_chunk = jnp.einsum('bhnl,bhnlk,bhnlv->bhnkv', wts, k, v)
    n_chunk = jnp.einsum('bhnl,bhnlk->bhnk', wts, k)

    def step(carry, inp):
        C, n, m = carry
        bl, ml, cc, nn = inp
        m_new = jnp.maximum(bl + m, ml)
        a = jnp.exp(bl + m - m_new)
        bb = jnp.exp(ml - m_new)
        C_new = a[..., None, None] * C + bb[..., None, None] * cc
        n_new = a[..., None] * n + bb[..., None] * nn
        return (C_new, n_new, m_new), (C, n, m)

    init = (jnp.zeros((B, H, Dh, Dh), jnp.float32), jnp.zeros((B, H, Dh), jnp.float32),
            jnp.zeros((B, H), jnp.float32))
    xs = (jnp.moveaxis(b_last, 2, 0), jnp.moveaxis(m_loc, 2, 0),
          jnp.moveaxis(c_chunk, 2, 0), jnp.moveaxis(n_chunk, 2, 0))
    _, (C_prev, n_prev, m_prev) = lax.scan(step, init, xs)
    C_prev = jnp.moveaxis(C_prev, 0, 2)
    n_prev = jnp.moveaxis(n_prev, 0, 2)
    m_prev = jnp.moveaxis(m_prev, 0, 2)

    causal = jnp.tril(jnp.ones((CHUNK, CHUNK), bool))
    log_d = jnp.where(causal, b[..., :, None] - b[..., None, :] + logi[..., None, :], -jnp.inf)
    inter = b + m_prev[..., None]
    m_t = jnp.maximum(inter, jnp.max(log_d, axis=-1))
    d_mat = jnp.exp(log_d - m_t[..., None])
    inter_w = jnp.exp(inter - m_t)
    s = jnp.einsum('bhnqd,bhnkd->bhnqk', q, k) * d_mat
    num = (jnp.einsum('bhnqk,bhnkd->bhnqd', s, v)
           + inter_w[..., None] * jnp.einsum('bhnqd,bhnde->bhnqe', q, C_prev))
    den = jnp.sum(s, axis=-1) + inter_w * jnp.einsum('bhnqd,bhnd->bhnq', q, n_prev)
    h = num / jnp.maximum(jnp.abs(den), jnp.exp(-m_t))[..., None]
    return h.reshape(B, H, S, Dh)

def dilated_branch(q, k, v, rel_bias, window, dilation):
    B, S, H, Dh = q.shape
    blk = window // dilation
    span = dilation * blk
    s_pad = -(-S // span) * span
    nb = s_pad // span

    def to_blocks(t):
        t = jnp.pad(t, ((0, 0), (0, s_pad - S), (0, 0), (0, 0)))
        return t.reshape(B, nb, blk, dilation, H, Dh).transpose(0, 3, 4, 1, 2, 5)

    qb, kb, vb = to_blocks(q), to_blocks(k), to_blocks(v)
    shift = lambda t: jnp.pad(t, ((0, 0), (0, 0), (0, 0), (1, 0), (0, 0), (0, 0)))[:, :, :, :-1]
    kk = jnp.concatenate([shift(kb), kb], axis=4)
    vv = jnp.concatenate([shift(vb), vb], axis=4)
    i = jnp.arange(blk)[:, None]
    j = jnp.arange(2 * blk)[None, :]
    steps = i + blk - j
    band = (steps >= 0) & (steps <= blk)
    valid = band[None] & ((jnp.arange(nb)[:, None, None] > 0) | (j >= blk)[None])
    bias = rel_bias[t5_bucket(jnp.maximum(steps, 0) * dilation)].transpose(2, 0, 1)
    s = (jnp.einsum('brhnqc,brhnkc->brhnqk', qb, kk).astype(jnp.float32) * (A_HEAD_DIM ** -0.5)
         + bias[None, None, :, None])
    s = jnp.where(valid[None, None, None], s, -jnp.inf)
    m = jnp.max(s, axis=-1, keepdims=True)
    p = jnp.exp(s - m)
    den = jnp.sum(p, axis=-1)
    o = jnp.einsum('brhnqk,brhnkc->brhnqc', p, vv) / den[..., None]
    lse = m[..., 0] + jnp.log(den)
    o = o.transpose(0, 3, 4, 1, 2, 5).reshape(B, s_pad, H, Dh)[:, :S]
    lse = lse.transpose(0, 3, 4, 1, 2).reshape(B, s_pad, H)[:, :S]
    return o, lse

def peer(h, w_query, sub_keys1, sub_keys2, expert_u, expert_v):
    B, S, D = h.shape
    T = B * S
    hf = h.reshape(T, D)
    q = (hf @ w_query).reshape(T, PEER_HEADS, 2, PEER_QDIM // 2)
    s1 = jnp.einsum('thc,hkc->thk', q[:, :, 0], sub_keys1).astype(jnp.float32)
    s2 = jnp.einsum('thc,hkc->thk', q[:, :, 1], sub_keys2).astype(jnp.float32)
    v1, i1 = lax.top_k(s1, PEER_TOPK)
    v2, i2 = lax.top_k(s2, PEER_TOPK)
    cand = (v1[..., :, None] + v2[..., None, :]).reshape(T, PEER_HEADS, PEER_TOPK * PEER_TOPK)
    vc, ic = lax.top_k(cand, PEER_TOPK)
    e1 = jnp.take_along_axis(i1, ic // PEER_TOPK, axis=-1)
    e2 = jnp.take_along_axis(i2, ic % PEER_TOPK, axis=-1)
    idx = (e1 * N_KEYS + e2).reshape(T, PEER_HEADS * PEER_TOPK)
    gate = jax.nn.softmax(vc, axis=-1).reshape(T, PEER_HEADS * PEER_TOPK)

    def block(args):
        xb, ib, gb = args
        u = expert_u[ib]
        pre = jnp.einsum('td,tkd->tk', xb, u).astype(jnp.float32)
        a = jax.nn.gelu(pre, approximate=False) * gb
        return jnp.einsum('tk,tkd->td', a, expert_v[ib])

    nblk = T // PEER_BLOCK
    out = lax.map(block, (hf.reshape(nblk, PEER_BLOCK, D),
                          idx.reshape(nblk, PEER_BLOCK, -1),
                          gate.reshape(nblk, PEER_BLOCK, -1)))
    return out.reshape(B, S, D).astype(h.dtype)

def first_inputs(seed: int = 0) -> dict:
    key = jax.random.key(seed)
    ks = jax.random.split(key, 24)
    n = lambda i, shape: jax.random.normal(ks[i], shape, jnp.float32)
    return {
        'x': n(0, (BATCH, SEQ, D_MODEL)),
        'norm1_g': 1.0 + 0.02 * n(1, (DEPTH, D_MODEL)),
        'w_in': n(2, (DEPTH, D_MODEL, IN_COLS)) * D_MODEL ** -0.5,
        'conv_w': n(3, (DEPTH, CONV_W, M_WIDTH)) * CONV_W ** -0.5,
        'conv_b': 0.02 * n(4, (DEPTH, M_WIDTH)),
        'wq_m': n(5, (DEPTH, M_HEADS, M_HEAD_DIM, M_HEAD_DIM)) * M_HEAD_DIM ** -0.5,
        'wk_m': n(6, (DEPTH, M_HEADS, M_HEAD_DIM, M_HEAD_DIM)) * M_HEAD_DIM ** -0.5,
        'ig_b': 0.1 * n(7, (DEPTH, M_HEADS)),
        'fg_b': jnp.linspace(3.0, 6.0, M_HEADS, dtype=jnp.float32)[None] + 0.1 * n(8, (DEPTH, M_HEADS)),
        'mh_norm_g': 1.0 + 0.02 * n(9, (DEPTH, M_HEADS, M_HEAD_DIM)),
        'skip_m': 1.0 + 0.02 * n(10, (DEPTH, M_HEADS, M_HEAD_DIM)),
        'qn_g': 1.0 + 0.02 * n(11, (DEPTH, A_HEADS, A_HEAD_DIM)),
        'kn_g': 1.0 + 0.02 * n(12, (DEPTH, A_HEADS, A_HEAD_DIM)),
        'rel_bias': 0.5 * n(13, (N_BUCKETS, A_HEADS)),
        'w_out': n(14, (DEPTH, MIX_WIDTH, D_MODEL)) * MIX_WIDTH ** -0.5,
        'norm2_g': 1.0 + 0.02 * n(15, (DEPTH, D_MODEL)),
        'w_query': n(16, (DEPTH, D_MODEL, PEER_HEADS * PEER_QDIM)) * D_MODEL ** -0.5,
        'sub_keys1': n(17, (DEPTH, PEER_HEADS, N_KEYS, PEER_QDIM // 2)) * (PEER_QDIM // 2) ** -0.5,
        'sub_keys2': n(18, (DEPTH, PEER_HEADS, N_KEYS, PEER_QDIM // 2)) * (PEER_QDIM // 2) ** -0.5,
        'expert_u': n(19, (DEPTH, N_EXPERTS, D_MODEL)) * D_MODEL ** -0.5,
        'expert_v': n(20, (DEPTH, N_EXPERTS, D_MODEL)) * D_MODEL ** -0.5,
    }

def first_block(x, norm1_g, w_in, conv_w, conv_b, wq_m, wk_m, ig_b, fg_b, mh_norm_g, skip_m,
              qn_g, kn_g, rel_bias, w_out, norm2_g, w_query, sub_keys1, sub_keys2,
              expert_u, expert_v):
    B, S, D = x.shape
    offsets = []
    acc = 0
    for sz in IN_SIZES[:-1]:
        acc += sz
        offsets.append(acc)
    for l in range(DEPTH):
        h = rms_norm(x, norm1_g[l])
        proj = h @ w_in[l]
        u, vm, z, ipre, fpre, qa, ka, va = jnp.split(proj, offsets, axis=-1)
        c = jax.nn.silu(causal_short_conv(u, conv_w[l], conv_b[l]))
        ch = c.reshape(B, S, M_HEADS, M_HEAD_DIM)
        qm = jnp.einsum('bshc,hcd->bhsd', ch, wq_m[l]).astype(jnp.float32)
        km = jnp.einsum('bshc,hcd->bhsd', ch, wk_m[l]).astype(jnp.float32) * (M_HEAD_DIM ** -0.5)
        vmh = vm.reshape(B, S, M_HEADS, M_HEAD_DIM).transpose(0, 2, 1, 3).astype(jnp.float32)
        ig = (ipre + ig_b[l]).astype(jnp.float32).transpose(0, 2, 1)
        fg = (fpre + fg_b[l]).astype(jnp.float32).transpose(0, 2, 1)
        hm = mlstm_chunkwise(qm, km, vmh, ig, fg).transpose(0, 2, 1, 3).astype(x.dtype)
        hm = rms_norm(hm, mh_norm_g[l]) + skip_m[l] * ch
        ym = jax.nn.sigmoid(z) * hm.reshape(B, S, M_WIDTH)
        qh = rms_norm(qa.reshape(B, S, A_HEADS, A_HEAD_DIM), qn_g[l])
        kh = rms_norm(ka.reshape(B, S, A_HEADS, A_HEAD_DIM), kn_g[l])
        vh = va.reshape(B, S, A_HEADS, A_HEAD_DIM)
        outs, lses = [], []
        for window, dilation in DIL_PATTERNS:
            o, lse = dilated_branch(qh, kh, vh, rel_bias, window, dilation)
            outs.append(o)
            lses.append(lse)
        wts = jax.nn.softmax(jnp.stack(lses, axis=0), axis=0)
        ya = jnp.sum(wts[..., None] * jnp.stack(outs, axis=0), axis=0)
        ya = ya.reshape(B, S, A_WIDTH).astype(x.dtype)
        x = x + jnp.concatenate([ym, ya], axis=-1) @ w_out[l]
        h2 = rms_norm(x, norm2_g[l])
        x = x + peer(h2, w_query[l], sub_keys1[l], sub_keys2[l], expert_u[l], expert_v[l])
    return x


DEPTH_2 = 2

CTX_LEN = 256
GRID_W = 64
N_MIXERS = 3
HEAD_DIM = 64
N_HEADS = D_MODEL // HEAD_DIM
N_KV_HEADS = max(1, N_HEADS // 4)
NA_WIN_H = 8
NA_WIN_W = 16
NA_QCOLS = 16
NA_KCOLS = NA_QCOLS + NA_WIN_W
SWA_RADIUS = 128
Q_BLOCK = 128
ROPE_THETA = 10000.0
D_FF = ((8 * D_MODEL // 3 + 127) // 128) * 128
CONV_W_2 = 3
RMS_EPS = 1e-6
NEG_INF = -1e30
N_LAYERS_NA = (DEPTH_2 + N_MIXERS - 1) // N_MIXERS
N_LAYERS_SWA = (DEPTH_2 + N_MIXERS - 2) // N_MIXERS
N_LAYERS_GA = (DEPTH_2 + N_MIXERS - 3) // N_MIXERS


def rmsnorm(x, g):
    x32 = x.astype(jnp.float32)
    y = x32 * lax.rsqrt(jnp.mean(x32 * x32, axis=-1, keepdims=True) + RMS_EPS)
    return (y * g.astype(jnp.float32)).astype(x.dtype)

def modulate(h, shift, scale):
    return h * (1 + scale) + shift

def axial_rope_tables(seq):
    t = jnp.arange(seq)
    row = (t // GRID_W).astype(jnp.float32)
    col = (t % GRID_W).astype(jnp.float32)
    n_axis = HEAD_DIM // 4
    inv = ROPE_THETA ** (-jnp.arange(n_axis, dtype=jnp.float32) / n_axis)
    ang = jnp.concatenate([row[:, None] * inv, col[:, None] * inv], axis=-1)
    return jnp.cos(ang), jnp.sin(ang)

def apply_rope(x, cos, sin):
    shp = (x.shape[1],) + (1,) * (x.ndim - 3) + (x.shape[-1] // 2,)
    cos = cos.reshape(shp).astype(x.dtype)
    sin = sin.reshape(shp).astype(x.dtype)
    x1, x2 = jnp.split(x, 2, axis=-1)
    return jnp.concatenate([x1 * cos - x2 * sin, x2 * cos + x1 * sin], axis=-1)

def attend(q, k, v, bias=None, mask=None, sink=None):
    s = jnp.einsum('...qngd,...knd->...ngqk', q, k).astype(jnp.float32) * (HEAD_DIM ** -0.5)
    if bias is not None:
        s = s + bias.astype(jnp.float32)
    if mask is not None:
        s = jnp.where(mask, s, NEG_INF)
    if sink is not None:
        sink_col = jnp.broadcast_to(sink.astype(jnp.float32)[:, :, None, None], s.shape[:-1] + (1,))
        s = jnp.concatenate([s, sink_col], axis=-1)
    p = jax.nn.softmax(s, axis=-1)
    if sink is not None:
        p = p[..., :-1]
    return jnp.einsum('...ngqk,...knd->...qngd', p.astype(v.dtype), v)

def attn_inputs(h, w_qkv, g_q, g_k, n_kv, with_q=True):
    bsz, t = h.shape[:2]
    kv_w = n_kv * HEAD_DIM
    if with_q:
        y = h @ w_qkv
        q = rmsnorm(y[..., :D_MODEL].reshape(bsz, t, n_kv, N_HEADS // n_kv, HEAD_DIM), g_q)
        kv = y[..., D_MODEL:]
    else:
        q = None
        kv = h @ w_qkv[:, D_MODEL:]
    k = rmsnorm(kv[..., :kv_w].reshape(bsz, t, n_kv, HEAD_DIM), g_k)
    v = kv[..., kv_w:].reshape(bsz, t, n_kv, HEAD_DIM)
    return q, k, v

def neighbourhood_attention(q, k, v, k_c, v_c, rpb):
    bsz, seq = q.shape[:2]
    n_ctx = k_c.shape[1]
    rows = seq // GRID_W
    kh = min(NA_WIN_H, rows)
    ncb = GRID_W // NA_QCOLS
    qg = q.reshape(bsz, rows, ncb, NA_QCOLS, N_HEADS, 1, HEAD_DIM)
    kg = k.reshape(bsz, rows, GRID_W, N_HEADS, HEAD_DIM)
    vg = v.reshape(bsz, rows, GRID_W, N_HEADS, HEAD_DIM)
    qcol = np.arange(GRID_W).reshape(ncb, NA_QCOLS)
    kcs = np.clip(np.arange(ncb) * NA_QCOLS - NA_WIN_W // 2, 0, GRID_W - NA_KCOLS)
    kcol = kcs[:, None] + np.arange(NA_KCOLS)
    cs = np.clip(qcol - NA_WIN_W // 2, 0, GRID_W - NA_WIN_W)
    col_ok = (kcol[:, None, :] >= cs[..., None]) & (kcol[:, None, :] < cs[..., None] + NA_WIN_W)
    dc_idx = np.clip(kcol[:, None, :] - qcol[..., None], -(NA_WIN_W - 1), NA_WIN_W - 1) + NA_WIN_W - 1
    lat_ok = np.broadcast_to(col_ok[:, :, None, :], (ncb, NA_QCOLS, kh, NA_KCOLS)).reshape(ncb, NA_QCOLS, kh * NA_KCOLS)
    mask = np.concatenate([lat_ok, np.ones((ncb, NA_QCOLS, n_ctx), bool)], axis=-1)[:, None, None]
    k_cb = jnp.broadcast_to(k_c[:, None], (bsz, ncb) + k_c.shape[1:])
    v_cb = jnp.broadcast_to(v_c[:, None], (bsz, ncb) + v_c.shape[1:])
    zero_ctx_bias = jnp.zeros((ncb, N_HEADS, NA_QCOLS, n_ctx), rpb.dtype)

    def row_step(r):
        rs = jnp.clip(r - kh // 2, 0, rows - kh)
        k_r = lax.dynamic_slice_in_dim(kg, rs, kh, axis=1)
        v_r = lax.dynamic_slice_in_dim(vg, rs, kh, axis=1)
        k_b = jnp.moveaxis(k_r[:, :, kcol], 1, 2).reshape(bsz, ncb, kh * NA_KCOLS, N_HEADS, HEAD_DIM)
        v_b = jnp.moveaxis(v_r[:, :, kcol], 1, 2).reshape(bsz, ncb, kh * NA_KCOLS, N_HEADS, HEAD_DIM)
        k_cat = jnp.concatenate([k_b, k_cb], axis=2)
        v_cat = jnp.concatenate([v_b, v_cb], axis=2)
        dr_idx = rs + jnp.arange(kh) - r + NA_WIN_H - 1
        b_lat = rpb[:, dr_idx[:, None, None, None], dc_idx[None]]
        b_lat = jnp.transpose(b_lat, (2, 0, 3, 1, 4)).reshape(ncb, N_HEADS, NA_QCOLS, kh * NA_KCOLS)
        bias = jnp.concatenate([b_lat, zero_ctx_bias], axis=-1)[:, :, None]
        q_r = lax.dynamic_index_in_dim(qg, r, axis=1, keepdims=False)
        return attend(q_r, k_cat, v_cat, bias=bias, mask=mask)

    out = lax.map(row_step, jnp.arange(rows))
    return jnp.moveaxis(out, 0, 1).reshape(bsz, seq, D_MODEL)

def sliding_window_attention(q, k, v, k_c, v_c, sink):
    bsz, seq = q.shape[:2]
    n_ctx = k_c.shape[1]
    nb = seq // Q_BLOCK
    span = Q_BLOCK + 2 * SWA_RADIUS
    pad = ((0, 0), (SWA_RADIUS, SWA_RADIUS), (0, 0), (0, 0))
    k_p = jnp.pad(k, pad)
    v_p = jnp.pad(v, pad)
    qoff = np.arange(Q_BLOCK)
    koff = np.arange(span) - SWA_RADIUS
    band = np.abs(qoff[:, None] - koff[None, :]) <= SWA_RADIUS
    ctx_ok = jnp.ones((Q_BLOCK, n_ctx), bool)

    def block_step(j):
        start = j * Q_BLOCK
        q_j = lax.dynamic_slice_in_dim(q, start, Q_BLOCK, axis=1)
        k_j = lax.dynamic_slice_in_dim(k_p, start, span, axis=1)
        v_j = lax.dynamic_slice_in_dim(v_p, start, span, axis=1)
        kpos = start - SWA_RADIUS + jnp.arange(span)
        valid = band & ((kpos >= 0) & (kpos < seq))[None, :]
        mask = jnp.concatenate([valid, ctx_ok], axis=-1)
        return attend(q_j, jnp.concatenate([k_j, k_c], axis=1), jnp.concatenate([v_j, v_c], axis=1),
                      mask=mask, sink=sink)

    out = lax.map(block_step, jnp.arange(nb))
    return jnp.moveaxis(out, 0, 1).reshape(bsz, seq, D_MODEL)

def blocked_global_attention(q, k, v, k_c, v_c):
    bsz, seq = q.shape[:2]
    nb = seq // Q_BLOCK
    k_all = jnp.concatenate([k, k_c], axis=1)
    v_all = jnp.concatenate([v, v_c], axis=1)

    def block_step(j):
        q_j = lax.dynamic_slice_in_dim(q, j * Q_BLOCK, Q_BLOCK, axis=1)
        return attend(q_j, k_all, v_all)

    out = lax.map(block_step, jnp.arange(nb))
    return jnp.moveaxis(out, 0, 1).reshape(bsz, seq, D_MODEL)

def conv_ffn(h, w_up, conv_w, conv_b, w_down):
    t = h.shape[1]
    u = h @ w_up
    u_p = jnp.pad(u, ((0, 0), (CONV_W_2 // 2, CONV_W_2 // 2), (0, 0)))
    u = sum(u_p[:, tap:tap + t] * conv_w[tap] for tap in range(CONV_W_2)) + conv_b
    a, g = jnp.split(u, 2, axis=-1)
    return (a * jax.nn.silu(g)) @ w_down

def second_inputs(seed: int = 0) -> dict:
    key = jax.random.key(seed)
    ks = iter(jax.random.split(key, 32))
    d = D_MODEL
    qkv_na = d + 2 * N_HEADS * HEAD_DIM
    qkv_gqa = d + 2 * N_KV_HEADS * HEAD_DIM

    def nrm(shape, scale):
        return scale * jax.random.normal(next(ks), shape, jnp.float32)

    return {
        'x': nrm((BATCH, SEQ, d), 1.0),
        'c': nrm((BATCH, d), 1.0),
        'ctx': nrm((BATCH, CTX_LEN, d), 1.0),
        'c_ctx': nrm((d,), 1.0),
        'w_mod': nrm((DEPTH_2, d, 6 * d), 0.5 * d ** -0.5),
        'b_mod': nrm((DEPTH_2, 6 * d), 0.02),
        'g_attn': 1.0 + nrm((DEPTH_2, d), 0.02),
        'g_ffn': 1.0 + nrm((DEPTH_2, d), 0.02),
        'na_w_qkv': nrm((N_LAYERS_NA, d, qkv_na), d ** -0.5),
        'na_g_q': 1.0 + nrm((N_LAYERS_NA, HEAD_DIM), 0.02),
        'na_g_k': 1.0 + nrm((N_LAYERS_NA, HEAD_DIM), 0.02),
        'na_rpb': nrm((N_LAYERS_NA, N_HEADS, 2 * NA_WIN_H - 1, 2 * NA_WIN_W - 1), 0.5),
        'na_w_o': nrm((N_LAYERS_NA, d, d), d ** -0.5),
        'swa_w_qkv': nrm((N_LAYERS_SWA, d, qkv_gqa), d ** -0.5),
        'swa_g_q': 1.0 + nrm((N_LAYERS_SWA, HEAD_DIM), 0.02),
        'swa_g_k': 1.0 + nrm((N_LAYERS_SWA, HEAD_DIM), 0.02),
        'swa_sink': nrm((N_LAYERS_SWA, N_HEADS), 0.5),
        'swa_w_o': nrm((N_LAYERS_SWA, d, d), d ** -0.5),
        'ga_w_qkv': nrm((N_LAYERS_GA, d, qkv_gqa), d ** -0.5),
        'ga_g_q': 1.0 + nrm((N_LAYERS_GA, HEAD_DIM), 0.02),
        'ga_g_k': 1.0 + nrm((N_LAYERS_GA, HEAD_DIM), 0.02),
        'ga_w_o': nrm((N_LAYERS_GA, d, d), d ** -0.5),
        'ffn_w_up': nrm((DEPTH_2, d, 2 * D_FF), d ** -0.5),
        'ffn_conv_w': nrm((DEPTH_2, CONV_W_2, 2 * D_FF), CONV_W_2 ** -0.5),
        'ffn_conv_b': nrm((DEPTH_2, 2 * D_FF), 0.02),
        'ffn_w_down': nrm((DEPTH_2, D_FF, d), D_FF ** -0.5),
    }

def second_block(x, c, ctx, c_ctx, w_mod, b_mod, g_attn, g_ffn,
              na_w_qkv, na_g_q, na_g_k, na_rpb, na_w_o,
              swa_w_qkv, swa_g_q, swa_g_k, swa_sink, swa_w_o,
              ga_w_qkv, ga_g_q, ga_g_k, ga_w_o,
              ffn_w_up, ffn_conv_w, ffn_conv_b, ffn_w_down):
    bsz, seq = x.shape[:2]
    n_ctx = ctx.shape[1]
    cos, sin = axial_rope_tables(seq)
    silu_c = jax.nn.silu(c)
    silu_cc = jax.nn.silu(c_ctx)
    for i in range(DEPTH_2):
        last = i == DEPTH_2 - 1
        kind, j = i % N_MIXERS, i // N_MIXERS
        mod = silu_c @ w_mod[i] + b_mod[i]
        mod_c = silu_cc @ w_mod[i] + b_mod[i]
        sh1, sc1, gt1, sh2, sc2, gt2 = jnp.split(mod[:, None, :], 6, axis=-1)
        sh1c, sc1c, gt1c, sh2c, sc2c, gt2c = jnp.split(mod_c, 6, axis=-1)

        h = modulate(rmsnorm(x, g_attn[i]), sh1, sc1)
        hc = modulate(rmsnorm(ctx, g_attn[i]), sh1c, sc1c)
        if kind == 0:
            w_in, w_out, gq, gk, n_kv, sink = na_w_qkv[j], na_w_o[j], na_g_q[j], na_g_k[j], N_HEADS, None
        elif kind == 1:
            w_in, w_out, gq, gk, n_kv = swa_w_qkv[j], swa_w_o[j], swa_g_q[j], swa_g_k[j], N_KV_HEADS
            sink = swa_sink[j].reshape(n_kv, N_HEADS // n_kv)
        else:
            w_in, w_out, gq, gk, n_kv, sink = ga_w_qkv[j], ga_w_o[j], ga_g_q[j], ga_g_k[j], N_KV_HEADS, None
        q, k, v = attn_inputs(h, w_in, gq, gk, n_kv)
        q_c, k_c, v_c = attn_inputs(hc, w_in, gq, gk, n_kv, with_q=not last)
        if kind == 0:
            o = neighbourhood_attention(q, k, v, k_c, v_c, na_rpb[j])
        else:
            q = apply_rope(q, cos, sin)
            k = apply_rope(k, cos, sin)
            if kind == 1:
                o = sliding_window_attention(q, k, v, k_c, v_c, sink)
            else:
                o = blocked_global_attention(q, k, v, k_c, v_c)
        x = x + gt1 * (o @ w_out)
        if not last:
            o_c = attend(q_c, k_c, v_c, sink=sink).reshape(bsz, n_ctx, D_MODEL)
            ctx = ctx + gt1c * (o_c @ w_out)

        h = modulate(rmsnorm(x, g_ffn[i]), sh2, sc2)
        x = x + gt2 * conv_ffn(h, ffn_w_up[i], ffn_conv_w[i], ffn_conv_b[i], ffn_w_down[i])
        if not last:
            hc = modulate(rmsnorm(ctx, g_ffn[i]), sh2c, sc2c)
            ctx = ctx + gt2c * conv_ffn(hc, ffn_w_up[i], ffn_conv_w[i], ffn_conv_b[i], ffn_w_down[i])
    return x


def setup_inputs(seed=0):
    out = dict(first_inputs(seed))
    for name, value in second_inputs(seed + 1).items():
        if name != "x":
            out[name + "_2"] = value
    return out


def reference(
    x, norm1_g, w_in, conv_w, conv_b, wq_m, wk_m, ig_b, fg_b, mh_norm_g, skip_m, qn_g, kn_g,
    rel_bias, w_out, norm2_g, w_query, sub_keys1, sub_keys2, expert_u, expert_v, c_2, ctx_2,
    c_ctx_2, w_mod_2, b_mod_2, g_attn_2, g_ffn_2, na_w_qkv_2, na_g_q_2, na_g_k_2, na_rpb_2,
    na_w_o_2, swa_w_qkv_2, swa_g_q_2, swa_g_k_2, swa_sink_2, swa_w_o_2, ga_w_qkv_2, ga_g_q_2,
    ga_g_k_2, ga_w_o_2, ffn_w_up_2, ffn_conv_w_2, ffn_conv_b_2, ffn_w_down_2,
):
    x = first_block(
        x, norm1_g, w_in, conv_w, conv_b, wq_m, wk_m, ig_b, fg_b, mh_norm_g, skip_m, qn_g, kn_g,
        rel_bias, w_out, norm2_g, w_query, sub_keys1, sub_keys2, expert_u, expert_v,
    )
    return second_block(
        x, c_2, ctx_2, c_ctx_2, w_mod_2, b_mod_2, g_attn_2, g_ffn_2, na_w_qkv_2, na_g_q_2,
        na_g_k_2, na_rpb_2, na_w_o_2, swa_w_qkv_2, swa_g_q_2, swa_g_k_2, swa_sink_2, swa_w_o_2,
        ga_w_qkv_2, ga_g_q_2, ga_g_k_2, ga_w_o_2, ffn_w_up_2, ffn_conv_w_2, ffn_conv_b_2,
        ffn_w_down_2,
    )


_drawn_inputs = setup_inputs


def setup_inputs(seed=0):
    import zlib

    import numpy as np

    out = dict(_drawn_inputs(seed))
    spreads = {}
    factors = {'norm1_g': 3.17,
     'conv_b': 4.444,
     'ig_b': 64.0,
     'mh_norm_g': 7.935,
     'skip_m': 8.0,
     'qn_g': 8.0,
     'kn_g': 8.0,
     'norm2_g': 8.0,
     'w_query': 4.022,
     'sub_keys1': 4.097,
     'sub_keys2': 4.085,
     'expert_u': 4.453,
     'expert_v': 4.028,
     'g_attn_2': 8.0,
     'g_ffn_2': 7.183,
     'na_g_q_2': 8.0,
     'na_g_k_2': 8.0,
     'na_rpb_2': 6.71,
     'swa_g_q_2': 8.0,
     'swa_g_k_2': 21.662,
     'swa_sink_2': 8.0,
     'ffn_conv_b_2': 7.74}
    for name, (base, spread) in spreads.items():
        noise = np.random.default_rng([zlib.crc32(name.encode()), seed]).standard_normal(out[name].shape)
        drawn = base * np.exp(spread * noise) if base else spread * noise
        out[name] = jnp.asarray(drawn.astype(out[name].dtype))
    for name, factor in factors.items():
        out[name] = (out[name] * factor).astype(out[name].dtype)
    return out
```

```python
import numpy as np

import concourse.bass as bass
from concourse import mybir

F32 = mybir.dt.float32
U32 = mybir.dt.uint32
FR = mybir.dt.float32r
ALU = mybir.AluOpType
ACT = mybir.ActivationFunctionType
AX_X = mybir.AxisListType.X

P = 128
BANK = 512
D = 1024
KD = D // P
SEQ = 512
CTX = 256
TOK = SEQ + CTX
TILES = SEQ // P
ALL_TILES = TOK // P
EPS = 1e-6
NEG = -1e30
RING = 4

M_HEADS = 4
CHUNKS = SEQ // P
UNITS = CHUNKS * M_HEADS
DIL_HEADS = 8
HEAD = 64
N_BUCKETS = 32
PEER_HEADS = 8
TOPK = 16
N_KEYS = 128
PICKS = PEER_HEADS * TOPK
NA_HEADS = 16
KV_HEADS = 4
GRID_W = 64
ROWS = SEQ // GRID_W
RPB_H = 15
RPB_W = 31
D_FF = 2816
FF_CHUNKS = D_FF // P
RADIUS = 128
LAYERS = 2
MODS = 6 * KD

PARAM_SIZES = dict(
    norm1_g=KD, conv_w=4 * M_HEADS, conv_b=M_HEADS, mh_g=M_HEADS, skip=M_HEADS, qn_g=4, kn_g=4, norm2_g=KD,
    gate_b=2 * M_HEADS, g_attn=LAYERS * KD, g_ffn=LAYERS * KD, b_mod=LAYERS * MODS, cond=2 * KD,
    na_gq=1, na_gk=1, swa_gq=1, swa_gk=1, sink=NA_HEADS,
    ffn_w=LAYERS * 2 * FF_CHUNKS * 3, ffn_b=LAYERS * 2 * FF_CHUNKS,
)
CONST_SIZES = dict(ident=P, tri=P, ones=P, iota=P, blocks=P, swap=P, causal=P, iota16=TOPK, band=3 * P)


def offsets(sizes):
    out, at = {}, 0
    for name, n in sizes.items():
        out[name] = (at, n)
        at += n
    return out, at


PARAMS, N_PARAMS = offsets(PARAM_SIZES)
CONSTS, N_CONSTS = offsets(CONST_SIZES)

SBUF_START = 16512
SBUF_FLOATS = (229344 - SBUF_START) // 4
PICKS_AT = 8560
H_HIGH = 10240
BIG = H_HIGH + KD * TOK
H_LOW = 47064


class Chain:

    def __init__(self, sem):
        self.sem, self.n = sem, 0

    def __call__(self, eng, ins):
        self.n += 1
        ins.then_inc(self.sem, 1)
        eng.wait_ge(self.sem, self.n)

    def restart(self, eng):
        eng.sem_clear(self.sem)
        self.n = 0


class Signal:

    def __init__(self, sem):
        self.sem, self.base = sem, 0

    def at(self, n):
        return n + self.base


class Core:

    def __init__(self, nc):
        self.nc = nc
        self.names = 0
        self.signals = {}
        self.psum = nc.alloc_psum_tensor("psum", [P, 8, BANK], F32)
        self.dve = Chain(nc.alloc_semaphore("vector_done"))
        self.act = Chain(nc.alloc_semaphore("scalar_done"))
        self.pool = Chain(nc.alloc_semaphore("gpsimd_done"))
        self.weights_in = [Signal(nc.alloc_semaphore(f"weights_in{r}")) for r in range(RING)]
        self.product_done = Signal(nc.alloc_semaphore("product_done"))
        self.bank_read = Signal(nc.alloc_semaphore("bank_read"))
        self.xT = self.place("xT", 0, KD, TOK)
        self.params = self.place("params", 6144, N_PARAMS)
        self.consts = self.place("consts", 6144 + 704, N_CONSTS)
        self.modT = self.place("modT", 8304, LAYERS * MODS, 2)
        self.gain = self.place("gain", 8512, 2, KD)
        self.h_high = self.place("h_high", H_HIGH, KD, TOK, dtype=FR)
        self.h_low = self.place("h_low", H_LOW, KD, TOK, dtype=FR)
        self.w_high, self.w_low, self.x_high, self.x_low = (self.shared(s) for s in ("w_high", "w_low", "x_high", "x_low"))

    def place(self, name, at, *shape, dtype=F32, rows=P):
        n = int(np.prod(shape))
        assert at + n <= SBUF_FLOATS, (name, at + n, SBUF_FLOATS)
        return self.nc.alloc_sbuf_tensor_at(name, [rows, *shape], dtype, offset=SBUF_START + 4 * at)

    def sem(self, name):
        return self.nc.alloc_semaphore(name)

    def shared(self, name):
        if name not in self.signals:
            self.signals[name] = Signal(self.nc.alloc_semaphore(name))
        return self.signals[name]

    def par(self, name, i=0, n=1):
        return self.params[:, bass.ds(i + PARAMS[name][0], n)]

    def const(self, name, rows=P):
        at, n = CONSTS[name]
        return self.consts[0:rows, at:at + n]


PIECES = ((0, SEQ), (SEQ, CTX))


def stage_load(k, t):
    loaded = k.sem("loaded")
    with k.nc.Block() as block:
        @block.sync
        def _(sp):
            sp.dma_start(k.xT[:, :, 0:SEQ], t["xT"]).then_inc(loaded, 16)
            sp.dma_start(k.xT[:, :, SEQ:TOK], t["ctxT"]).then_inc(loaded, 16)
            sp.dma_start(k.params[:, :], t["params"]).then_inc(loaded, 16)
            sp.dma_start(k.consts[:, :], t["consts"]).then_inc(loaded, 16)
            sp.wait_ge(loaded, 64)


def split_product(nc, bank, w_high, w_low, x_high, x_low, first, last):
    nc.tensor.matmul(bank, w_high, x_high, start=first, stop=False)
    nc.tensor.matmul(bank, w_high, x_low, start=False, stop=False)
    return nc.tensor.matmul(bank, w_low, x_high, start=False, stop=last)


def product(k, block, w, n_chunks, k_chunks, pieces, high, low, at, epilogue, scalar=None, full=None, parts=1, split_at=None):
    nc = k.nc
    k.names += 1
    kp = k_chunks // parts
    n_raw = RING // parts
    raw = [k.place(f"w_raw{k.names}_{r}", at + r * kp * P, kp, P) for r in range(n_raw)]
    split_at = at + n_raw * kp * P if split_at is None else split_at
    w_high, w_low = ([k.place(f"w_{s}{k.names}_{r}", split_at + (2 * i + r) * kp * P, kp, P, dtype=FR) for r in range(2)]
                     for i, s in enumerate(("high", "low")))
    per = RING // parts
    passes = n_chunks // per
    n_pieces = len(pieces)
    width = sum(n for _, n in pieces)
    assert passes * per == n_chunks and kp * parts == k_chunks

    def banks(r):
        return [k.psum[:, r // parts * n_pieces + i, 0:n] for i, (_, n) in enumerate(pieces)]

    @block.sync
    def _(sp):
        with sp.Fori(0, passes) as it:
            for r in range(RING):
                sp.wait_ge(k.w_low.sem, k.w_low.at(it * RING + (r + 1)))
                source = w[it * per + r // parts].rearrange("p (k n) -> p k n", n=P)[:, r % parts * kp:(r % parts + 1) * kp, :]
                sp.dma_start(raw[r % n_raw][:, :, :], source).then_inc(k.weights_in[r % n_raw].sem, 16)

    @block.scalar
    def _(act):
        def round_weights(it, r):
            act.wait_ge(k.weights_in[r % n_raw].sem, k.weights_in[r % n_raw].at(it * (16 * parts) + 16 * (r // n_raw + 1)))
            if not (isinstance(it, int) and it * RING + r < 2):
                act.wait_ge(k.product_done.sem, k.product_done.at((it * RING + (r - 1)) * n_pieces))
            nc.scalar.activation(w_high[r % 2][:, :, :], raw[r % n_raw][:, :, :], ACT.Copy).then_inc(k.w_high.sem, 1)

        if full is not None:
            for c in range(k_chunks):
                if c == 4:
                    round_weights(0, 0)
                    round_weights(0, 1)
                nc.scalar.activation(high[:, c, 0:width], full[:, c, 0:width], ACT.Copy).then_inc(k.x_high.sem, 1)
        else:
            round_weights(0, 0)
            round_weights(0, 1)
        if passes > 1:
            with act.Fori(0, passes - 1) as it:
                for r in range(RING):
                    round_weights(it, r + 2)
                    if scalar:
                        scalar(act, it, r)
        for r in range(RING):
            if r + 2 < RING:
                round_weights(passes - 1, r + 2)
            if scalar:
                scalar(act, passes - 1, r)

    @block.gpsimd
    def _(pool):
        pool.sem_inc(k.w_low.sem, n_raw)
        with pool.Fori(0, passes) as it:
            for r in range(RING):
                pool.wait_ge(k.w_high.sem, k.w_high.at(it * RING + (r + 1)))
                nc.gpsimd.tensor_tensor(w_low[r % 2][:, :, :], raw[r % n_raw][:, :, :], w_high[r % 2][:, :, :].bitcast(F32), ALU.subtract
                                        ).then_inc(k.w_low.sem, 1)

    @block.tensor
    def _(pe):
        with pe.Fori(0, passes) as it:
            for r in range(RING):
                pe.wait_ge(k.w_low.sem, k.w_low.at(it * RING + (n_raw + r + 1)))
                part = r % parts
                if part == 0:
                    pe.wait_ge(k.bank_read.sem, k.bank_read.at((it * per + (r // parts + 1)) * n_pieces))
                for bank, (t0, n) in zip(banks(r), pieces):
                    for c in range(kp):
                        kc = part * kp + c
                        if full is not None:
                            pe.wait_ge(k.x_low.sem, k.x_low.at(kc + 1))
                        mm = split_product(nc, bank, w_high[r % 2][:, c, :], w_low[r % 2][:, c, :], high[:, kc, t0:t0 + n], low[:, kc, t0:t0 + n],
                                           kc == 0, kc == k_chunks - 1)
                    mm.then_inc(k.product_done.sem, 1)

    @block.vector
    def _(dve):
        if full is not None:
            for c in range(k_chunks):
                dve.wait_ge(k.x_high.sem, k.x_high.at(c + 1))
                nc.vector.tensor_tensor(low[:, c, 0:width], full[:, c, 0:width], high[:, c, 0:width].bitcast(F32), ALU.subtract
                                        ).then_inc(k.x_low.sem, 1)
        dve.sem_inc(k.bank_read.sem, per * n_pieces)
        with dve.Fori(0, passes) as it:
            k.dve.restart(dve)
            for r in range(parts - 1, RING, parts):
                dve.wait_ge(k.product_done.sem, k.product_done.at((it * RING + (r + 1)) * n_pieces))
                epilogue(dve, it, r // parts, banks(r))

    for s in k.weights_in[0:n_raw]:
        s.base += 16 * passes * parts
    k.product_done.base += n_chunks * parts * n_pieces
    k.bank_read.base += (n_chunks + per) * n_pieces
    k.w_high.base += n_chunks * parts
    k.w_low.base += n_chunks * parts + n_raw
    if full is not None:
        k.x_high.base += k_chunks
        k.x_low.base += k_chunks


MOD_RING = 6


class Modulation:

    def __init__(self, k, t, at, bank, passes):
        self.k, self.nc, self.w = k, k.nc, t["w_mod"]
        self.slots = [k.place(f"w_mod{r}", at + r * KD * P, KD, P) for r in range(MOD_RING)]
        self.cond = k.place("cond", at + MOD_RING * KD * P, KD, 2)
        self.bank = bank
        self.share = LAYERS * MODS // passes
        assert self.share % MOD_RING == 0
        self.loaded = [k.sem(f"w_mod_in{r}") for r in range(MOD_RING)]
        self.cond_ready, self.used = k.sem("cond_ready"), k.sem("w_mod_used")

    def fetch(self, sp, it):
        for j in range(self.share):
            sp.wait_ge(self.used, it * self.share + (j + 1))
            sp.dma_start(self.slots[j % MOD_RING][:, :, :], self.w[it * self.share + j].rearrange("p (k n) -> p k n", n=P)
                         ).then_inc(self.loaded[j % MOD_RING], 16)

    def condition(self, act):
        self.nc.scalar.activation(self.cond[:, :, :].rearrange("p k c -> p (k c)"), self.k.par("cond", 0, 2 * KD),
                                  ACT.Silu).then_inc(self.cond_ready, 1)

    def start(self, pe):
        pe.sem_inc(self.used, MOD_RING)
        pe.wait_ge(self.cond_ready, 1)

    def multiply(self, pe, it):
        rounds = self.share // MOD_RING
        for j in range(self.share):
            r = j % MOD_RING
            pe.wait_ge(self.loaded[r], it * (16 * rounds) + 16 * (j // MOD_RING + 1))
            for c in range(KD):
                mm = self.nc.tensor.matmul(self.k.psum[:, self.bank, bass.ds(it * (2 * self.share) + 2 * j, 2)],
                                           self.slots[r][:, c, :], self.cond[:, c, :], start=(c == 0), stop=(c == KD - 1))
            mm.then_inc(self.used, 1)

    def finish(self, dve):
        k, nc = self.k, self.nc
        n = LAYERS * MODS
        dve.wait_ge(self.used, MOD_RING + n)
        b = k.par("b_mod", 0, n).unsqueeze(2).to_broadcast([P, n, 2])
        sums = k.psum[:, self.bank, 0:2 * n].rearrange("p (j c) -> p j c", c=2)
        k.dve(dve, nc.vector.tensor_tensor(k.modT[:, :, :], sums, b, ALU.add))
        for layer in range(LAYERS):
            for which in (1, 4):
                j = layer * MODS + which * KD
                k.dve(dve, nc.vector.tensor_scalar(k.modT[:, j:j + KD, :], k.modT[:, j:j + KD, :], 1.0, None, ALU.add))


def newton(k, dve, y, v, t):
    nc = k.nc
    k.dve(dve, nc.vector.tensor_tensor(t, y, y, ALU.mult))
    k.dve(dve, nc.vector.tensor_tensor(t, t, v, ALU.mult))
    k.dve(dve, nc.vector.tensor_scalar(t, t, -0.5, 1.5, ALU.mult, ALU.add))
    k.dve(dve, nc.vector.tensor_tensor(y, y, t, ALU.mult))


NEWTON = 4


def stage_norm(k, pieces, gain, shift):
    nc = k.nc
    k.names += 1
    width = sum(n for _, n in pieces)
    sq = k.place(f"norm_sq{k.names}", BIG, KD, TOK)
    v = k.place(f"norm_v{k.names}", BIG + KD * TOK, TOK)
    y = k.place(f"norm_y{k.names}", BIG + (KD + 1) * TOK, TOK)
    u = k.place(f"norm_u{k.names}", BIG + (KD + 2) * TOK, TOK)
    h = k.place(f"norm_h{k.names}", BIG + (KD + 3) * TOK, KD, TOK)
    sq_ready, sum_ready, v_ready, y_ready, h_ready, high_ready = (
        k.shared(f"norm_{s}") for s in ("sq_ready", "sum_ready", "v_ready", "y_ready", "h_ready", "high_ready"))
    with nc.Block() as block:
        @block.scalar
        def _(act):
            for c in range(KD):
                nc.scalar.activation(sq[:, c, 0:width], k.xT[:, c, 0:width], ACT.Square).then_inc(sq_ready.sem, 1)
            act.wait_ge(v_ready.sem, v_ready.at(len(pieces)))
            k.act(act, nc.scalar.activation(y[:, 0:width], v[:, 0:width], ACT.Ln))
            nc.scalar.activation(y[:, 0:width], y[:, 0:width], ACT.Exp, scale=-0.5).then_inc(y_ready.sem, 1)
            for c in range(KD):
                act.wait_ge(h_ready.sem, h_ready.at(c + 1))
                nc.scalar.activation(k.h_high[:, c, 0:width], h[:, c, 0:width], ACT.Copy).then_inc(high_ready.sem, 1)

        @block.gpsimd
        def _(pool):
            for c in range(KD):
                pool.wait_ge(high_ready.sem, high_ready.at(c + 1))
                nc.gpsimd.tensor_tensor(k.h_low[:, c, 0:width], h[:, c, 0:width], k.h_high[:, c, 0:width].bitcast(F32), ALU.subtract)

        @block.tensor
        def _(pe):
            for c in range(KD):
                pe.wait_ge(sq_ready.sem, sq_ready.at(c + 1))
                for i, (t0, n) in enumerate(pieces):
                    mm = nc.tensor.matmul(k.psum[:, i, 0:n], k.const("ones"), sq[:, c, t0:t0 + n],
                                          start=(c == 0), stop=(c == KD - 1))
            mm.then_inc(sum_ready.sem, 1)

        @block.vector
        def _(dve):
            dve.wait_ge(sum_ready.sem, sum_ready.at(1))
            for i, (t0, n) in enumerate(pieces):
                nc.vector.tensor_scalar(v[:, t0:t0 + n], k.psum[:, i, 0:n], 1.0 / D, EPS, ALU.mult, ALU.add
                                        ).then_inc(v_ready.sem, 1)
            dve.wait_ge(y_ready.sem, y_ready.at(1))
            newton(k, dve, y[:, 0:width], v[:, 0:width], u[:, 0:width])
            for c in range(KD):
                for i, (t0, n) in enumerate(pieces):
                    o = h[:, c, t0:t0 + n]
                    ins = nc.vector.scalar_tensor_tensor(o, k.xT[:, c, t0:t0 + n], gain(i, c), y[:, t0:t0 + n], ALU.mult, ALU.mult)
                    if shift is not None:
                        k.dve(dve, ins)
                        ins = nc.vector.tensor_scalar(o, o, shift(i, c), None, ALU.add)
                    if i < len(pieces) - 1:
                        k.dve(dve, ins)
                ins.then_inc(h_ready.sem, 1)
    for s, n in ((sq_ready, KD), (sum_ready, 1), (v_ready, len(pieces)), (y_ready, 1), (h_ready, KD), (high_ready, KD)):
        s.base += n


def stage_rows(k, w, n_blocks, width, tiles, out, at, extra=None):
    nc = k.nc
    k.names += 1
    blocks = [(w[b], width, lambda i, b=b: out(b, i)) for b in range(n_blocks)] + ([extra] if extra else [])
    raw = [k.place(f"rows_w{k.names}_{r}", at + r * BANK, BANK) for r in range(RING)]
    high, low = ([k.place(f"rows_{s}{k.names}_{r}", at + (RING * i + r) * BANK, BANK, dtype=FR) for r in range(RING)]
                 for i, s in ((1, "high"), (2, "low")))
    taken = k.shared("rows_taken")
    steps = [(b, c) for b in range(len(blocks)) for c in range(KD)]
    with nc.Block() as block:
        @block.sync
        def _(sp):
            for s, (b, c) in enumerate(steps):
                source, n, _ = blocks[b]
                if s >= RING:
                    sp.wait_ge(k.w_low.sem, k.w_low.at(s - RING + 1))
                sp.dma_start(raw[s % RING][:, 0:n], source[:, c * n:(c + 1) * n]).then_inc(k.weights_in[s % RING].sem, 16)

        @block.scalar
        def _(act):
            def round_rows(s):
                n = blocks[steps[s][0]][1]
                act.wait_ge(k.weights_in[s % RING].sem, k.weights_in[s % RING].at(16 * (s // RING + 1)))
                if s >= RING:
                    act.wait_ge(k.product_done.sem, k.product_done.at((s - RING + 1) * tiles))
                nc.scalar.activation(high[s % RING][:, 0:n], raw[s % RING][:, 0:n], ACT.Copy).then_inc(k.w_high.sem, 1)

            for s in range(RING - 1):
                round_rows(s)
            for s, (b, c) in enumerate(steps):
                if s + RING - 1 < len(steps):
                    round_rows(s + RING - 1)
                if c == KD - 1:
                    for i in range(tiles):
                        act.wait_ge(k.product_done.sem, k.product_done.at(s * tiles + i + 1))
                        nc.scalar.activation(blocks[b][2](i), k.psum[:, (b * tiles + i) % 8, 0:blocks[b][1]], ACT.Copy).then_inc(taken.sem, 1)

        @block.vector
        def _(dve):
            for s, (b, c) in enumerate(steps):
                n = blocks[b][1]
                dve.wait_ge(k.w_high.sem, k.w_high.at(s + 1))
                nc.vector.tensor_tensor(low[s % RING][:, 0:n], raw[s % RING][:, 0:n], high[s % RING][:, 0:n].bitcast(F32), ALU.subtract
                                        ).then_inc(k.w_low.sem, 1)

        @block.tensor
        def _(pe):
            for s, (b, c) in enumerate(steps):
                n = blocks[b][1]
                pe.wait_ge(k.w_low.sem, k.w_low.at(s + 1))
                for i in range(tiles):
                    job = b * tiles + i
                    if c == 0 and job >= 8:
                        pe.wait_ge(taken.sem, taken.at(job - 7))
                    t = slice(i * P, (i + 1) * P)
                    split_product(nc, k.psum[:, job % 8, 0:n], k.h_high[:, c, t], k.h_low[:, c, t], high[s % RING][:, 0:n], low[s % RING][:, 0:n],
                                  c == 0, c == KD - 1).then_inc(k.product_done.sem, 1)
    for r in range(RING):
        k.weights_in[r].base += 16 * len(range(r, len(steps), RING))
    k.product_done.base += len(steps) * tiles
    k.w_high.base += len(steps)
    k.w_low.base += len(steps)
    taken.base += len(blocks) * tiles


class First:

    def __init__(self, k):
        self.pT = k.place("projT", BIG, 16, SEQ)
        self.vm = k.place("vm", 24576, CHUNKS, BANK)
        self.va = k.place("va", 26624, CHUNKS, BANK)
        self.gates = k.place("gates", 28672, CHUNKS, 2 * M_HEADS)
        self.cT = k.place("convT", 28800, M_HEADS, SEQ)
        self.w_qk = k.place("w_qk", 30848, 2, M_HEADS, P)
        self.qT = k.place("m_qT", 31872, M_HEADS, SEQ)
        self.kT = k.place("m_kT", 33920, M_HEADS, SEQ)
        self.k_rows = k.place("m_k_rows", 35968, CHUNKS, M_HEADS, P)
        self.mixT = k.place("mixT", 10240, KD, SEQ)


M_SCALE = P ** -0.5


def stage_conv(k, t, f):
    nc = k.nc
    w_in, conv_done, c_ready, qk_summed, qk_taken, rows_summed = (
        k.sem(s) for s in ("w_qk_in", "conv_done", "c_ready", "qk_summed", "qk_taken", "k_rows_summed"))
    with nc.Block() as block:
        @block.sync
        def _(sp):
            sp.dma_start(f.w_qk[:, :, :, :], t["w_qk"]).then_inc(w_in, 16)

        @block.vector
        def _(dve):
            for h in range(M_HEADS):
                u, c = f.pT[:, h, :], f.cT[:, h, :]
                tap = lambda j: k.par("conv_w", h * 4 + j)
                k.dve(dve, nc.vector.tensor_scalar(c, u, tap(3), k.par("conv_b", h), ALU.mult, ALU.add))
                for back in (1, 2, 3):
                    ins = nc.vector.scalar_tensor_tensor(c[:, back:SEQ], u[:, 0:SEQ - back], tap(3 - back),
                                                         c[:, back:SEQ], ALU.mult, ALU.add)
                    if back < 3:
                        k.dve(dve, ins)
                    else:
                        ins.then_inc(conv_done, 1)
            for i in range(2 * M_HEADS):
                dve.wait_ge(qk_summed, i + 1)
                o, scale = (f.qT[:, i, :], 1.0) if i < M_HEADS else (f.kT[:, i - M_HEADS, :], M_SCALE)
                nc.vector.tensor_scalar(o, k.psum[:, i, :], scale, None, ALU.mult).then_inc(qk_taken, 1)
            for n in range(CHUNKS):
                dve.wait_ge(rows_summed, n + 1)
                nc.vector.tensor_scalar(f.k_rows[:, n, :, :].rearrange("p h d -> p (h d)"), k.psum[:, n, :], M_SCALE, None, ALU.mult)

        @block.scalar
        def _(act):
            for h in range(M_HEADS):
                act.wait_ge(conv_done, h + 1)
                nc.scalar.activation(f.cT[:, h, :], f.cT[:, h, :], ACT.Silu).then_inc(c_ready, 1)
            nc.scalar.activation(f.pT[:, 4:8, :], f.pT[:, 4:8, :], ACT.Sigmoid)

        @block.tensor
        def _(pe):
            pe.wait_ge(w_in, 16)
            for i in range(2 * M_HEADS):
                h = i % M_HEADS
                if i < M_HEADS:
                    pe.wait_ge(c_ready, h + 1)
                nc.tensor.matmul(k.psum[:, i, :], f.w_qk[:, i // M_HEADS, h, :], f.cT[:, h, :], start=True, stop=True).then_inc(qk_summed, 1)
            for n in range(CHUNKS):
                pe.wait_ge(qk_taken, n + 1)
                for h in range(M_HEADS):
                    mm = nc.tensor.matmul(k.psum[:, n, h * P:(h + 1) * P], f.cT[:, h, n * P:(n + 1) * P], f.w_qk[:, 1, h, :],
                                          start=True, stop=True)
                mm.then_inc(rows_summed, 1)


def stage_mlstm(k, t, f):
    nc = k.nc
    V = k.dve
    small = 51904
    v_aug = k.place("v_aug", 38016, UNITS, P + 1)
    dm = k.place("d_mat", 40080, UNITS, P)
    sdT = k.place("sdT", 42128, UNITS, P)
    state = k.place("state", 44176, CHUNKS - 1, M_HEADS, P + 1)
    pick = k.place("pick", 45728, UNITS, P, rows=UNITS)
    num = k.place("num", 47776, UNITS, P + 1)
    tmp = k.place("m_tmp", 49840, UNITS, P + 1)
    col = lambda i, n=UNITS: k.place(f"m_col{i}", small + i * UNITS, n)
    lf, li, b, g, inter, mt, iw, den, wts, bl = (col(i) for i in range(10))
    bcast = k.place("m_bcast", small + 10 * UNITS, 4, UNITS)
    line = k.place("m_line", small + 14 * UNITS, 6, UNITS, rows=1)
    rT = k.place("m_rT", small + 20 * UNITS, P, rows=UNITS)
    bT = k.place("m_bT", small + 20 * UNITS + P, P, rows=UNITS)
    mlT = k.place("m_mlT", small + 20 * UNITS + 2 * P, 1, rows=UNITS)
    gb = k.place("m_gb", small + 20 * UNITS + 2 * P + 32, CHUNKS, 2 * M_HEADS)
    (pick_in, gates_ready, soft_ready, lf_ready, cum_summed, r_ready, ml_ready, ml_turned, scan_ready, scan_exp, pack_ready,
     packed, g_ready, wts_ready, kw_ready, carried, rows_spread, d_ready, d_exp, scored, taken, sd_ready, turned, sdT_ready,
     state_ready, num_summed, num_taken, rms_ready, rms_done, h_ready, h_turned, h_taken) = (k.sem("m_" + s) for s in (
         "pick_in", "gates_ready", "soft_ready", "lf_ready", "cum_summed", "r_ready", "ml_ready", "ml_turned", "scan_ready",
         "scan_exp", "pack_ready", "packed", "g_ready", "wts_ready", "kw_ready", "carried", "rows_spread", "d_ready", "d_exp",
         "scored", "taken", "sd_ready", "turned", "sdT_ready", "state_ready", "num_summed", "num_taken", "rms_ready",
         "rms_done", "h_ready", "h_turned", "h_taken"))
    ps = k.psum
    flat4 = lambda bank: ps[:, bank:bank + 4, :].rearrange("p b (h l) -> p (b h) l", l=P)
    over = lambda c: c.unsqueeze(2).to_broadcast([P, UNITS, P])
    W1 = P + 1

    with nc.Block() as block:
        @block.sync
        def _(sp):
            sp.dma_start(pick[:, :, :], t["pick"]).then_inc(pick_in, 16)

        @block.vector
        def _(dve):
            bias = k.par("gate_b", 0, 2 * M_HEADS).unsqueeze(1).to_broadcast([P, CHUNKS, 2 * M_HEADS])
            V(dve, nc.vector.tensor_tensor(gb[:, :, :], f.gates[:, :, :], bias, ALU.add))
            by_unit = lambda c: c[:, :].rearrange("p (n h) -> p n h", h=M_HEADS)
            V(dve, nc.vector.tensor_copy(by_unit(li), gb[:, :, 0:M_HEADS]))
            V(dve, nc.vector.tensor_copy(by_unit(lf), gb[:, :, M_HEADS:2 * M_HEADS]))
            nc.vector.scalar_tensor_tensor(g[:, :], lf[:, :], -1.0, lf[:, :], ALU.mult, ALU.min).then_inc(gates_ready, 1)
            V(dve, nc.vector.tensor_scalar(lf[:, :], lf[:, :], 0.0, None, ALU.min))
            dve.wait_ge(soft_ready, 1)
            nc.vector.tensor_tensor(lf[:, :], lf[:, :], g[:, :], ALU.subtract).then_inc(lf_ready, 1)
            V(dve, nc.vector.memset(v_aug[:, :, P:W1], 1.0))
            V(dve, nc.vector.tensor_copy(v_aug[:, :, 0:P], f.vm[:, :, :].rearrange("p n (h d) -> p (n h) d", d=P)))
            dve.wait_ge(cum_summed, 1)
            V(dve, nc.vector.tensor_copy(b[:, :], ps[:, 0, 0:UNITS]))
            V(dve, nc.vector.tensor_copy(bl[:, :], ps[:, 0, UNITS:2 * UNITS]))
            V(dve, nc.vector.tensor_copy(line[0:1, 0, :], ps[0:1, 3, 0:UNITS]))
            V(dve, nc.vector.tensor_copy(bT[:, :], ps[0:UNITS, 1, 0:P]))
            nc.vector.tensor_tensor(rT[:, :], ps[0:UNITS, 2, 0:P], bT[:, :], ALU.subtract).then_inc(r_ready, 1)
            dve.wait_ge(r_ready, 1)
            V(dve, nc.vector.tensor_reduce(mlT[:, :], rT[:, :], AX_X, ALU.max))
            nc.vector.tensor_tensor(mlT[:, :], mlT[:, :], bT[:, P - 1:P], ALU.add).then_inc(ml_ready, 1)
            dve.wait_ge(ml_turned, 1)
            V(dve, nc.vector.tensor_copy(line[0:1, 4, :], ps[0:1, 3, UNITS:2 * UNITS]))
            V(dve, nc.vector.memset(line[0:1, 1, 0:M_HEADS], 0.0))
            for n in range(CHUNKS):
                s = slice(n * M_HEADS, (n + 1) * M_HEADS)
                V(dve, nc.vector.tensor_tensor(line[0:1, 2, s], line[0:1, 0, s], line[0:1, 1, s], ALU.add))
                m_new = line[0:1, 1, (n + 1) * M_HEADS:(n + 2) * M_HEADS] if n < CHUNKS - 1 else line[0:1, 5, 0:M_HEADS]
                V(dve, nc.vector.tensor_tensor(m_new, line[0:1, 2, s], line[0:1, 4, s], ALU.max))
                V(dve, nc.vector.tensor_tensor(line[0:1, 2, s], line[0:1, 2, s], m_new, ALU.subtract))
                last = nc.vector.tensor_tensor(line[0:1, 3, s], line[0:1, 4, s], m_new, ALU.subtract)
                if n < CHUNKS - 1:
                    V(dve, last)
            last.then_inc(scan_ready, 1)
            dve.wait_ge(packed, 1)
            V(dve, nc.vector.tensor_copy(bcast[:, :, :].rearrange("p a u -> p (a u)"), ps[:, 3, 64:64 + 4 * UNITS]))
            V(dve, nc.vector.tensor_tensor(g[:, :], bl[:, :], b[:, :], ALU.subtract))
            V(dve, nc.vector.tensor_tensor(g[:, :], g[:, :], li[:, :], ALU.add))
            nc.vector.tensor_tensor(g[:, :], g[:, :], bcast[:, 3, :], ALU.subtract).then_inc(g_ready, 1)
            V(dve, nc.vector.tensor_tensor(inter[:, :], b[:, :], bcast[:, 0, :], ALU.add))
            dve.wait_ge(wts_ready, 1)
            kr = f.k_rows[:, :, :, :].rearrange("p n h d -> p (n h) d")
            nc.vector.tensor_tensor(kr, kr, over(wts[:, :]), ALU.mult).then_inc(kw_ready, 1)
            dve.wait_ge(rows_spread, 1)
            V(dve, nc.vector.tensor_tensor(dm[:, :, :], flat4(4), over(b[:, :]), ALU.add))
            V(dve, nc.vector.tensor_tensor(dm[:, :, :], dm[:, :, :],
                                           k.const("causal").unsqueeze(1).to_broadcast([P, UNITS, P]), ALU.add))
            V(dve, nc.vector.tensor_reduce(mt[:, :], dm[:, :, :], AX_X, ALU.max))
            V(dve, nc.vector.tensor_tensor(mt[:, :], mt[:, :], inter[:, :], ALU.max))
            V(dve, nc.vector.tensor_tensor(iw[:, :], inter[:, :], mt[:, :], ALU.subtract))
            nc.vector.tensor_tensor(dm[:, :, :], dm[:, :, :], over(mt[:, :]), ALU.subtract).then_inc(d_ready, 1)
            dve.wait_ge(carried, 1)
            for n in range(CHUNKS - 1):
                for h in range(M_HEADS):
                    u = n * M_HEADS + h
                    cc = ps[:, u // 3, (u % 3) * W1:(u % 3 + 1) * W1]
                    own = nc.vector.tensor_scalar(state[:, n, h, :], cc, bcast[:, 2, u:u + 1], None, ALU.mult)
                    if n == 0:
                        own.then_inc(state_ready, 1)
                        continue
                    V(dve, own)
                    if h == 0:
                        dve.wait_ge(state_ready, n * M_HEADS)
                    nc.vector.scalar_tensor_tensor(state[:, n, h, :], state[:, n - 1, h, :], bcast[:, 1, u:u + 1],
                                                   state[:, n, h, :], ALU.mult, ALU.add).then_inc(state_ready, 1)
            dve.wait_ge(d_exp, 1)
            dve.wait_ge(scored, 1)
            nc.vector.tensor_tensor(dm[:, :, :], flat4(4), dm[:, :, :], ALU.mult).then_inc(sd_ready, 1)
            dve.wait_ge(turned, 1)
            nc.vector.tensor_copy(sdT[:, :, :], flat4(0)).then_inc(sdT_ready, 1)
            for n in range(CHUNKS):
                dve.wait_ge(num_summed, n + 1)
                for h in range(M_HEADS):
                    u = n * M_HEADS + h
                    own = ps[:, 4 + h // 2, (h % 2) * W1:(h % 2 + 1) * W1]
                    ins = nc.vector.tensor_copy(num[:, u, :], own)
                    if n:
                        V(dve, ins)
                        past = ps[:, 6 + h // 2, (h % 2) * W1:(h % 2 + 1) * W1]
                        ins = nc.vector.scalar_tensor_tensor(num[:, u, :], past, iw[:, u:u + 1], num[:, u, :], ALU.mult, ALU.add)
                    if h < M_HEADS - 1:
                        V(dve, ins)
                ins.then_inc(num_taken, 1)
            dve.wait_ge(num_taken, CHUNKS)
            row_sum = num[:, :, P:W1].rearrange("p u o -> p (u o)")
            V(dve, nc.vector.scalar_tensor_tensor(den[:, :], row_sum, -1.0, row_sum, ALU.mult, ALU.max))
            V(dve, nc.vector.tensor_tensor(den[:, :], den[:, :], mt[:, :], ALU.max))
            V(dve, nc.vector.reciprocal(den[:, :], den[:, :]))
            hn = num[:, :, 0:P]
            V(dve, nc.vector.tensor_tensor(hn, hn, over(den[:, :]), ALU.mult))
            V(dve, nc.vector.tensor_tensor(tmp[:, :, 0:P], hn, hn, ALU.mult))
            V(dve, nc.vector.tensor_reduce(wts[:, :], tmp[:, :, 0:P], AX_X, ALU.add))
            nc.vector.tensor_scalar(wts[:, :], wts[:, :], 1.0 / P, EPS, ALU.mult, ALU.add).then_inc(rms_ready, 1)
            dve.wait_ge(rms_done, 1)
            newton(k, dve, g[:, :], wts[:, :], den[:, :])
            nc.vector.tensor_tensor(hn, hn, over(g[:, :]), ALU.mult).then_inc(h_ready, 1)
            for h in range(M_HEADS):
                dve.wait_ge(h_turned, h + 1)
                c = f.cT[:, h, :]
                V(dve, nc.vector.tensor_scalar(c, c, k.par("skip", h), None, ALU.mult))
                V(dve, nc.vector.scalar_tensor_tensor(c, ps[:, h, :], k.par("mh_g", h), c, ALU.mult, ALU.add))
                V(dve, nc.vector.tensor_tensor(f.mixT[:, h, :], c, f.pT[:, M_HEADS + h, :], ALU.mult))

        @block.scalar
        def _(act):
            act.wait_ge(gates_ready, 1)
            k.act(act, nc.scalar.activation(g[:, :], g[:, :], ACT.Exp))
            nc.scalar.activation(g[:, :], g[:, :], ACT.Ln, bias=1.0).then_inc(soft_ready, 1)
            act.wait_ge(scan_ready, 1)
            nc.scalar.activation(line[0:1, 2:4, :], line[0:1, 2:4, :], ACT.Exp).then_inc(scan_exp, 1)
            act.wait_ge(g_ready, 1)
            nc.scalar.activation(wts[:, :], g[:, :], ACT.Exp).then_inc(wts_ready, 1)
            act.wait_ge(d_ready, 1)
            k.act(act, nc.scalar.activation(iw[:, :], iw[:, :], ACT.Exp))
            k.act(act, nc.scalar.activation(mt[:, :], mt[:, :], ACT.Exp, scale=-1.0))
            nc.scalar.activation(dm[:, :, :], dm[:, :, :], ACT.Exp).then_inc(d_exp, 1)
            act.wait_ge(rms_ready, 1)
            k.act(act, nc.scalar.activation(g[:, :], wts[:, :], ACT.Ln))
            nc.scalar.activation(g[:, :], g[:, :], ACT.Exp, scale=-0.5).then_inc(rms_done, 1)

        @block.tensor
        def _(pe):
            pe.wait_ge(lf_ready, 1)
            nc.tensor.matmul(ps[:, 0, 0:UNITS], k.const("tri"), lf[:, :], start=True, stop=True)
            nc.tensor.matmul(ps[:, 0, UNITS:2 * UNITS], k.const("ones"), lf[:, :], start=True, stop=True)
            nc.tensor.matmul(ps[0:UNITS, 1, 0:P], lf[:, :], k.const("tri"), start=True, stop=True)
            nc.tensor.matmul(ps[0:1, 3, 0:UNITS], k.const("ones")[:, 0:1], lf[:, :], start=True, stop=True)
            nc.tensor.matmul(ps[0:UNITS, 2, 0:P], li[:, :], k.const("ident"), start=True, stop=True).then_inc(cum_summed, 1)
            pe.wait_ge(ml_ready, 1)
            nc.tensor.matmul(ps[0:1, 3, UNITS:2 * UNITS], mlT[:, :], k.const("ident", UNITS)[:, 0:UNITS], start=True, stop=True).then_inc(ml_turned, 1)
            pe.wait_ge(pick_in, 16)
            for u in range(UNITS):
                mm = nc.tensor.matmul(flat4(4)[:, u, :], pick[:, u, :], rT[:, :], start=True, stop=True)
            mm.then_inc(rows_spread, 1)
            pe.wait_ge(scan_exp, 1)
            nc.tensor.matmul(ps[:, 3, 64:64 + 4 * UNITS], k.const("ones", 1), line[0:1, 1:5, :], start=True, stop=True).then_inc(packed, 1)
            pe.wait_ge(kw_ready, 1)
            for u in range(UNITS - M_HEADS):
                mm = nc.tensor.matmul(ps[:, u // 3, (u % 3) * W1:(u % 3 + 1) * W1], f.k_rows[:, u // M_HEADS, u % M_HEADS, :],
                                      v_aug[:, u, :], start=True, stop=True)
            mm.then_inc(carried, 1)
            pe.wait_ge(d_ready, 1)
            for n in range(CHUNKS):
                s = slice(n * P, (n + 1) * P)
                for h in range(M_HEADS):
                    mm = nc.tensor.matmul(flat4(4)[:, n * M_HEADS + h, :], f.qT[:, h, s], f.kT[:, h, s], start=True, stop=True)
            mm.then_inc(scored, 1)
            pe.wait_ge(sd_ready, 1)
            pe.wait_ge(state_ready, (CHUNKS - 1) * M_HEADS)
            for u in range(UNITS):
                mm = nc.tensor.transpose(flat4(0)[:, u, :], dm[:, u, :], k.const("ident"))
            mm.then_inc(turned, 1)
            pe.wait_ge(sdT_ready, 1)
            for n in range(CHUNKS):
                if n:
                    pe.wait_ge(num_taken, n)
                for h in range(M_HEADS):
                    o = slice((h % 2) * W1, (h % 2 + 1) * W1)
                    mm = nc.tensor.matmul(ps[:, 4 + h // 2, o], sdT[:, n * M_HEADS + h, :], v_aug[:, n * M_HEADS + h, :], start=True, stop=True)
                    if n:
                        mm = nc.tensor.matmul(ps[:, 6 + h // 2, o], f.qT[:, h, n * P:(n + 1) * P], state[:, n - 1, h, :], start=True, stop=True)
                mm.then_inc(num_summed, 1)
            pe.wait_ge(h_ready, 1)
            for h in range(M_HEADS):
                for n in range(CHUNKS):
                    mm = nc.tensor.transpose(ps[:, h, n * P:(n + 1) * P], num[:, n * M_HEADS + h, 0:P], k.const("ident"))
                mm.then_inc(h_turned, 1)


def stage_head_norm(k, name, jobs, at):
    nc = k.nc
    sq = k.place(f"{name}_sq", at, 4, TOK)
    v = k.place(f"{name}_v", at + 4 * TOK, 4, TOK)
    y = k.place(f"{name}_y", at + 8 * TOK, 4, TOK)
    squared, summed, v_ready, y_ready, scaled = signals = [k.shared(f"head_norm_{s}") for s in ("squared", "summed", "v_ready", "y_ready", "scaled")]
    with k.nc.Block() as block:
        @block.scalar
        def _(act):
            for j, (x, c0, pieces, _) in enumerate(jobs):
                w = sum(n for _, n in pieces)
                if j:
                    act.wait_ge(scaled.sem, scaled.at(j))
                nc.scalar.activation(sq[:, :, 0:w], x[:, c0:c0 + 4, 0:w], ACT.Square).then_inc(squared.sem, 1)
                act.wait_ge(v_ready.sem, v_ready.at(j + 1))
                k.act(act, nc.scalar.activation(y[:, :, 0:w], v[:, :, 0:w], ACT.Ln))
                nc.scalar.activation(y[:, :, 0:w], y[:, :, 0:w], ACT.Exp, scale=-0.5).then_inc(y_ready.sem, 1)

        @block.tensor
        def _(pe):
            for j, (_, _, pieces, _) in enumerate(jobs):
                pe.wait_ge(squared.sem, squared.at(j + 1))
                if j:
                    pe.wait_ge(v_ready.sem, v_ready.at(j))
                for i, (t0, n) in enumerate(pieces):
                    for c in range(4):
                        mm = nc.tensor.matmul(k.psum[:, 4 * i + c, 0:n], k.const("blocks"), sq[:, c, t0:t0 + n], start=True, stop=True)
                mm.then_inc(summed.sem, 1)

        @block.vector
        def _(dve):
            for j, (x, c0, pieces, gain) in enumerate(jobs):
                w = sum(n for _, n in pieces)
                dve.wait_ge(summed.sem, summed.at(j + 1))
                for i, (t0, n) in enumerate(pieces):
                    ins = nc.vector.tensor_scalar(v[:, :, t0:t0 + n], k.psum[:, 4 * i:4 * i + 4, 0:n], 1.0 / HEAD, EPS, ALU.mult, ALU.add)
                    if i < len(pieces) - 1:
                        k.dve(dve, ins)
                ins.then_inc(v_ready.sem, 1)
                dve.wait_ge(y_ready.sem, y_ready.at(j + 1))
                newton(k, dve, y[:, :, 0:w], v[:, :, 0:w], sq[:, :, 0:w])
                for c in range(4):
                    o = x[:, c0 + c, 0:w]
                    ins = nc.vector.scalar_tensor_tensor(o, o, gain(c0 + c), y[:, c, 0:w], ALU.mult, ALU.mult)
                    if c < 3:
                        k.dve(dve, ins)
                ins.then_inc(scaled.sem, 1)
    for s in signals:
        s.base += len(jobs)


def stage_dilated_table(k, t, tab, at):
    nc = k.nc
    z_len = SEQ + P
    rel = k.place("rel_bias", at, DIL_HEADS, rows=N_BUCKETS + 1)
    spread = k.place("rel_spread", at + 16, DIL_HEADS, P, rows=N_BUCKETS + 1)
    hot = k.place("bucket_hot", at + 16 + DIL_HEADS * P, z_len, rows=N_BUCKETS + 1)
    line = k.place("bias_line", at + 16 + DIL_HEADS * P + z_len, DIL_HEADS, z_len)
    tables_in, spread_ready, line_summed, line_ready, skew_out, skew_in = (k.sem("dil_" + s) for s in (
        "tables_in", "spread_ready", "line_summed", "line_ready", "skew_out", "skew_in"))
    skew = nc.dram_tensor("skew", (DIL_HEADS, P, z_len), F32)
    with nc.Block() as block:
        @block.sync
        def _(sp):
            sp.dma_start(rel[0:N_BUCKETS, :], t["rel_bias"]).then_inc(tables_in, 16)
            sp.dma_start(hot[:, :], t["bucket_hot"]).then_inc(tables_in, 16)
            for h in range(DIL_HEADS):
                sp.wait_ge(line_ready, 2 * h + 2)
                sp.dma_start(skew.ap()[h], line[:, h, :]).then_inc(skew_out, 16)
            sp.wait_ge(skew_out, 16 * DIL_HEADS)
            for h in range(DIL_HEADS):
                back = bass.AP(skew, h * P * z_len + P - 1, [[z_len - 1, P], [1, SEQ]])
                sp.dma_start(tab[:, h, :], back).then_inc(skew_in, 16)
            sp.wait_ge(skew_in, 16 * DIL_HEADS)

        @block.vector
        def _(dve):
            dve.wait_ge(tables_in, 32)
            k.dve(dve, nc.vector.memset(spread[N_BUCKETS:N_BUCKETS + 1, :, :], 1.0))
            nc.vector.tensor_copy(spread[0:N_BUCKETS, :, :], rel[0:N_BUCKETS, :].unsqueeze(2).to_broadcast([N_BUCKETS, DIL_HEADS, P])
                                  ).then_inc(spread_ready, 1)
            for h in range(DIL_HEADS):
                for i, (z0, n) in enumerate(((0, SEQ), (SEQ, P))):
                    dve.wait_ge(line_summed, 2 * h + i + 1)
                    nc.vector.tensor_copy(line[:, h, z0:z0 + n], k.psum[:, (2 * h + i) % 8, 0:n]).then_inc(line_ready, 1)

        @block.tensor
        def _(pe):
            pe.wait_ge(spread_ready, 1)
            for h in range(DIL_HEADS):
                for i, (z0, n) in enumerate(((0, SEQ), (SEQ, P))):
                    if 2 * h + i >= 8:
                        pe.wait_ge(line_ready, 2 * h + i - 7)
                    nc.tensor.matmul(k.psum[:, (2 * h + i) % 8, 0:n], spread[:, h, :], hot[:, z0:z0 + n], start=True, stop=True
                                     ).then_inc(line_summed, 1)


def stage_attention(k, name, times, units, stages, out, at, sink=None):
    nc = k.nc
    V = k.dve
    n_units = len(units)
    sc = k.place(f"{name}_scores", at, 2, TOK)
    pT = k.place(f"{name}_probsT", at + 2 * TOK, 2, TOK)
    stat = k.place(f"{name}_stat", at + 4 * TOK, 8)
    staged, scored, reduced, exped, normed, turned, copied, summed, stored = (k.shared(f"attention_{s}") for s in (
        "staged", "scored", "reduced", "exped", "normed", "turned", "copied", "summed", "stored"))
    n_stages = len(stages(0))
    n_out = len(out(0))
    scale = HEAD ** -0.5
    keys = lambda u: sum(n for _, n in units[u][1])
    nm = lambda b: stat[:, b:b + 1]
    den = lambda b: stat[:, 2 + b:3 + b]
    es = lambda b: stat[:, 4 + b:5 + b]

    with nc.Block() as block:
        @block.gpsimd
        def _(pool):
            with pool.Fori(0, times) as it:
                pool.wait_ge(summed.sem, summed.at(it * n_units + 2))
                for to, source in stages(it):
                    nc.gpsimd.tensor_copy(to, source).then_inc(staged.sem, 1)

        @block.tensor
        def _(pe):
            pe.sem_inc(turned.sem, 2)
            pe.sem_inc(summed.sem, 2)
            with pe.Fori(0, times) as it:
                def score(u):
                    pe.wait_ge(reduced.sem, reduced.at(it * n_units + (u + 1)))
                    for i, (kk, n) in enumerate(units[u][1]):
                        mm = nc.tensor.matmul(k.psum[:, (u % 2) * 2 + i, 0:n], units[u][0], kk, start=True, stop=True)
                    mm.then_inc(scored.sem, 1)

                pe.wait_ge(staged.sem, staged.at(it * n_stages + n_stages))
                score(0)
                pe.wait_ge(stored.sem, stored.at(it * n_out + n_out))
                for u, (_, _, _, values, o) in enumerate(units):
                    if u + 1 < n_units:
                        score(u + 1)
                    pe.wait_ge(normed.sem, normed.at(it * n_units + (u + 1)))
                    pe.wait_ge(copied.sem, copied.at(it * n_units + (u + 1)))
                    tiles = keys(u) // P
                    for j in range(tiles):
                        mm = nc.tensor.transpose(k.psum[:, 4 + j // 4, (j % 4) * P:(j % 4 + 1) * P], sc[:, u % 2, j * P:(j + 1) * P], k.const("ident"))
                    mm.then_inc(turned.sem, 1)
                    pe.wait_ge(copied.sem, copied.at(it * n_units + (u + 2)))
                    for j in range(tiles):
                        mm = nc.tensor.matmul(o, values(j), pT[:, u % 2, j * P:(j + 1) * P], start=(j == 0), stop=(j == tiles - 1))
                    mm.then_inc(summed.sem, 1)

        @block.vector
        def _(dve):
            dve.sem_inc(reduced.sem, 2)
            with dve.Fori(0, times) as it:
                V.restart(dve)

                def gather(u):
                    b = u % 2
                    dve.wait_ge(scored.sem, scored.at(it * n_units + (u + 1)))
                    dve.wait_ge(turned.sem, turned.at(it * n_units + (u + 1)))
                    at_key = 0
                    for i, (_, n) in enumerate(units[u][1]):
                        o, s = sc[:, b, at_key:at_key + n], k.psum[:, b * 2 + i, 0:n]
                        if i == 0 and units[u][2] is not None:
                            V(dve, nc.vector.scalar_tensor_tensor(o, s, scale, units[u][2](it), ALU.mult, ALU.add))
                        else:
                            V(dve, nc.vector.tensor_scalar(o, s, scale, None, ALU.mult))
                        at_key += n
                    if sink is None:
                        nc.vector.tensor_reduce(nm(b), sc[:, b, 0:at_key], AX_X, ALU.max, negate=True).then_inc(reduced.sem, 1)
                    else:
                        V(dve, nc.vector.tensor_reduce(nm(b), sc[:, b, 0:at_key], AX_X, ALU.max))
                        nc.vector.tensor_scalar(nm(b), nm(b), sink(u), -1.0, ALU.max, ALU.mult).then_inc(reduced.sem, 1)

                if sink is not None:
                    dve.wait_ge(staged.sem, staged.at(it * n_stages + n_stages))
                gather(0)
                for u in range(n_units):
                    if u + 1 < n_units:
                        gather(u + 1)
                    b = u % 2
                    dve.wait_ge(exped.sem, exped.at(it * n_units + (u + 1)))
                    if sink is not None:
                        V(dve, nc.vector.tensor_tensor(den(b), den(b), es(b), ALU.add))
                    V(dve, nc.vector.reciprocal(den(b), den(b)))
                    p = sc[:, b, 0:keys(u)]
                    nc.vector.tensor_scalar(p, p, den(b), None, ALU.mult).then_inc(normed.sem, 1)

        @block.scalar
        def _(act):
            act.sem_inc(copied.sem, 1)
            act.sem_inc(stored.sem, n_out)
            with act.Fori(0, times) as it:
                def exp(u):
                    b = u % 2
                    act.wait_ge(reduced.sem, reduced.at(it * n_units + (u + 3)))
                    p = sc[:, b, 0:keys(u)]
                    if sink is not None:
                        nc.scalar.activation(es(b), sink(u), ACT.Exp, bias=nm(b))
                    nc.scalar.activation(p, p, ACT.Exp, bias=nm(b), accum_out=den(b)).then_inc(exped.sem, 1)

                exp(0)
                for u in range(n_units):
                    if u + 1 < n_units:
                        exp(u + 1)
                    act.wait_ge(turned.sem, turned.at(it * n_units + (u + 3)))
                    act.wait_ge(summed.sem, summed.at(it * n_units + (u + 1)))
                    n = keys(u)
                    nc.scalar.activation(pT[:, u % 2, 0:n], k.psum[:, 4:6, :].rearrange("p b n -> p (b n)")[:, 0:n], ACT.Copy).then_inc(copied.sem, 1)
                act.wait_ge(summed.sem, summed.at(it * n_units + (n_units + 2)))
                for to, source in out(it):
                    nc.scalar.activation(to, source, ACT.Copy).then_inc(stored.sem, 1)
    for s in (scored, exped, normed):
        s.base += times * n_units
    for s, grant in ((reduced, 2), (turned, 2), (summed, 2), (copied, 1)):
        s.base += times * n_units + grant
    staged.base += times * n_stages
    stored.base += (times + 1) * n_out


def stage_dilated(k, t, f):
    tab = k.place("dil_tab", 28800, DIL_HEADS, SEQ)
    stage_dilated_table(k, t, tab, 32896)
    q, key = f.pT[:, 8:12, :], f.pT[:, 12:16, :]
    pieces = ((0, SEQ),)
    stage_head_norm(k, "dil_norm", [(f.pT, 8, pieces, lambda c: k.par("qn_g", c - 8)), (f.pT, 12, pieces, lambda c: k.par("kn_g", c - 12))], 33000)
    qs, ks, vs = (k.place("dil_" + s, 33000 + i * SEQ, SEQ) for i, s in enumerate(("qs", "ks", "vs")))
    v3 = vs[:, :].rearrange("p (t d) -> p t d", d=P)
    units = []
    for half in range(2):
        h = slice(half * HEAD, (half + 1) * HEAD)
        for i in range(TILES):
            n = (i + 1) * P
            units.append((qs[h, i * P:(i + 1) * P], [(ks[h, 0:n], n)],
                          lambda it, half=half, i=i, n=n: tab[:, bass.ds(it * 2 + half, 1), (3 - i) * P:(3 - i) * P + n].rearrange("p o y -> p (o y)"),
                          lambda j, h=h: v3[:, j, h], k.psum[h, 6, i * P:(i + 1) * P]))
    flat = lambda x: x.rearrange("p o y -> p (o y)")
    stage_attention(k, "dil", DIL_HEADS // 2, units,
                    lambda it: [(qs[:, :], flat(f.pT[:, bass.ds(it + 8, 1), :])), (ks[:, :], flat(f.pT[:, bass.ds(it + 12, 1), :])),
                                (v3, f.va[:, :, bass.ds(it * P, P)])],
                    lambda it: [(flat(f.mixT[:, bass.ds(it + 4, 1), :]), k.psum[:, 6, :])], 35000)


def add_to_x(k, gate, pieces, per=RING):
    def epilogue(dve, it, r, banks):
        for i, ((t0, n), bank) in enumerate(zip(pieces, banks)):
            x = k.xT[:, bass.ds(it * per + r, 1), t0:t0 + n].rearrange("p o y -> p (o y)")
            k.nc.vector.scalar_tensor_tensor(x, bank, gate(it * per + r, i), x, ALU.mult, ALU.add).then_inc(k.bank_read.sem, 1)
    return epilogue


def copy_to(k, place, pieces):
    def epilogue(dve, it, r, banks):
        for i, bank in enumerate(banks):
            k.nc.vector.tensor_copy(place(it, r, i), bank).then_inc(k.bank_read.sem, 1)
    return epilogue


def one(buf, c, t0, n):
    return buf[:, bass.ds(c, 1), t0:t0 + n].rearrange("p o y -> p (o y)")


LATENT = ((0, SEQ),)


def first_block(k, t, upto=99):
    stage_norm(k, LATENT, lambda i, c: k.par("norm1_g", c), None)
    f = First(k)
    with k.nc.Block() as block:
        product(k, block, t["w_projT"], 16, KD, LATENT, k.h_high, k.h_low, 28800,
                copy_to(k, lambda it, r, i: one(f.pT, it * RING + r, 0, SEQ), LATENT))
    stage_rows(k, t["w_projV"], 2, BANK, TILES, lambda b, i: (f.vm, f.va)[b][:, i, :], 28800,
               (t["w_gates"], 2 * M_HEADS, lambda i: f.gates[:, i, :]))
    stage_conv(k, t, f)
    stage_mlstm(k, t, f)
    stage_dilated(k, t, f)
    with k.nc.Block() as block:
        high, low = k.place("mix_high", BIG, KD, SEQ, dtype=FR), k.place("mix_low", BIG + KD * SEQ, KD, SEQ, dtype=FR)
        product(k, block, t["w_out"], KD, KD, LATENT, high, low, BIG + 2 * KD * SEQ, add_to_x(k, lambda c, i: 1.0, LATENT), full=f.mixT)
    return f


class Peer:

    def __init__(self, k):
        self.qT = k.place("peer_qT", BIG, 2 * PEER_HEADS, SEQ)
        self.picks = k.place("picks", PICKS_AT, 3, SEQ)
        self.gates = k.nc.dram_tensor("gates_dram", (N_KEYS, N_KEYS, SEQ), F32).ap()


def stage_topk(k, t, f):
    nc = k.nc
    V = k.dve
    H2 = 2 * PEER_HEADS
    at = 24576

    def take(name, *shape, dtype=F32):
        nonlocal at
        b = k.place("topk_" + name, at, *shape, dtype=dtype)
        at += int(np.prod(shape))
        return b

    keys = take("keys", H2, N_KEYS)
    qs = take("qs", H2, P)
    s = take("s", H2, N_KEYS)
    rest = take("rest", H2, N_KEYS)
    best = take("best", H2, TOPK)
    best_at = take("best_at", H2, TOPK, dtype=U32)
    best_f = take("best_f", H2, TOPK)
    cand = take("cand", PEER_HEADS, TOPK, TOPK)
    cand_rest = take("cand_rest", PEER_HEADS, TOPK * TOPK)
    top = take("top", PEER_HEADS, TOPK)
    top_at = take("top_at", PEER_HEADS, TOPK, dtype=U32)
    half_at = [take(f"half_at{i}", PICKS, dtype=U32) for i in range(2)]
    half_f = [take(f"half_f{i}", PICKS) for i in range(2)]
    equal = take("equal", PICKS, TOPK)
    out = [take(f"out{i}", PICKS) for i in range(3)]
    total = take("total", PEER_HEADS)
    mod = Modulation(k, t, at, 5, TILES)
    keys_in, staged, scored, copied, shifted, exped, picked, turned, stored = (k.sem("topk_" + x) for x in (
        "keys_in", "staged", "scored", "copied", "shifted", "exped", "picked", "turned", "stored"))
    with nc.Block() as block:
        @block.sync
        def _(sp):
            sp.dma_start(keys[:, :, :], t["keys"].rearrange("p (h n) -> p h n", n=N_KEYS)).then_inc(keys_in, 16)
            with sp.Fori(0, TILES) as it:
                mod.fetch(sp, it)

        @block.gpsimd
        def _(pool):
            pool.sem_inc(scored, 1)
            with pool.Fori(0, TILES) as it:
                pool.wait_ge(scored, it + 1)
                nc.gpsimd.tensor_copy(qs[:, :, :], f.qT[:, :, bass.ds(it * P, P)]).then_inc(staged, 1)

        @block.tensor
        def _(pe):
            mod.start(pe)
            pe.wait_ge(keys_in, 16)
            with pe.Fori(0, TILES) as it:
                pe.wait_ge(staged, it + 1)
                pe.wait_ge(copied, it + 1)
                for i in range(H2):
                    mm = nc.tensor.matmul(k.psum[:, i // 4, (i % 4) * P:(i % 4 + 1) * P], qs[:, i, :], keys[:, i, :], start=True, stop=True)
                mm.then_inc(scored, 1)
                mod.multiply(pe, it)
                pe.wait_ge(picked, it + 1)
                for i in range(3):
                    mm = nc.tensor.transpose(k.psum[:, 4, i * P:(i + 1) * P], out[i][:, :], k.const("ident"))
                mm.then_inc(turned, 1)

        @block.scalar
        def _(act):
            mod.condition(act)
            act.sem_inc(copied, 1)
            with act.Fori(0, TILES) as it:
                act.wait_ge(scored, it + 2)
                act.wait_ge(stored, it + 1)
                nc.scalar.activation(s[:, 4:H2, :].rearrange("p h n -> p (h n)"), k.psum[:, 1:4, :].rearrange("p b n -> p (b n)"), ACT.Copy).then_inc(copied, 1)
                act.wait_ge(shifted, it + 1)
                nc.scalar.activation(out[2][:, :], out[2][:, :], ACT.Exp).then_inc(exped, 1)

        @block.vector
        def _(dve):
            dve.sem_inc(stored, 1)
            with dve.Fori(0, TILES) as it:
                V.restart(dve)

                def best16(values, left, best, where):
                    V(dve, nc.vector.max(best[:, 0:8], values))
                    V(dve, nc.vector.max_index(where[:, 0:8], best[:, 0:8], values))
                    V(dve, nc.vector.match_replace(left, best[:, 0:8], values, -3e38))
                    V(dve, nc.vector.max(best[:, 8:16], left))
                    V(dve, nc.vector.max_index(where[:, 8:16], best[:, 8:16], left))

                dve.wait_ge(copied, it + 2)
                V(dve, nc.vector.tensor_copy(s[:, 0:4, :].rearrange("p h n -> p (h n)"), k.psum[:, 0, :]))
                for i in range(H2):
                    best16(s[:, i, :], rest[:, i, :], best[:, i, :], best_at[:, i, :])
                for h in range(PEER_HEADS):
                    first = best[:, 2 * h, :].unsqueeze(2).to_broadcast([P, TOPK, TOPK])
                    second = best[:, 2 * h + 1, :].unsqueeze(1).to_broadcast([P, TOPK, TOPK])
                    V(dve, nc.vector.tensor_tensor(cand[:, h, :, :], first, second, ALU.add))
                    best16(cand[:, h, :, :].rearrange("p a b -> p (a b)"), cand_rest[:, h, :], top[:, h, :], top_at[:, h, :])
                weight = out[2][:, :].rearrange("p (h s) -> p h s", s=TOPK)
                nc.vector.tensor_tensor(weight, top[:, :, :], top[:, :, 0:1].to_broadcast([P, PEER_HEADS, TOPK]), ALU.subtract).then_inc(shifted, 1)
                where = top_at[:, :, :].rearrange("p h s -> p (h s)")
                V(dve, nc.vector.tensor_scalar(half_at[0][:, :], where, 4, None, ALU.logical_shift_right))
                V(dve, nc.vector.tensor_scalar(half_at[1][:, :], where, TOPK - 1, None, ALU.bitwise_and))
                V(dve, nc.vector.tensor_copy(best_f[:, :, :], best_at[:, :, :]))
                for i in range(2):
                    V(dve, nc.vector.tensor_copy(half_f[i][:, :], half_at[i][:, :]))
                for i in range(2):
                    V(dve, nc.vector.tensor_tensor(equal[:, :, :], half_f[i][:, :].unsqueeze(2).to_broadcast([P, PICKS, TOPK]),
                                                   k.const("iota16").unsqueeze(1).to_broadcast([P, PICKS, TOPK]), ALU.is_equal))
                    eq = equal[:, :, :].rearrange("p (h s) a -> p h s a", s=TOPK)
                    number = best_f[:, :, :].rearrange("p (h i) a -> p h i a", i=2)[:, :, i, :].unsqueeze(2).to_broadcast([P, PEER_HEADS, TOPK, TOPK])
                    V(dve, nc.vector.tensor_tensor(eq, eq, number, ALU.mult))
                    V(dve, nc.vector.tensor_reduce(out[i][:, :], equal[:, :, :], AX_X, ALU.add))
                dve.wait_ge(exped, it + 1)
                V(dve, nc.vector.tensor_reduce(total[:, :], weight, AX_X, ALU.add))
                V(dve, nc.vector.reciprocal(total[:, :], total[:, :]))
                nc.vector.tensor_tensor(weight, weight, total[:, :].unsqueeze(2).to_broadcast([P, PEER_HEADS, TOPK]), ALU.mult).then_inc(picked, 1)
                dve.wait_ge(turned, it + 1)
                nc.vector.tensor_copy(f.picks[:, :, bass.ds(it * P, P)], k.psum[:, 4, 0:3 * P].rearrange("p (i n) -> p i n", n=P)).then_inc(stored, 1)
            mod.finish(dve)


GATE_TOK = 64
GROUP = 8


def stage_gates(k, f):
    nc = k.nc
    hot1 = k.place("hot1", BIG, 2, GROUP, N_KEYS)
    hot2 = k.place("hot2", BIG + 2 * GROUP * N_KEYS, 2, GROUP, N_KEYS)
    plane = k.place("gate_plane", BIG + 4 * GROUP * N_KEYS, 2, N_KEYS, GATE_TOK)
    groups = GATE_TOK // GROUP
    hot1_ready, hot2_ready, summed, taken = (k.sem("gates_" + x) for x in ("hot1_ready", "hot2_ready", "summed", "taken"))
    stored = [k.sem(f"gates_stored{b}") for b in range(2)]
    times = SEQ // (2 * GATE_TOK)
    n_body = 2 * groups
    mine = k.place("gate_first", BIG + 4 * GROUP * N_KEYS + 2 * N_KEYS * GATE_TOK, 2, GROUP)
    own = k.place("gate_second", BIG + 4 * GROUP * N_KEYS + 2 * N_KEYS * GATE_TOK + 2 * GROUP, 2, 3, GROUP)
    by_pool = 5

    def tokens(it, g):
        return bass.ds(it * (2 * GATE_TOK) + g * GROUP, GROUP)

    with nc.Block() as block:
        @block.gpsimd
        def _(pool):
            pool.sem_inc(summed, 2)
            with pool.Fori(0, times) as it:
                k.pool.restart(pool)
                for g in range(n_body):
                    b = g % 2
                    pool.wait_ge(summed, it * n_body + (g + 1))
                    k.pool(pool, nc.gpsimd.tensor_copy(mine[:, b, :], f.picks[:, 0, tokens(it, g)]))
                    for j in range(by_pool):
                        hot = nc.gpsimd.tensor_scalar(hot1[:, b, j, :], k.const("iota"), mine[:, b, j:j + 1], None, ALU.is_equal)
                    hot.then_inc(hot1_ready, 1)

        @block.vector
        def _(dve):
            with dve.Fori(0, times) as it:
                k.dve.restart(dve)
                for g in range(n_body):
                    b = g % 2
                    dve.wait_ge(summed, it * n_body + (g + 1))
                    k.dve(dve, nc.vector.tensor_copy(own[:, b, :, :], f.picks[:, :, tokens(it, g)]))
                    for j in range(by_pool, GROUP):
                        nc.vector.tensor_scalar(hot1[:, b, j, :], k.const("iota"), own[:, b, 0, j:j + 1], None, ALU.is_equal)
                    for j in range(GROUP):
                        hot = nc.vector.tensor_scalar(hot2[:, b, j, :], k.const("iota"), own[:, b, 1, j:j + 1], own[:, b, 2, j:j + 1],
                                                      ALU.is_equal, ALU.mult)
                    hot.then_inc(hot2_ready, 1)

        @block.tensor
        def _(pe):
            with pe.Fori(0, times) as it:
                for g in range(n_body):
                    pe.wait_ge(hot1_ready, it * n_body + (g + 1))
                    pe.wait_ge(hot2_ready, it * n_body + (g + 1))
                    pe.wait_ge(taken, it * n_body + (g + 1))
                    for j in range(GROUP):
                        mm = nc.tensor.matmul(k.psum[:, 2 * (g % 4) + j // 4, (j % 4) * P:(j % 4 + 1) * P], hot1[:, g % 2, j, :], hot2[:, g % 2, j, :],
                                              start=True, stop=True)
                    mm.then_inc(summed, 1)

        @block.scalar
        def _(act):
            act.sem_inc(taken, 4)
            with act.Fori(0, times) as it:
                for g in range(n_body):
                    b = g // groups
                    act.wait_ge(summed, it * n_body + (g + 3))
                    if g % groups == 0:
                        act.wait_ge(stored[b], it * 16 + 16)
                    o = plane[:, b, :, (g % groups) * GROUP:(g % groups + 1) * GROUP].rearrange("p e t -> p t e")
                    nc.scalar.activation(o, k.psum[:, 2 * (g % 4):2 * (g % 4) + 2, :].rearrange("p b (t e) -> p (b t) e", e=N_KEYS), ACT.Copy).then_inc(taken, 1)

        @block.sync
        def _(sp):
            for b in range(2):
                sp.sem_inc(stored[b], 16)
            with sp.Fori(0, times) as it:
                for b in range(2):
                    sp.wait_ge(taken, it * n_body + (4 + (b + 1) * groups))
                    o = f.gates.rearrange("c e t -> e c t")[:, :, bass.ds(it * (2 * GATE_TOK) + b * GATE_TOK, GATE_TOK)]
                    sp.dma_start(o, plane[:, b, :, :]).then_inc(stored[b], 16)
            for b in range(2):
                sp.wait_ge(stored[b], 16 + times * 16)


def stage_experts(k, t, f):
    nc = k.nc
    eight, pair = range(8), 2
    at = BIG

    def take(name, n, *shape, dtype=F32):
        nonlocal at
        size = int(np.prod(shape))
        at += n * size
        return [k.place(f"{name}{r}", at + (r - n) * size, *shape, dtype=dtype) for r in range(n)]

    u_raw, v_raw, g_slot = take("u_raw", 4, KD, N_KEYS), take("v_raw", 4, D), take("g", 4, SEQ)
    u_high, u_low = take("u_high", 2, KD, N_KEYS, dtype=FR), take("u_low", 2, KD, N_KEYS, dtype=FR)
    v_high, v_low = take("v_high", 4, D, dtype=FR), take("v_low", 4, D, dtype=FR)
    a_high, a_low = take("a_high", 4, SEQ, dtype=FR), take("a_low", 4, SEQ, dtype=FR)
    gelu, a_full = take("gelu", 2, SEQ), take("a_full", 2, SEQ)
    u_in, v_in, g_in = ([k.sem(f"{x}_in{r}") for r in range(4)] for x in "uvg")
    (u_high_ready, u_split, v_high_ready, v_split, pre_done, gelu_done, gated, out_summed, x_added) = (
        k.sem("peer_" + x) for x in ("u_high_ready", "u_split", "v_high_ready", "v_split",
                                     "pre_done", "gelu_done", "gated", "out_summed", "x_added"))
    times = N_KEYS // 8
    v_rows = t["expert_v"].rearrange("(e c) d -> c e d", c=N_KEYS)

    with nc.Block() as block:
        @block.sync
        def _(sp):
            with sp.Fori(0, times) as it:
                for r in eight:
                    c = it * 8 + r
                    sp.wait_ge(u_split, it * 8 + (r + 1))
                    sp.dma_start(u_raw[r % 4][:, :, :], t["expert_uT"][c].rearrange("p (k e) -> p k e", e=N_KEYS)).then_inc(u_in[r % 4], 16)
                    sp.wait_ge(v_split, it * 8 + (r + 1))
                    sp.dma_start(v_raw[r % 4][:, :], v_rows[c]).then_inc(v_in[r % 4], 16)
                    sp.wait_ge(gated, it * 8 + (r + 1))
                    sp.dma_start(g_slot[r % 4][:, :], f.gates[c]).then_inc(g_in[r % 4], 16)

        @block.scalar
        def _(act):
            act.sem_inc(gelu_done, 2)
            with act.Fori(0, times) as it:
                def round_u(r):
                    act.wait_ge(u_in[r % 4], it * 32 + 16 * (r // 4 + 1))
                    act.wait_ge(pre_done, it * 8 + (r + 1))
                    nc.scalar.activation(u_high[r % 2][:, :, :], u_raw[r % 4][:, :, :], ACT.Copy).then_inc(u_high_ready, 1)

                round_u(0)
                for r in eight:
                    if r < 7:
                        round_u(r + 1)
                    act.wait_ge(v_in[r % 4], it * 32 + 16 * (r // 4 + 1))
                    act.wait_ge(out_summed, it * 32 + (r // pair * KD + KD))
                    nc.scalar.activation(v_high[r % 4][:, :], v_raw[r % 4][:, :], ACT.Copy).then_inc(v_high_ready, 1)
                    act.wait_ge(pre_done, it * 8 + (2 + r + 1))
                    act.wait_ge(gated, it * 8 + (4 + r - 1))
                    nc.scalar.activation(gelu[r % 2][:, :], k.psum[:, r % 2, :], ACT.Gelu).then_inc(gelu_done, 1)

        @block.gpsimd
        def _(pool):
            pool.sem_inc(u_split, 4)
            with pool.Fori(0, times) as it:
                for r in eight:
                    pool.wait_ge(u_high_ready, it * 8 + (r + 1))
                    nc.gpsimd.tensor_tensor(u_low[r % 2][:, :, :], u_raw[r % 4][:, :, :], u_high[r % 2][:, :, :].bitcast(F32), ALU.subtract
                                            ).then_inc(u_split, 1)

        @block.tensor
        def _(pe):
            pe.sem_inc(pre_done, 2)
            pe.sem_inc(out_summed, 2 * KD)
            with pe.Fori(0, times) as it:
                def multiply_u(r):
                    pe.wait_ge(u_split, it * 8 + (4 + r + 1))
                    pe.wait_ge(gelu_done, it * 8 + (r + 1))
                    for c in range(KD):
                        mm = split_product(nc, k.psum[:, r % 2, :], u_high[r % 2][:, c, :], u_low[r % 2][:, c, :], k.h_high[:, c, 0:SEQ], k.h_low[:, c, 0:SEQ],
                                           c == 0, c == KD - 1)
                    mm.then_inc(pre_done, 1)

                def multiply_v(q):
                    pe.wait_ge(v_split, it * 8 + (4 + (q + 1) * pair))
                    pe.wait_ge(gated, it * 8 + (4 + (q + 1) * pair))
                    for d in range(KD):
                        pe.wait_ge(x_added, it * 32 + (q * KD + d + 1))
                        for j in range(pair):
                            r = (q * pair + j) % 4
                            s = slice(d * P, (d + 1) * P)
                            mm = split_product(nc, k.psum[:, 2 + d % 4, :], v_high[r][:, s], v_low[r][:, s], a_high[r][:, :], a_low[r][:, :],
                                               j == 0, j == pair - 1)
                        mm.then_inc(out_summed, 1)

                for r in eight:
                    multiply_u(r)
                    if r in (3, 5, 7):
                        multiply_v((r - 3) // pair)
                multiply_v(3)

        @block.vector
        def _(dve):
            dve.sem_inc(gated, 4)
            dve.sem_inc(x_added, 4)
            dve.sem_inc(v_split, 4)
            with dve.Fori(0, times) as it:
                k.dve.restart(dve)

                def add(q):
                    for d in range(KD):
                        dve.wait_ge(out_summed, it * 32 + (2 * KD + q * KD + d + 1))
                        x = k.xT[:, d, 0:SEQ]
                        nc.vector.tensor_tensor(x, x, k.psum[:, 2 + d % 4, :], ALU.add).then_inc(x_added, 1)

                for r in eight:
                    dve.wait_ge(v_high_ready, it * 8 + (r + 1))
                    nc.vector.tensor_tensor(v_low[r % 4][:, :], v_raw[r % 4][:, :], v_high[r % 4][:, :].bitcast(F32), ALU.subtract).then_inc(v_split, 1)
                    dve.wait_ge(gelu_done, it * 8 + (2 + r + 1))
                    dve.wait_ge(g_in[r % 4], it * 32 + 16 * (r // 4 + 1))
                    k.dve(dve, nc.vector.tensor_tensor(a_full[r % 2][:, :], gelu[r % 2][:, :], g_slot[r % 4][:, :], ALU.mult))
                    dve.wait_ge(out_summed, it * 32 + (r // pair * KD + KD))
                    k.dve(dve, nc.vector.tensor_copy(a_high[r % 4][:, :], a_full[r % 2][:, :]))
                    nc.vector.tensor_tensor(a_low[r % 4][:, :], a_full[r % 2][:, :], a_high[r % 4][:, :].bitcast(F32), ALU.subtract).then_inc(gated, 1)
                    if r in (3, 5, 7):
                        add((r - 3) // pair)
                add(3)


def peer(k, t):
    f = Peer(k)
    stage_norm(k, LATENT, lambda i, c: k.par("norm2_g", c), None)
    with k.nc.Block() as block:
        product(k, block, t["w_query"], 2 * PEER_HEADS, KD, LATENT, k.h_high, k.h_low, BIG + 2 * PEER_HEADS * SEQ,
                copy_to(k, lambda it, r, i: one(f.qT, it * RING + r, 0, SEQ), LATENT))
    stage_topk(k, t, f)
    stage_gates(k, f)
    stage_experts(k, t, f)
    return f


class Layer:

    def __init__(self, k, i):
        self.q = k.place(f"q{i}", BIG, KD, TOK)
        self.key = k.place(f"k{i}", BIG + KD * TOK, KD, TOK)
        self.v = k.place(f"v_rows{i}", BIG + 2 * KD * TOK, ALL_TILES, D)


FREE = BIG + 3 * KD * TOK


def mod_col(k, layer, which, c, piece):
    return k.modT[:, bass.ds(c + (layer * MODS + which * KD), 1), piece]


def stage_gain(k, layer, name, which):
    with k.nc.Block() as block:
        @block.vector
        def _(dve):
            j = layer * MODS + which * KD
            for i in range(2):
                k.dve(dve, k.nc.vector.tensor_tensor(k.gain[:, i, :], k.par(name, layer * KD, KD), k.modT[:, j:j + KD, i], ALU.mult))


def modulated_norm(k, layer, name, first, pieces):
    stage_gain(k, layer, name, first + 1)
    stage_norm(k, pieces, lambda i, c: k.gain[:, i, c:c + 1], lambda i, c: mod_col(k, layer, first, c, i))


def stage_na_table(k, t, tab):
    nc = k.nc
    half_cols = GRID_W // 2
    shift = k.place("na_shift", 10240, half_cols, P, rows=RPB_W + 1)
    rpb = k.place("na_rpb", 10240 + half_cols * P, NA_HEADS * RPB_H, rows=RPB_W + 1)
    tables_in, summed, taken = (k.sem("na_table_" + s) for s in ("in", "summed", "taken"))
    wide = NA_HEADS * RPB_H
    n_pairs = GRID_W // 2
    with nc.Block() as block:
        @block.sync
        def _(sp):
            sp.dma_start(rpb[:, :], t["rpbT"]).then_inc(tables_in, 16)
            s = t["shift"].rearrange("x (c p) -> x c p", p=P)
            sp.dma_start(shift[:, :, :], s[:, 0:half_cols, :]).then_inc(tables_in, 16)
            sp.wait_ge(summed, n_pairs // 2)
            sp.dma_start(shift[:, :, :], s[:, half_cols:GRID_W, :]).then_inc(tables_in, 16)

        @block.tensor
        def _(pe):
            for j in range(n_pairs):
                if j == 0:
                    pe.wait_ge(tables_in, 32)
                if j == n_pairs // 2:
                    pe.wait_ge(tables_in, 48)
                if j >= 8:
                    pe.wait_ge(taken, 2 * (j - 7))
                for i in range(2):
                    mm = nc.tensor.matmul(k.psum[:, j % 8, i * wide:(i + 1) * wide], shift[:, (2 * j + i) % half_cols, :], rpb[:, :], start=True, stop=True)
                mm.then_inc(summed, 1)

        @block.vector
        def _(dve):
            for j in range(n_pairs):
                dve.wait_ge(summed, j + 1)
                for half in range(2):
                    p = slice(half * HEAD, (half + 1) * HEAD)
                    o = tab[p, :, half:half + RPB_H, 2 * j:2 * j + 2]
                    nc.vector.tensor_copy(o, k.psum[p, j % 8, 0:2 * wide].rearrange("p (c h s) -> p h s c", c=2, s=RPB_H)).then_inc(taken, 1)


def na_layer(k, t, layer):
    b = Layer(k, layer)
    both = PIECES
    modulated_norm(k, layer, "g_attn", 0, both)
    with k.nc.Block() as block:
        product(k, block, t["na_qk"][0:KD], KD, KD, both, k.h_high, k.h_low, FREE,
                copy_to(k, lambda it, r, i: one(b.q, it * RING + r, *both[i]), both))
    with k.nc.Block() as block:
        product(k, block, t["na_qk"][KD:2 * KD], KD, KD, both, k.h_high, k.h_low, FREE,
                copy_to(k, lambda it, r, i: one(b.key, it * RING + r, *both[i]), both))
    stage_rows(k, t["na_v"], 2, BANK, ALL_TILES, lambda n, i: b.v[:, i, n * BANK:(n + 1) * BANK], FREE)
    stage_head_norm(k, "na_norm", [(x, c0, both, lambda c, g=g: k.par(g)) for x, g in ((b.q, "na_gq"), (b.key, "na_gk")) for c0 in (0, 4)], FREE)
    tab = k.place("na_tab", FREE, NA_HEADS, RPB_H + 1, GRID_W)
    stage_na_table(k, t, tab)
    qs, ks, vs = (k.place("na_" + s, 10240 + i * TOK, TOK) for i, s in enumerate(("qs", "ks", "vs")))
    v3 = vs[:, :].rearrange("p (t d) -> p t d", d=P)
    units = []
    for half in range(2):
        h = slice(half * HEAD, (half + 1) * HEAD)
        context = (ks[h, SEQ:TOK], CTX)
        for i in range(TILES):
            units.append((qs[h, i * P:(i + 1) * P], [(ks[h, 0:SEQ], SEQ), context],
                          lambda it, half=half, i=i: tab[:, bass.ds(it * 2 + half, 1), 7 - 2 * i:15 - 2 * i, :].rearrange("p o s c -> p (o s c)"),
                          lambda j, h=h: v3[:, j, h], k.psum[h, 6, i * P:(i + 1) * P]))
        for i in range(CTX // P):
            units.append((qs[h, SEQ + i * P:SEQ + (i + 1) * P], [context], None,
                          lambda j, h=h: v3[:, TILES + j, h], k.psum[h, 7, i * P:(i + 1) * P]))
    stage_attention(k, "na", NA_HEADS // 2, units,
                    lambda it: [(qs[:, :], one(b.q, it, 0, TOK)), (ks[:, :], one(b.key, it, 0, TOK)), (v3, b.v[:, :, bass.ds(it * P, P)])],
                    lambda it: [(one(b.q, it, t0, n), k.psum[:, 6 + i, 0:n]) for i, (t0, n) in enumerate(both)], 10240 + 3 * TOK)
    with k.nc.Block() as block:
        high, low = split_of_q(k, "na", layer)
        product(k, block, t["na_o"], KD, KD, both, high, low, FREE, add_to_x(k, lambda c, i: mod_col(k, layer, 2, c, i), both), full=b.q)


def split_of_q(k, name, layer):
    return k.place(f"{name}_o_high", H_HIGH, KD, TOK, dtype=FR), k.place(f"{name}_o_low", BIG, KD, TOK, dtype=FR)


def stage_rope(k, t, jobs, at):
    nc = k.nc
    rope = k.place("rope", at, 2, SEQ)
    part = k.place("rope_part", at + 2 * SEQ, 2, SEQ)
    rope_in, swapped, turned = (k.sem("rope_" + s) for s in ("in", "swapped", "turned"))
    with nc.Block() as block:
        @block.sync
        def _(sp):
            sp.dma_start(rope[:, :, :], t["rope"]).then_inc(rope_in, 16)

        @block.tensor
        def _(pe):
            for j, x in enumerate(jobs):
                if j >= 8:
                    pe.wait_ge(turned, j - 7)
                nc.tensor.matmul(k.psum[:, j % 8, :], k.const("swap"), x, start=True, stop=True).then_inc(swapped, 1)

        @block.vector
        def _(dve):
            dve.wait_ge(rope_in, 16)
            for j, x in enumerate(jobs):
                dve.wait_ge(swapped, j + 1)
                k.dve(dve, nc.vector.tensor_tensor(part[:, j % 2, :], k.psum[:, j % 8, :], rope[:, 1, :], ALU.mult))
                k.dve(dve, nc.vector.tensor_tensor(x, x, rope[:, 0, :], ALU.mult))
                nc.vector.tensor_tensor(x, x, part[:, j % 2, :], ALU.add).then_inc(turned, 1)


def swa_layer(k, t, layer):
    b = Layer(k, layer)
    both = PIECES
    modulated_norm(k, layer, "g_attn", 0, both)
    with k.nc.Block() as block:
        product(k, block, t["swa_q"], KD, KD, LATENT, k.h_high, k.h_low, FREE, copy_to(k, lambda it, r, i: one(b.q, it * RING + r, 0, SEQ), LATENT))
    with k.nc.Block() as block:
        product(k, block, t["swa_k"], KV_HEADS, KD, both, k.h_high, k.h_low, FREE, copy_to(k, lambda it, r, i: one(b.key, it * RING + r, *both[i]), both))
    width = KV_HEADS * HEAD
    stage_rows(k, t["swa_v"], 1, width, ALL_TILES, lambda n, i: b.v[:, i, 0:width], FREE)
    stage_head_norm(k, "swa_norm", [(b.q, 0, LATENT, lambda c: k.par("swa_gq")), (b.q, 4, LATENT, lambda c: k.par("swa_gq")),
                                    (b.key, 0, both, lambda c: k.par("swa_gk"))], FREE)
    stage_rope(k, t, [b.q[:, c, 0:SEQ] for c in range(KD)] + [b.key[:, c, 0:SEQ] for c in range(KV_HEADS)], FREE)
    per = 2
    qs = k.place("swa_qs", FREE, per, SEQ)
    ks = k.place("swa_ks", FREE + per * SEQ, TOK)
    vs = k.place("swa_vs", FREE + per * SEQ + TOK, ALL_TILES, HEAD)
    sink = k.place("swa_sinks", FREE + per * SEQ + TOK + ALL_TILES * HEAD, 2 * per)
    units, sinks = [], []
    for qc in range(per):
        for half in range(2):
            h = slice(half * HEAD, (half + 1) * HEAD)
            for i in range(TILES):
                lo, hi = max(0, i - 1), min(TILES, i + 2)
                n = (hi - lo) * P
                y = (lo - (i - 1)) * P
                units.append((qs[h, qc, i * P:(i + 1) * P], [(ks[h, lo * P:hi * P], n), (ks[h, SEQ:TOK], CTX)],
                              lambda it, y=y, n=n: k.const("band")[:, y:y + n],
                              lambda j, lo=lo, hi=hi: vs[:, lo + j if j < hi - lo else TILES + j - (hi - lo), :],
                              k.psum[h, 6 + qc, i * P:(i + 1) * P]))
                sinks.append(sink[:, qc * 2 + half:qc * 2 + half + 1])
    stage_attention(k, "swa", KV_HEADS, units,
                    lambda it: [(qs[:, :, :], b.q[:, bass.ds(it * per, per), 0:SEQ]), (ks[:, :], one(b.key, it, 0, TOK)),
                                (vs[:, :, :], b.v[:, :, bass.ds(it * HEAD, HEAD)]), (sink[:, :], k.par("sink", it * (2 * per), 2 * per))],
                    lambda it: [(one(b.q, it * per + c, 0, SEQ), k.psum[:, 6 + c, :]) for c in range(per)], FREE + 4096, lambda u: sinks[u])
    with k.nc.Block() as block:
        high, low = split_of_q(k, "swa", layer)
        product(k, block, t["swa_o"], KD, KD, LATENT, high, low, FREE, add_to_x(k, lambda c, i: mod_col(k, layer, 2, c, i), LATENT), full=b.q)


def conv_ffn(k, t, layer, pieces):
    nc = k.nc
    modulated_norm(k, layer, "g_ffn", 3, pieces)
    act_T = k.place(f"ffn_act{layer}", BIG, FF_CHUNKS, TOK)
    at = BIG + FF_CHUNKS * TOK
    conv = k.place(f"ffn_conv{layer}", at, 2, 2, TOK)
    conv_done, silu_done = k.sem(f"ffn_conv_done{layer}"), k.sem(f"ffn_silu_done{layer}")
    width = sum(n for _, n in pieces)
    np_ = len(pieces)

    def epilogue(dve, it, r, banks):
        pair, gate = r // 2, r % 2
        j = it * RING + (layer * 2 * FF_CHUNKS + r)
        tap = lambda i: k.par("ffn_w", j * 3 + i)
        o = conv[:, pair, gate, :]
        for (t0, n), bank in zip(pieces, banks):
            k.dve(dve, nc.vector.tensor_scalar(o[:, t0:t0 + n], bank, tap(1), k.par("ffn_b", j), ALU.mult, ALU.add))
        for (t0, n), bank in zip(pieces, banks):
            k.dve(dve, nc.vector.scalar_tensor_tensor(o[:, t0 + 1:t0 + n], bank[:, 0:n - 1], tap(0), o[:, t0 + 1:t0 + n], ALU.mult, ALU.add))
        for (t0, n), bank in zip(pieces, banks):
            nc.vector.scalar_tensor_tensor(o[:, t0:t0 + n - 1], bank[:, 1:n], tap(2), o[:, t0:t0 + n - 1], ALU.mult, ALU.add).then_inc(k.bank_read.sem, 1)
        dve.wait_ge(k.bank_read.sem, k.bank_read.at((it * RING + (RING + r + 1)) * np_))
        if gate:
            dve.sem_inc(conv_done, 1)
            dve.wait_ge(silu_done, it * 2 + (pair + 1))
            k.dve(dve, nc.vector.tensor_tensor(act_T[:, bass.ds(it * 2 + pair, 1), 0:width].rearrange("p o y -> p (o y)"),
                                               conv[:, pair, 0, 0:width], conv[:, pair, 1, 0:width], ALU.mult))

    def silu(act, it, r):
        if r % 2:
            g = conv[:, r // 2, 1, 0:width]
            act.wait_ge(conv_done, it * 2 + (r // 2 + 1))
            nc.scalar.activation(g, g, ACT.Silu).then_inc(silu_done, 1)

    with nc.Block() as block:
        product(k, block, t[f"ffn_up{layer}"], 2 * FF_CHUNKS, KD, pieces, k.h_high, k.h_low, at + 4 * TOK, epilogue, silu)
    high, low = k.place(f"ffn_high{layer}", at, FF_CHUNKS, TOK, dtype=FR), k.place(f"ffn_low{layer}", BIG, FF_CHUNKS, TOK, dtype=FR)
    with nc.Block() as block:
        product(k, block, t[f"ffn_down{layer}"], KD, FF_CHUNKS, pieces, high, low, at + FF_CHUNKS * TOK,
                add_to_x(k, lambda c, i: mod_col(k, layer, 5, c, i), pieces, RING // 2), full=act_T, parts=2, split_at=H_HIGH)


def stage_store(k, out):
    stored = k.sem("stored")
    with k.nc.Block() as block:
        @block.sync
        def _(sp):
            sp.dma_start(out, k.xT[:, :, 0:SEQ]).then_inc(stored, 16)
            sp.wait_ge(stored, 16)


def build(nc, t, out):
    k = Core(nc)
    stage_load(k, t)
    first_block(k, t)
    peer(k, t)
    na_layer(k, t, 0)
    conv_ffn(k, t, 0, PIECES)
    swa_layer(k, t, 1)
    conv_ffn(k, t, 1, LATENT)
    stage_store(k, out)


def constants():
    f = np.float32
    p, x = np.arange(P)[:, None], np.arange(P)[None, :]
    parts = dict(
        ident=p == x, tri=p <= x, ones=np.ones((P, P)), iota=np.broadcast_to(x, (P, P)),
        blocks=p // HEAD == x // HEAD, swap=p == (x // HEAD) * HEAD + (x % HEAD + HEAD // 2) % HEAD,
        causal=np.where(x <= p, 0, NEG), iota16=np.broadcast_to(np.arange(TOPK)[None], (P, TOPK)),
        band=np.where(np.abs(p + P - np.arange(3 * P)[None]) <= RADIUS, 0, NEG))
    consts = np.concatenate([np.asarray(parts[n], f) for n in CONST_SIZES], 1)
    pick = np.zeros((UNITS, UNITS, P), f)
    pick[np.arange(UNITS), np.arange(UNITS)] = 1
    dist = SEQ - 1 - np.arange(SEQ + P)
    exact = N_BUCKETS // 2
    ratio = np.log(np.maximum(dist, 1).astype(f) / f(exact)) / np.log(2048 / exact)
    large = np.minimum(exact + (ratio * (N_BUCKETS - exact)).astype(np.int32), N_BUCKETS - 1)
    bucket = np.where(dist < exact, dist, large)
    hot = np.zeros((N_BUCKETS + 1, SEQ + P), f)
    ok = dist >= 0
    hot[bucket[ok], np.nonzero(ok)[0]] = 1
    count = (dist <= 128).astype(int) + (dist % 4 == 0) + (dist % 16 == 0)
    hot[N_BUCKETS] = np.where(ok & (count > 0), np.log(np.maximum(count, 1)), NEG)
    shift = np.zeros((RPB_W + 1, GRID_W, 2, GRID_W), f)
    for kc in range(GRID_W):
        for qc in range(GRID_W):
            start = min(max(qc - 8, 0), GRID_W - 16)
            if start <= kc < start + 16:
                shift[kc - qc + 15, kc, :, qc] = 1
            else:
                shift[RPB_W, kc, :, qc] = 1
    tok = np.arange(SEQ)
    inv = (10000.0 ** (-np.arange(16, dtype=f) / f(16))).astype(f)
    ang = np.concatenate([(tok // GRID_W).astype(f)[:, None] * inv, (tok % GRID_W).astype(f)[:, None] * inv], 1)
    d = np.arange(P) % HEAD
    cos = np.cos(ang)[:, d % 32].T.astype(f)
    sin = (np.sin(ang)[:, d % 32] * np.where(d < 32, -1, 1)).T.astype(f)
    return dict(consts=consts, pick=pick, bucket_hot=hot, shift=shift.reshape(RPB_W + 1, -1), rope=np.stack([cos, sin], 1))


def layouts(a):
    cc = np.ascontiguousarray

    def chunks(w):
        kk, n = w.shape
        return cc(w.reshape(kk // P, P, n // P, P).transpose(2, 1, 0, 3)).reshape(n // P, P, -1)

    def blocks(w, width):
        kk, n = w.shape
        return cc(w.reshape(kk // P, P, n // width, width).transpose(2, 1, 0, 3)).reshape(n // width, P, -1)

    def cols(v):
        return v.reshape(-1, P).T

    def rows(v):
        return np.broadcast_to(v.reshape(1, -1), (P, v.size))

    def ff(v):
        return v.reshape(*v.shape[:-1], 2, FF_CHUNKS, P).swapaxes(-3, -2)

    w_in = a["w_in"][0]
    mw, aw = M_HEADS * P, DIL_HEADS * HEAD
    u, vm, z, gates = w_in[:, 0:mw], w_in[:, mw:2 * mw], w_in[:, 2 * mw:3 * mw], w_in[:, 3 * mw:3 * mw + 2 * M_HEADS]
    at = 3 * mw + 2 * M_HEADS
    qa, ka, va = (w_in[:, at + i * aw:at + (i + 1) * aw] for i in range(3))
    qkv = a["swa_w_qkv_2"][0]
    swa_k = qkv[:, D:D + KV_HEADS * HEAD].reshape(D, KV_HEADS, 1, HEAD)
    swa_k = np.broadcast_to(swa_k, (D, KV_HEADS, 2, HEAD)).reshape(D, -1)
    na = a["na_w_qkv_2"][0]
    rpb = a["na_rpb_2"][0]
    rpbT = np.concatenate([rpb.transpose(2, 0, 1), np.full((1, NA_HEADS, RPB_H), NEG, np.float32)], 0)
    c2 = np.stack([a["c_2"][0], a["c_ctx_2"]], 1)
    parts = dict(
        norm1_g=cols(a["norm1_g"][0]), conv_w=a["conv_w"][0].reshape(4, M_HEADS, P).transpose(2, 1, 0).reshape(P, -1),
        conv_b=cols(a["conv_b"][0]), mh_g=cols(a["mh_norm_g"][0]), skip=cols(a["skip_m"][0]), qn_g=cols(a["qn_g"][0]),
        kn_g=cols(a["kn_g"][0]), norm2_g=cols(a["norm2_g"][0]), gate_b=rows(np.concatenate([a["ig_b"][0], a["fg_b"][0]])),
        g_attn=cols(a["g_attn_2"]), g_ffn=cols(a["g_ffn_2"]), b_mod=cols(a["b_mod_2"]),
        cond=c2.reshape(KD, P, 2).transpose(1, 0, 2).reshape(P, -1),
        na_gq=np.tile(a["na_g_q_2"][0], 2)[:, None], na_gk=np.tile(a["na_g_k_2"][0], 2)[:, None],
        swa_gq=np.tile(a["swa_g_q_2"][0], 2)[:, None], swa_gk=np.tile(a["swa_g_k_2"][0], 2)[:, None],
        sink=rows(a["swa_sink_2"][0]),
        ffn_w=ff(a["ffn_conv_w_2"]).transpose(4, 0, 2, 3, 1).reshape(P, -1),
        ffn_b=ff(a["ffn_conv_b_2"]).transpose(3, 0, 1, 2).reshape(P, -1))
    out = dict(constants())
    out.update(
        xT=cc(a["x"][0].T.reshape(KD, P, SEQ).transpose(1, 0, 2)), ctxT=cc(a["ctx_2"][0].T.reshape(KD, P, CTX).transpose(1, 0, 2)),
        params=cc(np.concatenate([parts[n] for n in PARAM_SIZES], 1)),
        w_mod=chunks(np.concatenate(list(a["w_mod_2"]), 1)),
        w_projT=chunks(np.concatenate([u, z, qa, ka], 1)), w_projV=blocks(np.concatenate([vm, va], 1), BANK),
        w_gates=blocks(gates, 2 * M_HEADS)[0],
        w_qk=cc(np.stack([a["wq_m"][0], a["wk_m"][0]]).transpose(2, 0, 1, 3)),
        rel_bias=a["rel_bias"], w_out=chunks(a["w_out"][0]), w_query=chunks(a["w_query"][0]),
        keys=cc(np.stack([a["sub_keys1"][0], a["sub_keys2"][0]]).transpose(3, 1, 0, 2)).reshape(P, -1),
        expert_uT=cc(a["expert_u"][0].reshape(N_KEYS, N_KEYS, KD, P).transpose(1, 3, 2, 0)).reshape(N_KEYS, P, -1),
        expert_v=a["expert_v"][0],
        na_qk=chunks(na[:, 0:2 * D]), na_v=blocks(na[:, 2 * D:], BANK), na_o=chunks(a["na_w_o_2"][0]), rpbT=cc(rpbT).reshape(RPB_W + 1, -1),
        swa_q=chunks(qkv[:, 0:D]), swa_k=chunks(swa_k), swa_v=blocks(qkv[:, D + KV_HEADS * HEAD:], KV_HEADS * HEAD),
        swa_o=chunks(a["swa_w_o_2"][0]))
    for i in range(LAYERS):
        out[f"ffn_up{i}"] = chunks(ff(a["ffn_w_up_2"][i]).reshape(D, -1))
        out[f"ffn_down{i}"] = chunks(a["ffn_w_down_2"][i])
    return {n: cc(v) for n, v in out.items()}


def kernel(**inputs):
    import concourse.bacc as bacc
    from concourse.bass_utils import run_bass_kernel_spmd as run

    arrays = layouts({n: np.asarray(v) for n, v in inputs.items()})
    nc = bacc.Bacc("TRN2", target_bir_lowering=False, num_devices=1)
    t = {n: nc.dram_tensor(f"in_{n}", v.shape, mybir.dt.from_np(v.dtype), kind="ExternalInput").ap() for n, v in arrays.items()}
    out = nc.dram_tensor("out_xT", (P, KD, SEQ), F32, kind="ExternalOutput").ap()
    build(nc, t, out)
    got = run(nc, [{f"in_{n}": v for n, v in arrays.items()}], core_ids=[0]).results[0]["out_xT"]
    return np.ascontiguousarray(np.asarray(got).transpose(1, 0, 2).reshape(D, SEQ).T)[None]
```

```python
import numpy as np

import concourse.bass as bass
from concourse import mybir

F32 = mybir.dt.float32
U32 = mybir.dt.uint32
FR = mybir.dt.float32r
ALU = mybir.AluOpType
ACT = mybir.ActivationFunctionType
AX_X = mybir.AxisListType.X

P = 128
BANK = 512
D = 1024
KD = D // P
SEQ = 512
CTX = 256
TOK = SEQ + CTX
TILES = SEQ // P
ALL_TILES = TOK // P
EPS = 1e-6
NEG = -1e30
RING = 4

M_HEADS = 4
CHUNKS = SEQ // P
UNITS = CHUNKS * M_HEADS
DIL_HEADS = 8
HEAD = 64
N_BUCKETS = 32
PEER_HEADS = 8
TOPK = 16
N_KEYS = 128
PICKS = PEER_HEADS * TOPK
NA_HEADS = 16
KV_HEADS = 4
GRID_W = 64
ROWS = SEQ // GRID_W
RPB_H = 15
RPB_W = 31
D_FF = 2816
FF_CHUNKS = D_FF // P
RADIUS = 128
LAYERS = 2
MODS = 6 * KD

PARAM_SIZES = dict(
    norm1_g=KD, conv_w=4 * M_HEADS, conv_b=M_HEADS, mh_g=M_HEADS, skip=M_HEADS, qn_g=4, kn_g=4, norm2_g=KD,
    gate_b=2 * M_HEADS, g_attn=LAYERS * KD, g_ffn=LAYERS * KD, b_mod=LAYERS * MODS,
    na_gq=1, na_gk=1, swa_gq=1, swa_gk=1, sink=NA_HEADS,
    ffn_w=LAYERS * 2 * FF_CHUNKS * 3, ffn_b=LAYERS * 2 * FF_CHUNKS,
)
CONST_SIZES = dict(ident=P, tri=P, ones=P, iota=P, blocks=P, swap=P, causal=P, iota16=TOPK, band=3 * P)


def offsets(sizes):
    out, at = {}, 0
    for name, n in sizes.items():
        out[name] = (at, n)
        at += n
    return out, at


PARAMS, N_PARAMS = offsets(PARAM_SIZES)
CONSTS, N_CONSTS = offsets(CONST_SIZES)

SBUF_START = 16512
SBUF_FLOATS = (229344 - SBUF_START) // 4
PICKS_AT = 8560
H_HIGH = 10240
BIG = H_HIGH + KD * TOK
H_LOW = 47064


class Chain:

    def __init__(self, sem):
        self.sem, self.n = sem, 0

    def __call__(self, eng, ins):
        self.n += 1
        ins.then_inc(self.sem, 1)
        eng.wait_ge(self.sem, self.n)

    def restart(self, eng):
        eng.sem_clear(self.sem)
        self.n = 0


class Signal:

    def __init__(self, sem):
        self.sem, self.base = sem, 0

    def at(self, n):
        return n + self.base


class Core:

    def __init__(self, nc):
        self.nc = nc
        self.names = 0
        self.signals = {}
        self.psum = nc.alloc_psum_tensor("psum", [P, 8, BANK], F32)
        self.dve = Chain(nc.alloc_semaphore("vector_done"))
        self.act = Chain(nc.alloc_semaphore("scalar_done"))
        self.pool = Chain(nc.alloc_semaphore("gpsimd_done"))
        self.weights_in = [Signal(nc.alloc_semaphore(f"weights_in{r}")) for r in range(RING)]
        self.product_done = Signal(nc.alloc_semaphore("product_done"))
        self.bank_read = Signal(nc.alloc_semaphore("bank_read"))
        self.xT = self.place("xT", 0, KD, TOK)
        self.params = self.place("params", 6144, N_PARAMS)
        self.consts = self.place("consts", 6144 + 704, N_CONSTS)
        self.modT = self.place("modT", 8304, LAYERS * MODS, 2)
        self.gain = self.place("gain", 8512, 2, KD)
        self.h_high = self.place("h_high", H_HIGH, KD, TOK, dtype=FR)
        self.h_low = self.place("h_low", H_LOW, KD, TOK, dtype=FR)
        self.w_high, self.w_low, self.x_high, self.x_low = (self.shared(s) for s in ("w_high", "w_low", "x_high", "x_low"))

    def place(self, name, at, *shape, dtype=F32, rows=P):
        n = int(np.prod(shape))
        assert at + n <= SBUF_FLOATS, (name, at + n, SBUF_FLOATS)
        return self.nc.alloc_sbuf_tensor_at(name, [rows, *shape], dtype, offset=SBUF_START + 4 * at)

    def sem(self, name):
        return self.nc.alloc_semaphore(name)

    def shared(self, name):
        if name not in self.signals:
            self.signals[name] = Signal(self.nc.alloc_semaphore(name))
        return self.signals[name]

    def par(self, name, i=0, n=1):
        return self.params[:, bass.ds(i + PARAMS[name][0], n)]

    def const(self, name, rows=P):
        at, n = CONSTS[name]
        return self.consts[0:rows, at:at + n]


PIECES = ((0, SEQ), (SEQ, CTX))


def stage_load(k, t):
    loaded = k.sem("loaded")
    with k.nc.Block() as block:
        @block.sync
        def _(sp):
            sp.dma_start(k.xT[:, :, 0:SEQ], t["xT"]).then_inc(loaded, 16)
            sp.dma_start(k.xT[:, :, SEQ:TOK], t["ctxT"]).then_inc(loaded, 16)
            sp.dma_start(k.params[:, :], t["params"]).then_inc(loaded, 16)
            sp.dma_start(k.consts[:, :], t["consts"]).then_inc(loaded, 16)
            sp.wait_ge(loaded, 64)


def split_product(nc, bank, w_high, w_low, x_high, x_low, first, last):
    nc.tensor.matmul(bank, w_high, x_high, start=first, stop=False)
    nc.tensor.matmul(bank, w_high, x_low, start=False, stop=False)
    return nc.tensor.matmul(bank, w_low, x_high, start=False, stop=last)


def product(k, block, w, n_chunks, k_chunks, pieces, high, low, at, epilogue, scalar=None, full=None, parts=1, split_at=None):
    nc = k.nc
    k.names += 1
    kp = k_chunks // parts
    n_raw = RING // parts
    raw = [k.place(f"w_raw{k.names}_{r}", at + r * kp * P, kp, P) for r in range(n_raw)]
    split_at = at + n_raw * kp * P if split_at is None else split_at
    w_high, w_low = ([k.place(f"w_{s}{k.names}_{r}", split_at + (2 * i + r) * kp * P, kp, P, dtype=FR) for r in range(2)]
                     for i, s in enumerate(("high", "low")))
    per = RING // parts
    passes = n_chunks // per
    n_pieces = len(pieces)
    width = sum(n for _, n in pieces)
    assert passes * per == n_chunks and kp * parts == k_chunks

    def banks(r):
        return [k.psum[:, r // parts * n_pieces + i, 0:n] for i, (_, n) in enumerate(pieces)]

    @block.sync
    def _(sp):
        with sp.Fori(0, passes) as it:
            for r in range(RING):
                sp.wait_ge(k.w_low.sem, k.w_low.at(it * RING + (r + 1)))
                source = w[it * per + r // parts].rearrange("p (k n) -> p k n", n=P)[:, r % parts * kp:(r % parts + 1) * kp, :]
                sp.dma_start(raw[r % n_raw][:, :, :], source).then_inc(k.weights_in[r % n_raw].sem, 16)

    @block.scalar
    def _(act):
        def round_weights(it, r):
            act.wait_ge(k.weights_in[r % n_raw].sem, k.weights_in[r % n_raw].at(it * (16 * parts) + 16 * (r // n_raw + 1)))
            if not (isinstance(it, int) and it * RING + r < 2):
                act.wait_ge(k.product_done.sem, k.product_done.at((it * RING + (r - 1)) * n_pieces))
            nc.scalar.activation(w_high[r % 2][:, :, :], raw[r % n_raw][:, :, :], ACT.Copy).then_inc(k.w_high.sem, 1)

        if full is not None:
            for c in range(k_chunks):
                if c == 4:
                    round_weights(0, 0)
                    round_weights(0, 1)
                nc.scalar.activation(high[:, c, 0:width], full[:, c, 0:width], ACT.Copy).then_inc(k.x_high.sem, 1)
        else:
            round_weights(0, 0)
            round_weights(0, 1)
        if passes > 1:
            with act.Fori(0, passes - 1) as it:
                for r in range(RING):
                    round_weights(it, r + 2)
                    if scalar:
                        scalar(act, it, r)
        for r in range(RING):
            if r + 2 < RING:
                round_weights(passes - 1, r + 2)
            if scalar:
                scalar(act, passes - 1, r)

    @block.gpsimd
    def _(pool):
        pool.sem_inc(k.w_low.sem, n_raw)
        with pool.Fori(0, passes) as it:
            for r in range(RING):
                pool.wait_ge(k.w_high.sem, k.w_high.at(it * RING + (r + 1)))
                nc.gpsimd.tensor_tensor(w_low[r % 2][:, :, :], raw[r % n_raw][:, :, :], w_high[r % 2][:, :, :].bitcast(F32), ALU.subtract
                                        ).then_inc(k.w_low.sem, 1)

    @block.tensor
    def _(pe):
        with pe.Fori(0, passes) as it:
            for r in range(RING):
                pe.wait_ge(k.w_low.sem, k.w_low.at(it * RING + (n_raw + r + 1)))
                part = r % parts
                if part == 0:
                    pe.wait_ge(k.bank_read.sem, k.bank_read.at((it * per + (r // parts + 1)) * n_pieces))
                for bank, (t0, n) in zip(banks(r), pieces):
                    for c in range(kp):
                        kc = part * kp + c
                        if full is not None:
                            pe.wait_ge(k.x_low.sem, k.x_low.at(kc + 1))
                        mm = split_product(nc, bank, w_high[r % 2][:, c, :], w_low[r % 2][:, c, :], high[:, kc, t0:t0 + n], low[:, kc, t0:t0 + n],
                                           kc == 0, kc == k_chunks - 1)
                    mm.then_inc(k.product_done.sem, 1)

    @block.vector
    def _(dve):
        if full is not None:
            for c in range(k_chunks):
                dve.wait_ge(k.x_high.sem, k.x_high.at(c + 1))
                nc.vector.tensor_tensor(low[:, c, 0:width], full[:, c, 0:width], high[:, c, 0:width].bitcast(F32), ALU.subtract
                                        ).then_inc(k.x_low.sem, 1)
        dve.sem_inc(k.bank_read.sem, per * n_pieces)
        with dve.Fori(0, passes) as it:
            k.dve.restart(dve)
            for r in range(parts - 1, RING, parts):
                dve.wait_ge(k.product_done.sem, k.product_done.at((it * RING + (r + 1)) * n_pieces))
                epilogue(dve, it, r // parts, banks(r))

    for s in k.weights_in[0:n_raw]:
        s.base += 16 * passes * parts
    k.product_done.base += n_chunks * parts * n_pieces
    k.bank_read.base += (n_chunks + per) * n_pieces
    k.w_high.base += n_chunks * parts
    k.w_low.base += n_chunks * parts + n_raw
    if full is not None:
        k.x_high.base += k_chunks
        k.x_low.base += k_chunks


def newton(k, dve, y, v, t):
    nc = k.nc
    k.dve(dve, nc.vector.tensor_tensor(t, y, y, ALU.mult))
    k.dve(dve, nc.vector.tensor_tensor(t, t, v, ALU.mult))
    k.dve(dve, nc.vector.tensor_scalar(t, t, -0.5, 1.5, ALU.mult, ALU.add))
    k.dve(dve, nc.vector.tensor_tensor(y, y, t, ALU.mult))


NEWTON = 4


def stage_norm(k, pieces, gain, shift):
    nc = k.nc
    k.names += 1
    width = sum(n for _, n in pieces)
    sq = k.place(f"norm_sq{k.names}", BIG, KD, TOK)
    v = k.place(f"norm_v{k.names}", BIG + KD * TOK, TOK)
    y = k.place(f"norm_y{k.names}", BIG + (KD + 1) * TOK, TOK)
    u = k.place(f"norm_u{k.names}", BIG + (KD + 2) * TOK, TOK)
    h = k.place(f"norm_h{k.names}", BIG + (KD + 3) * TOK, KD, TOK)
    sq_ready, sum_ready, v_ready, y_ready, h_ready, high_ready = (
        k.shared(f"norm_{s}") for s in ("sq_ready", "sum_ready", "v_ready", "y_ready", "h_ready", "high_ready"))
    with nc.Block() as block:
        @block.scalar
        def _(act):
            for c in range(KD):
                nc.scalar.activation(sq[:, c, 0:width], k.xT[:, c, 0:width], ACT.Square).then_inc(sq_ready.sem, 1)
            act.wait_ge(v_ready.sem, v_ready.at(len(pieces)))
            k.act(act, nc.scalar.activation(y[:, 0:width], v[:, 0:width], ACT.Ln))
            nc.scalar.activation(y[:, 0:width], y[:, 0:width], ACT.Exp, scale=-0.5).then_inc(y_ready.sem, 1)
            for c in range(KD):
                act.wait_ge(h_ready.sem, h_ready.at(c + 1))
                nc.scalar.activation(k.h_high[:, c, 0:width], h[:, c, 0:width], ACT.Copy).then_inc(high_ready.sem, 1)

        @block.gpsimd
        def _(pool):
            for c in range(KD):
                pool.wait_ge(high_ready.sem, high_ready.at(c + 1))
                nc.gpsimd.tensor_tensor(k.h_low[:, c, 0:width], h[:, c, 0:width], k.h_high[:, c, 0:width].bitcast(F32), ALU.subtract)

        @block.tensor
        def _(pe):
            for c in range(KD):
                pe.wait_ge(sq_ready.sem, sq_ready.at(c + 1))
                for i, (t0, n) in enumerate(pieces):
                    mm = nc.tensor.matmul(k.psum[:, i, 0:n], k.const("ones"), sq[:, c, t0:t0 + n],
                                          start=(c == 0), stop=(c == KD - 1))
            mm.then_inc(sum_ready.sem, 1)

        @block.vector
        def _(dve):
            dve.wait_ge(sum_ready.sem, sum_ready.at(1))
            for i, (t0, n) in enumerate(pieces):
                nc.vector.tensor_scalar(v[:, t0:t0 + n], k.psum[:, i, 0:n], 1.0 / D, EPS, ALU.mult, ALU.add
                                        ).then_inc(v_ready.sem, 1)
            dve.wait_ge(y_ready.sem, y_ready.at(1))
            newton(k, dve, y[:, 0:width], v[:, 0:width], u[:, 0:width])
            for c in range(KD):
                for i, (t0, n) in enumerate(pieces):
                    o = h[:, c, t0:t0 + n]
                    ins = nc.vector.scalar_tensor_tensor(o, k.xT[:, c, t0:t0 + n], gain(i, c), y[:, t0:t0 + n], ALU.mult, ALU.mult)
                    if shift is not None:
                        k.dve(dve, ins)
                        ins = nc.vector.tensor_scalar(o, o, shift(i, c), None, ALU.add)
                    if i < len(pieces) - 1:
                        k.dve(dve, ins)
                ins.then_inc(h_ready.sem, 1)
    for s, n in ((sq_ready, KD), (sum_ready, 1), (v_ready, len(pieces)), (y_ready, 1), (h_ready, KD), (high_ready, KD)):
        s.base += n


def stage_rows(k, w, n_blocks, width, tiles, out, at, extra=None):
    nc = k.nc
    k.names += 1
    blocks = [(w[b], width, lambda i, b=b: out(b, i)) for b in range(n_blocks)] + ([extra] if extra else [])
    raw = [k.place(f"rows_w{k.names}_{r}", at + r * BANK, BANK) for r in range(RING)]
    high, low = ([k.place(f"rows_{s}{k.names}_{r}", at + (RING * i + r) * BANK, BANK, dtype=FR) for r in range(RING)]
                 for i, s in ((1, "high"), (2, "low")))
    taken = k.shared("rows_taken")
    steps = [(b, c) for b in range(len(blocks)) for c in range(KD)]
    with nc.Block() as block:
        @block.sync
        def _(sp):
            for s, (b, c) in enumerate(steps):
                source, n, _ = blocks[b]
                if s >= RING:
                    sp.wait_ge(k.w_low.sem, k.w_low.at(s - RING + 1))
                sp.dma_start(raw[s % RING][:, 0:n], source[:, c * n:(c + 1) * n]).then_inc(k.weights_in[s % RING].sem, 16)

        @block.scalar
        def _(act):
            def round_rows(s):
                n = blocks[steps[s][0]][1]
                act.wait_ge(k.weights_in[s % RING].sem, k.weights_in[s % RING].at(16 * (s // RING + 1)))
                if s >= RING:
                    act.wait_ge(k.product_done.sem, k.product_done.at((s - RING + 1) * tiles))
                nc.scalar.activation(high[s % RING][:, 0:n], raw[s % RING][:, 0:n], ACT.Copy).then_inc(k.w_high.sem, 1)

            for s in range(RING - 1):
                round_rows(s)
            for s, (b, c) in enumerate(steps):
                if s + RING - 1 < len(steps):
                    round_rows(s + RING - 1)
                if c == KD - 1:
                    for i in range(tiles):
                        act.wait_ge(k.product_done.sem, k.product_done.at(s * tiles + i + 1))
                        nc.scalar.activation(blocks[b][2](i), k.psum[:, (b * tiles + i) % 8, 0:blocks[b][1]], ACT.Copy).then_inc(taken.sem, 1)

        @block.vector
        def _(dve):
            for s, (b, c) in enumerate(steps):
                n = blocks[b][1]
                dve.wait_ge(k.w_high.sem, k.w_high.at(s + 1))
                nc.vector.tensor_tensor(low[s % RING][:, 0:n], raw[s % RING][:, 0:n], high[s % RING][:, 0:n].bitcast(F32), ALU.subtract
                                        ).then_inc(k.w_low.sem, 1)

        @block.tensor
        def _(pe):
            for s, (b, c) in enumerate(steps):
                n = blocks[b][1]
                pe.wait_ge(k.w_low.sem, k.w_low.at(s + 1))
                for i in range(tiles):
                    job = b * tiles + i
                    if c == 0 and job >= 8:
                        pe.wait_ge(taken.sem, taken.at(job - 7))
                    t = slice(i * P, (i + 1) * P)
                    split_product(nc, k.psum[:, job % 8, 0:n], k.h_high[:, c, t], k.h_low[:, c, t], high[s % RING][:, 0:n], low[s % RING][:, 0:n],
                                  c == 0, c == KD - 1).then_inc(k.product_done.sem, 1)
    for r in range(RING):
        k.weights_in[r].base += 16 * len(range(r, len(steps), RING))
    k.product_done.base += len(steps) * tiles
    k.w_high.base += len(steps)
    k.w_low.base += len(steps)
    taken.base += len(blocks) * tiles


class First:

    def __init__(self, k):
        self.pT = k.place("projT", BIG, 16, SEQ)
        self.vm = k.place("vm", 24576, CHUNKS, BANK)
        self.va = k.place("va", 26624, CHUNKS, BANK)
        self.gates = k.place("gates", 28672, CHUNKS, 2 * M_HEADS)
        self.cT = k.place("convT", 28800, M_HEADS, SEQ)
        self.w_qk = k.place("w_qk", 30848, 2, M_HEADS, P)
        self.qT = k.place("m_qT", 31872, M_HEADS, SEQ)
        self.kT = k.place("m_kT", 33920, M_HEADS, SEQ)
        self.k_rows = k.place("m_k_rows", 35968, CHUNKS, M_HEADS, P)
        self.mixT = k.place("mixT", 10240, KD, SEQ)


M_SCALE = P ** -0.5


def stage_conv(k, t, f):
    nc = k.nc
    w_in, conv_done, c_ready, qk_summed, qk_taken, rows_summed = (
        k.sem(s) for s in ("w_qk_in", "conv_done", "c_ready", "qk_summed", "qk_taken", "k_rows_summed"))
    with nc.Block() as block:
        @block.sync
        def _(sp):
            sp.dma_start(f.w_qk[:, :, :, :], t["w_qk"]).then_inc(w_in, 16)

        @block.vector
        def _(dve):
            for h in range(M_HEADS):
                u, c = f.pT[:, h, :], f.cT[:, h, :]
                tap = lambda j: k.par("conv_w", h * 4 + j)
                k.dve(dve, nc.vector.tensor_scalar(c, u, tap(3), k.par("conv_b", h), ALU.mult, ALU.add))
                for back in (1, 2, 3):
                    ins = nc.vector.scalar_tensor_tensor(c[:, back:SEQ], u[:, 0:SEQ - back], tap(3 - back),
                                                         c[:, back:SEQ], ALU.mult, ALU.add)
                    if back < 3:
                        k.dve(dve, ins)
                    else:
                        ins.then_inc(conv_done, 1)
            for i in range(2 * M_HEADS):
                dve.wait_ge(qk_summed, i + 1)
                o, scale = (f.qT[:, i, :], 1.0) if i < M_HEADS else (f.kT[:, i - M_HEADS, :], M_SCALE)
                nc.vector.tensor_scalar(o, k.psum[:, i, :], scale, None, ALU.mult).then_inc(qk_taken, 1)
            for n in range(CHUNKS):
                dve.wait_ge(rows_summed, n + 1)
                nc.vector.tensor_scalar(f.k_rows[:, n, :, :].rearrange("p h d -> p (h d)"), k.psum[:, n, :], M_SCALE, None, ALU.mult)

        @block.scalar
        def _(act):
            for h in range(M_HEADS):
                act.wait_ge(conv_done, h + 1)
                nc.scalar.activation(f.cT[:, h, :], f.cT[:, h, :], ACT.Silu).then_inc(c_ready, 1)
            nc.scalar.activation(f.pT[:, 4:8, :], f.pT[:, 4:8, :], ACT.Sigmoid)

        @block.tensor
        def _(pe):
            pe.wait_ge(w_in, 16)
            for i in range(2 * M_HEADS):
                h = i % M_HEADS
                if i < M_HEADS:
                    pe.wait_ge(c_ready, h + 1)
                nc.tensor.matmul(k.psum[:, i, :], f.w_qk[:, i // M_HEADS, h, :], f.cT[:, h, :], start=True, stop=True).then_inc(qk_summed, 1)
            for n in range(CHUNKS):
                pe.wait_ge(qk_taken, n + 1)
                for h in range(M_HEADS):
                    mm = nc.tensor.matmul(k.psum[:, n, h * P:(h + 1) * P], f.cT[:, h, n * P:(n + 1) * P], f.w_qk[:, 1, h, :],
                                          start=True, stop=True)
                mm.then_inc(rows_summed, 1)


def stage_mlstm(k, t, f):
    nc = k.nc
    V = k.dve
    small = 51904
    v_aug = k.place("v_aug", 38016, UNITS, P + 1)
    dm = k.place("d_mat", 40080, UNITS, P)
    sdT = k.place("sdT", 42128, UNITS, P)
    state = k.place("state", 44176, CHUNKS - 1, M_HEADS, P + 1)
    pick = k.place("pick", 45728, UNITS, P, rows=UNITS)
    num = k.place("num", 47776, UNITS, P + 1)
    tmp = k.place("m_tmp", 49840, UNITS, P + 1)
    col = lambda i, n=UNITS: k.place(f"m_col{i}", small + i * UNITS, n)
    lf, li, b, g, inter, mt, iw, den, wts, bl = (col(i) for i in range(10))
    bcast = k.place("m_bcast", small + 10 * UNITS, 4, UNITS)
    line = k.place("m_line", small + 14 * UNITS, 6, UNITS, rows=1)
    rT = k.place("m_rT", small + 20 * UNITS, P, rows=UNITS)
    bT = k.place("m_bT", small + 20 * UNITS + P, P, rows=UNITS)
    mlT = k.place("m_mlT", small + 20 * UNITS + 2 * P, 1, rows=UNITS)
    gb = k.place("m_gb", small + 20 * UNITS + 2 * P + 32, CHUNKS, 2 * M_HEADS)
    (pick_in, gates_ready, soft_ready, lf_ready, cum_summed, r_ready, ml_ready, ml_turned, scan_ready, scan_exp, pack_ready,
     packed, g_ready, wts_ready, kw_ready, carried, rows_spread, d_ready, d_exp, scored, taken, sd_ready, turned, sdT_ready,
     state_ready, num_summed, num_taken, rms_ready, rms_done, h_ready, h_turned, h_taken) = (k.sem("m_" + s) for s in (
         "pick_in", "gates_ready", "soft_ready", "lf_ready", "cum_summed", "r_ready", "ml_ready", "ml_turned", "scan_ready",
         "scan_exp", "pack_ready", "packed", "g_ready", "wts_ready", "kw_ready", "carried", "rows_spread", "d_ready", "d_exp",
         "scored", "taken", "sd_ready", "turned", "sdT_ready", "state_ready", "num_summed", "num_taken", "rms_ready",
         "rms_done", "h_ready", "h_turned", "h_taken"))
    ps = k.psum
    flat4 = lambda bank: ps[:, bank:bank + 4, :].rearrange("p b (h l) -> p (b h) l", l=P)
    over = lambda c: c.unsqueeze(2).to_broadcast([P, UNITS, P])
    W1 = P + 1

    with nc.Block() as block:
        @block.sync
        def _(sp):
            sp.dma_start(pick[:, :, :], t["pick"]).then_inc(pick_in, 16)

        @block.vector
        def _(dve):
            bias = k.par("gate_b", 0, 2 * M_HEADS).unsqueeze(1).to_broadcast([P, CHUNKS, 2 * M_HEADS])
            V(dve, nc.vector.tensor_tensor(gb[:, :, :], f.gates[:, :, :], bias, ALU.add))
            by_unit = lambda c: c[:, :].rearrange("p (n h) -> p n h", h=M_HEADS)
            V(dve, nc.vector.tensor_copy(by_unit(li), gb[:, :, 0:M_HEADS]))
            V(dve, nc.vector.tensor_copy(by_unit(lf), gb[:, :, M_HEADS:2 * M_HEADS]))
            nc.vector.scalar_tensor_tensor(g[:, :], lf[:, :], -1.0, lf[:, :], ALU.mult, ALU.min).then_inc(gates_ready, 1)
            V(dve, nc.vector.tensor_scalar(lf[:, :], lf[:, :], 0.0, None, ALU.min))
            dve.wait_ge(soft_ready, 1)
            nc.vector.tensor_tensor(lf[:, :], lf[:, :], g[:, :], ALU.subtract).then_inc(lf_ready, 1)
            V(dve, nc.vector.memset(v_aug[:, :, P:W1], 1.0))
            V(dve, nc.vector.tensor_copy(v_aug[:, :, 0:P], f.vm[:, :, :].rearrange("p n (h d) -> p (n h) d", d=P)))
            dve.wait_ge(cum_summed, 1)
            V(dve, nc.vector.tensor_copy(b[:, :], ps[:, 0, 0:UNITS]))
            V(dve, nc.vector.tensor_copy(bl[:, :], ps[:, 0, UNITS:2 * UNITS]))
            V(dve, nc.vector.tensor_copy(line[0:1, 0, :], ps[0:1, 3, 0:UNITS]))
            V(dve, nc.vector.tensor_copy(bT[:, :], ps[0:UNITS, 1, 0:P]))
            nc.vector.tensor_tensor(rT[:, :], ps[0:UNITS, 2, 0:P], bT[:, :], ALU.subtract).then_inc(r_ready, 1)
            dve.wait_ge(r_ready, 1)
            V(dve, nc.vector.tensor_reduce(mlT[:, :], rT[:, :], AX_X, ALU.max))
            nc.vector.tensor_tensor(mlT[:, :], mlT[:, :], bT[:, P - 1:P], ALU.add).then_inc(ml_ready, 1)
            dve.wait_ge(ml_turned, 1)
            V(dve, nc.vector.tensor_copy(line[0:1, 4, :], ps[0:1, 3, UNITS:2 * UNITS]))
            V(dve, nc.vector.memset(line[0:1, 1, 0:M_HEADS], 0.0))
            for n in range(CHUNKS):
                s = slice(n * M_HEADS, (n + 1) * M_HEADS)
                V(dve, nc.vector.tensor_tensor(line[0:1, 2, s], line[0:1, 0, s], line[0:1, 1, s], ALU.add))
                m_new = line[0:1, 1, (n + 1) * M_HEADS:(n + 2) * M_HEADS] if n < CHUNKS - 1 else line[0:1, 5, 0:M_HEADS]
                V(dve, nc.vector.tensor_tensor(m_new, line[0:1, 2, s], line[0:1, 4, s], ALU.max))
                V(dve, nc.vector.tensor_tensor(line[0:1, 2, s], line[0:1, 2, s], m_new, ALU.subtract))
                last = nc.vector.tensor_tensor(line[0:1, 3, s], line[0:1, 4, s], m_new, ALU.subtract)
                if n < CHUNKS - 1:
                    V(dve, last)
            last.then_inc(scan_ready, 1)
            dve.wait_ge(packed, 1)
            V(dve, nc.vector.tensor_copy(bcast[:, :, :].rearrange("p a u -> p (a u)"), ps[:, 3, 64:64 + 4 * UNITS]))
            V(dve, nc.vector.tensor_tensor(g[:, :], bl[:, :], b[:, :], ALU.subtract))
            V(dve, nc.vector.tensor_tensor(g[:, :], g[:, :], li[:, :], ALU.add))
            nc.vector.tensor_tensor(g[:, :], g[:, :], bcast[:, 3, :], ALU.subtract).then_inc(g_ready, 1)
            V(dve, nc.vector.tensor_tensor(inter[:, :], b[:, :], bcast[:, 0, :], ALU.add))
            dve.wait_ge(wts_ready, 1)
            kr = f.k_rows[:, :, :, :].rearrange("p n h d -> p (n h) d")
            nc.vector.tensor_tensor(kr, kr, over(wts[:, :]), ALU.mult).then_inc(kw_ready, 1)
            dve.wait_ge(rows_spread, 1)
            V(dve, nc.vector.tensor_tensor(dm[:, :, :], flat4(4), over(b[:, :]), ALU.add))
            V(dve, nc.vector.tensor_tensor(dm[:, :, :], dm[:, :, :],
                                           k.const("causal").unsqueeze(1).to_broadcast([P, UNITS, P]), ALU.add))
            V(dve, nc.vector.tensor_reduce(mt[:, :], dm[:, :, :], AX_X, ALU.max))
            V(dve, nc.vector.tensor_tensor(mt[:, :], mt[:, :], inter[:, :], ALU.max))
            V(dve, nc.vector.tensor_tensor(iw[:, :], inter[:, :], mt[:, :], ALU.subtract))
            nc.vector.tensor_tensor(dm[:, :, :], dm[:, :, :], over(mt[:, :]), ALU.subtract).then_inc(d_ready, 1)
            dve.wait_ge(carried, 1)
            for n in range(CHUNKS - 1):
                for h in range(M_HEADS):
                    u = n * M_HEADS + h
                    cc = ps[:, u // 3, (u % 3) * W1:(u % 3 + 1) * W1]
                    own = nc.vector.tensor_scalar(state[:, n, h, :], cc, bcast[:, 2, u:u + 1], None, ALU.mult)
                    if n == 0:
                        own.then_inc(state_ready, 1)
                        continue
                    V(dve, own)
                    if h == 0:
                        dve.wait_ge(state_ready, n * M_HEADS)
                    nc.vector.scalar_tensor_tensor(state[:, n, h, :], state[:, n - 1, h, :], bcast[:, 1, u:u + 1],
                                                   state[:, n, h, :], ALU.mult, ALU.add).then_inc(state_ready, 1)
            dve.wait_ge(d_exp, 1)
            dve.wait_ge(scored, 1)
            nc.vector.tensor_tensor(dm[:, :, :], flat4(4), dm[:, :, :], ALU.mult).then_inc(sd_ready, 1)
            dve.wait_ge(turned, 1)
            nc.vector.tensor_copy(sdT[:, :, :], flat4(0)).then_inc(sdT_ready, 1)
            for n in range(CHUNKS):
                dve.wait_ge(num_summed, n + 1)
                for h in range(M_HEADS):
                    u = n * M_HEADS + h
                    own = ps[:, 4 + h // 2, (h % 2) * W1:(h % 2 + 1) * W1]
                    ins = nc.vector.tensor_copy(num[:, u, :], own)
                    if n:
                        V(dve, ins)
                        past = ps[:, 6 + h // 2, (h % 2) * W1:(h % 2 + 1) * W1]
                        ins = nc.vector.scalar_tensor_tensor(num[:, u, :], past, iw[:, u:u + 1], num[:, u, :], ALU.mult, ALU.add)
                    if h < M_HEADS - 1:
                        V(dve, ins)
                ins.then_inc(num_taken, 1)
            dve.wait_ge(num_taken, CHUNKS)
            row_sum = num[:, :, P:W1].rearrange("p u o -> p (u o)")
            V(dve, nc.vector.scalar_tensor_tensor(den[:, :], row_sum, -1.0, row_sum, ALU.mult, ALU.max))
            V(dve, nc.vector.tensor_tensor(den[:, :], den[:, :], mt[:, :], ALU.max))
            V(dve, nc.vector.reciprocal(den[:, :], den[:, :]))
            hn = num[:, :, 0:P]
            V(dve, nc.vector.tensor_tensor(hn, hn, over(den[:, :]), ALU.mult))
            V(dve, nc.vector.tensor_tensor(tmp[:, :, 0:P], hn, hn, ALU.mult))
            V(dve, nc.vector.tensor_reduce(wts[:, :], tmp[:, :, 0:P], AX_X, ALU.add))
            nc.vector.tensor_scalar(wts[:, :], wts[:, :], 1.0 / P, EPS, ALU.mult, ALU.add).then_inc(rms_ready, 1)
            dve.wait_ge(rms_done, 1)
            newton(k, dve, g[:, :], wts[:, :], den[:, :])
            nc.vector.tensor_tensor(hn, hn, over(g[:, :]), ALU.mult).then_inc(h_ready, 1)
            for h in range(M_HEADS):
                dve.wait_ge(h_turned, h + 1)
                c = f.cT[:, h, :]
                V(dve, nc.vector.tensor_scalar(c, c, k.par("skip", h), None, ALU.mult))
                V(dve, nc.vector.scalar_tensor_tensor(c, ps[:, h, :], k.par("mh_g", h), c, ALU.mult, ALU.add))
                V(dve, nc.vector.tensor_tensor(f.mixT[:, h, :], c, f.pT[:, M_HEADS + h, :], ALU.mult))

        @block.scalar
        def _(act):
            act.wait_ge(gates_ready, 1)
            k.act(act, nc.scalar.activation(g[:, :], g[:, :], ACT.Exp))
            nc.scalar.activation(g[:, :], g[:, :], ACT.Ln, bias=1.0).then_inc(soft_ready, 1)
            act.wait_ge(scan_ready, 1)
            nc.scalar.activation(line[0:1, 2:4, :], line[0:1, 2:4, :], ACT.Exp).then_inc(scan_exp, 1)
            act.wait_ge(g_ready, 1)
            nc.scalar.activation(wts[:, :], g[:, :], ACT.Exp).then_inc(wts_ready, 1)
            act.wait_ge(d_ready, 1)
            k.act(act, nc.scalar.activation(iw[:, :], iw[:, :], ACT.Exp))
            k.act(act, nc.scalar.activation(mt[:, :], mt[:, :], ACT.Exp, scale=-1.0))
            nc.scalar.activation(dm[:, :, :], dm[:, :, :], ACT.Exp).then_inc(d_exp, 1)
            act.wait_ge(rms_ready, 1)
            k.act(act, nc.scalar.activation(g[:, :], wts[:, :], ACT.Ln))
            nc.scalar.activation(g[:, :], g[:, :], ACT.Exp, scale=-0.5).then_inc(rms_done, 1)

        @block.tensor
        def _(pe):
            pe.wait_ge(lf_ready, 1)
            nc.tensor.matmul(ps[:, 0, 0:UNITS], k.const("tri"), lf[:, :], start=True, stop=True)
            nc.tensor.matmul(ps[:, 0, UNITS:2 * UNITS], k.const("ones"), lf[:, :], start=True, stop=True)
            nc.tensor.matmul(ps[0:UNITS, 1, 0:P], lf[:, :], k.const("tri"), start=True, stop=True)
            nc.tensor.matmul(ps[0:1, 3, 0:UNITS], k.const("ones")[:, 0:1], lf[:, :], start=True, stop=True)
            nc.tensor.matmul(ps[0:UNITS, 2, 0:P], li[:, :], k.const("ident"), start=True, stop=True).then_inc(cum_summed, 1)
            pe.wait_ge(ml_ready, 1)
            nc.tensor.matmul(ps[0:1, 3, UNITS:2 * UNITS], mlT[:, :], k.const("ident", UNITS)[:, 0:UNITS], start=True, stop=True).then_inc(ml_turned, 1)
            pe.wait_ge(pick_in, 16)
            for u in range(UNITS):
                mm = nc.tensor.matmul(flat4(4)[:, u, :], pick[:, u, :], rT[:, :], start=True, stop=True)
            mm.then_inc(rows_spread, 1)
            pe.wait_ge(scan_exp, 1)
            nc.tensor.matmul(ps[:, 3, 64:64 + 4 * UNITS], k.const("ones", 1), line[0:1, 1:5, :], start=True, stop=True).then_inc(packed, 1)
            pe.wait_ge(kw_ready, 1)
            for u in range(UNITS - M_HEADS):
                mm = nc.tensor.matmul(ps[:, u // 3, (u % 3) * W1:(u % 3 + 1) * W1], f.k_rows[:, u // M_HEADS, u % M_HEADS, :],
                                      v_aug[:, u, :], start=True, stop=True)
            mm.then_inc(carried, 1)
            pe.wait_ge(d_ready, 1)
            for n in range(CHUNKS):
                s = slice(n * P, (n + 1) * P)
                for h in range(M_HEADS):
                    mm = nc.tensor.matmul(flat4(4)[:, n * M_HEADS + h, :], f.qT[:, h, s], f.kT[:, h, s], start=True, stop=True)
            mm.then_inc(scored, 1)
            pe.wait_ge(sd_ready, 1)
            pe.wait_ge(state_ready, (CHUNKS - 1) * M_HEADS)
            for u in range(UNITS):
                mm = nc.tensor.transpose(flat4(0)[:, u, :], dm[:, u, :], k.const("ident"))
            mm.then_inc(turned, 1)
            pe.wait_ge(sdT_ready, 1)
            for n in range(CHUNKS):
                if n:
                    pe.wait_ge(num_taken, n)
                for h in range(M_HEADS):
                    o = slice((h % 2) * W1, (h % 2 + 1) * W1)
                    mm = nc.tensor.matmul(ps[:, 4 + h // 2, o], sdT[:, n * M_HEADS + h, :], v_aug[:, n * M_HEADS + h, :], start=True, stop=True)
                    if n:
                        mm = nc.tensor.matmul(ps[:, 6 + h // 2, o], f.qT[:, h, n * P:(n + 1) * P], state[:, n - 1, h, :], start=True, stop=True)
                mm.then_inc(num_summed, 1)
            pe.wait_ge(h_ready, 1)
            for h in range(M_HEADS):
                for n in range(CHUNKS):
                    mm = nc.tensor.transpose(ps[:, h, n * P:(n + 1) * P], num[:, n * M_HEADS + h, 0:P], k.const("ident"))
                mm.then_inc(h_turned, 1)


def stage_head_norm(k, name, jobs, at):
    nc = k.nc
    sq = k.place(f"{name}_sq", at, 4, TOK)
    v = k.place(f"{name}_v", at + 4 * TOK, 4, TOK)
    y = k.place(f"{name}_y", at + 8 * TOK, 4, TOK)
    squared, summed, v_ready, y_ready, scaled = signals = [k.shared(f"head_norm_{s}") for s in ("squared", "summed", "v_ready", "y_ready", "scaled")]
    with k.nc.Block() as block:
        @block.scalar
        def _(act):
            for j, (x, c0, pieces, _) in enumerate(jobs):
                w = sum(n for _, n in pieces)
                if j:
                    act.wait_ge(scaled.sem, scaled.at(j))
                nc.scalar.activation(sq[:, :, 0:w], x[:, c0:c0 + 4, 0:w], ACT.Square).then_inc(squared.sem, 1)
                act.wait_ge(v_ready.sem, v_ready.at(j + 1))
                k.act(act, nc.scalar.activation(y[:, :, 0:w], v[:, :, 0:w], ACT.Ln))
                nc.scalar.activation(y[:, :, 0:w], y[:, :, 0:w], ACT.Exp, scale=-0.5).then_inc(y_ready.sem, 1)

        @block.tensor
        def _(pe):
            for j, (_, _, pieces, _) in enumerate(jobs):
                pe.wait_ge(squared.sem, squared.at(j + 1))
                if j:
                    pe.wait_ge(v_ready.sem, v_ready.at(j))
                for i, (t0, n) in enumerate(pieces):
                    for c in range(4):
                        mm = nc.tensor.matmul(k.psum[:, 4 * i + c, 0:n], k.const("blocks"), sq[:, c, t0:t0 + n], start=True, stop=True)
                mm.then_inc(summed.sem, 1)

        @block.vector
        def _(dve):
            for j, (x, c0, pieces, gain) in enumerate(jobs):
                w = sum(n for _, n in pieces)
                dve.wait_ge(summed.sem, summed.at(j + 1))
                for i, (t0, n) in enumerate(pieces):
                    ins = nc.vector.tensor_scalar(v[:, :, t0:t0 + n], k.psum[:, 4 * i:4 * i + 4, 0:n], 1.0 / HEAD, EPS, ALU.mult, ALU.add)
                    if i < len(pieces) - 1:
                        k.dve(dve, ins)
                ins.then_inc(v_ready.sem, 1)
                dve.wait_ge(y_ready.sem, y_ready.at(j + 1))
                newton(k, dve, y[:, :, 0:w], v[:, :, 0:w], sq[:, :, 0:w])
                for c in range(4):
                    o = x[:, c0 + c, 0:w]
                    ins = nc.vector.scalar_tensor_tensor(o, o, gain(c0 + c), y[:, c, 0:w], ALU.mult, ALU.mult)
                    if c < 3:
                        k.dve(dve, ins)
                ins.then_inc(scaled.sem, 1)
    for s in signals:
        s.base += len(jobs)


def stage_dilated_table(k, t, tab, at):
    nc = k.nc
    z_len = SEQ + P
    rel = k.place("rel_bias", at, DIL_HEADS, rows=N_BUCKETS + 1)
    spread = k.place("rel_spread", at + 16, DIL_HEADS, P, rows=N_BUCKETS + 1)
    hot = k.place("bucket_hot", at + 16 + DIL_HEADS * P, z_len, rows=N_BUCKETS + 1)
    line = k.place("bias_line", at + 16 + DIL_HEADS * P + z_len, DIL_HEADS, z_len)
    tables_in, spread_ready, line_summed, line_ready, skew_out, skew_in = (k.sem("dil_" + s) for s in (
        "tables_in", "spread_ready", "line_summed", "line_ready", "skew_out", "skew_in"))
    skew = nc.dram_tensor("skew", (DIL_HEADS, P, z_len), F32)
    with nc.Block() as block:
        @block.sync
        def _(sp):
            sp.dma_start(rel[0:N_BUCKETS, :], t["rel_bias"]).then_inc(tables_in, 16)
            sp.dma_start(hot[:, :], t["bucket_hot"]).then_inc(tables_in, 16)
            for h in range(DIL_HEADS):
                sp.wait_ge(line_ready, 2 * h + 2)
                sp.dma_start(skew.ap()[h], line[:, h, :]).then_inc(skew_out, 16)
            sp.wait_ge(skew_out, 16 * DIL_HEADS)
            for h in range(DIL_HEADS):
                back = bass.AP(skew, h * P * z_len + P - 1, [[z_len - 1, P], [1, SEQ]])
                sp.dma_start(tab[:, h, :], back).then_inc(skew_in, 16)
            sp.wait_ge(skew_in, 16 * DIL_HEADS)

        @block.vector
        def _(dve):
            dve.wait_ge(tables_in, 32)
            k.dve(dve, nc.vector.memset(spread[N_BUCKETS:N_BUCKETS + 1, :, :], 1.0))
            nc.vector.tensor_copy(spread[0:N_BUCKETS, :, :], rel[0:N_BUCKETS, :].unsqueeze(2).to_broadcast([N_BUCKETS, DIL_HEADS, P])
                                  ).then_inc(spread_ready, 1)
            for h in range(DIL_HEADS):
                for i, (z0, n) in enumerate(((0, SEQ), (SEQ, P))):
                    dve.wait_ge(line_summed, 2 * h + i + 1)
                    nc.vector.tensor_copy(line[:, h, z0:z0 + n], k.psum[:, (2 * h + i) % 8, 0:n]).then_inc(line_ready, 1)

        @block.tensor
        def _(pe):
            pe.wait_ge(spread_ready, 1)
            for h in range(DIL_HEADS):
                for i, (z0, n) in enumerate(((0, SEQ), (SEQ, P))):
                    if 2 * h + i >= 8:
                        pe.wait_ge(line_ready, 2 * h + i - 7)
                    nc.tensor.matmul(k.psum[:, (2 * h + i) % 8, 0:n], spread[:, h, :], hot[:, z0:z0 + n], start=True, stop=True
                                     ).then_inc(line_summed, 1)


def stage_attention(k, name, groups, units, stages, out, at, stat_at, sink=None):
    nc = k.nc
    V = k.dve
    units = [units(s) for s in range(2)]
    n_group = len(units[0])
    n_units = 2 * n_group
    units = units[0] + units[1]
    sc = k.place(f"{name}_scores", at, 3, TOK)
    pT = k.place(f"{name}_probsT", at + 3 * TOK, 2, TOK)
    stat = k.place(f"{name}_stat", stat_at, 9)
    staged, scored, reduced, exped, normed, turned, copied, summed, stored = (k.shared(f"attention_{s}") for s in (
        "staged", "scored", "reduced", "exped", "normed", "turned", "copied", "summed", "stored"))
    passes = groups // 2
    n_stages = len(stages(0, 0))
    n_out = len(out(0))
    scale = HEAD ** -0.5
    keys = lambda u: sum(n for _, n in units[u][1])
    nm = lambda b: stat[:, b:b + 1]
    den = lambda b: stat[:, 3 + b:4 + b]
    es = lambda b: stat[:, 6 + b:7 + b]

    with nc.Block() as block:
        @block.gpsimd
        def _(pool):
            with pool.Fori(0, passes) as it:
                for s in range(2):
                    pool.wait_ge(summed.sem, summed.at(it * n_units + (s + 1) * n_group))
                    for to, source in stages(it * 2 + s, s):
                        nc.gpsimd.tensor_copy(to, source).then_inc(staged.sem, 1)

        @block.tensor
        def _(pe):
            pe.sem_inc(turned.sem, 3)
            pe.sem_inc(summed.sem, n_units)
            with pe.Fori(0, passes) as it:
                def score(u):
                    if u % n_group == 0:
                        pe.wait_ge(staged.sem, staged.at(it * (2 * n_stages) + (u // n_group + 1) * n_stages))
                    pe.wait_ge(reduced.sem, reduced.at(it * n_units + (u + 1)))
                    for i, (kk, n) in enumerate(units[u][1]):
                        mm = nc.tensor.matmul(k.psum[:, (u % 2) * 2 + i, 0:n], units[u][0], kk, start=True, stop=True)
                    mm.then_inc(scored.sem, 1)

                def multiply(u):
                    _, _, _, values, o = units[u]
                    pe.wait_ge(copied.sem, copied.at(it * n_units + (u + 2)))
                    if u % n_group == 0:
                        pe.wait_ge(stored.sem, stored.at(it * (2 * n_out) + (u // n_group + 1) * n_out))
                    tiles = keys(u) // P
                    for j in range(tiles):
                        mm = nc.tensor.matmul(o, values(j), pT[:, u % 2, j * P:(j + 1) * P], start=(j == 0), stop=(j == tiles - 1))
                    mm.then_inc(summed.sem, 1)

                for u in range(3):
                    score(u)
                for u in range(n_units):
                    pe.wait_ge(normed.sem, normed.at(it * n_units + (u + 1)))
                    pe.wait_ge(copied.sem, copied.at(it * n_units + (u + 1)))
                    for j in range(keys(u) // P):
                        mm = nc.tensor.transpose(k.psum[:, 4 + j // 4, (j % 4) * P:(j % 4 + 1) * P], sc[:, u % 3, j * P:(j + 1) * P], k.const("ident"))
                    mm.then_inc(turned.sem, 1)
                    if u + 3 < n_units:
                        score(u + 3)
                    if u:
                        multiply(u - 1)
                multiply(n_units - 1)

        @block.vector
        def _(dve):
            dve.sem_inc(reduced.sem, 2)
            with dve.Fori(0, passes) as it:
                V.restart(dve)

                def gather(u):
                    b = u % 3
                    dve.wait_ge(scored.sem, scored.at(it * n_units + (u + 1)))
                    dve.wait_ge(turned.sem, turned.at(it * n_units + (u + 1)))
                    at_key = 0
                    for i, (_, n) in enumerate(units[u][1]):
                        o, s = sc[:, b, at_key:at_key + n], k.psum[:, u % 2 * 2 + i, 0:n]
                        if i == 0 and units[u][2] is not None:
                            ins = nc.vector.scalar_tensor_tensor(o, s, scale, units[u][2](it * 2 + u // n_group), ALU.mult, ALU.add)
                        else:
                            ins = nc.vector.tensor_scalar(o, s, scale, None, ALU.mult)
                        at_key += n
                    V(dve, ins)
                    if sink is None:
                        nc.vector.tensor_reduce(nm(b), sc[:, b, 0:at_key], AX_X, ALU.max, negate=True).then_inc(reduced.sem, 1)
                    else:
                        V(dve, nc.vector.tensor_reduce(nm(b), sc[:, b, 0:at_key], AX_X, ALU.max))
                        nc.vector.tensor_scalar(nm(b), nm(b), sink(u), -1.0, ALU.max, ALU.mult).then_inc(reduced.sem, 1)

                def norm(u):
                    b = u % 3
                    dve.wait_ge(exped.sem, exped.at(it * n_units + (u + 1)))
                    if sink is not None:
                        V(dve, nc.vector.tensor_tensor(den(b), den(b), es(b), ALU.add))
                    V(dve, nc.vector.reciprocal(den(b), den(b)))
                    p = sc[:, b, 0:keys(u)]
                    nc.vector.tensor_scalar(p, p, den(b), None, ALU.mult).then_inc(normed.sem, 1)

                gather(0)
                gather(1)
                for u in range(n_units):
                    norm(u)
                    if u + 2 < n_units:
                        gather(u + 2)

        @block.scalar
        def _(act):
            act.sem_inc(copied.sem, 1)
            act.sem_inc(stored.sem, n_out)
            with act.Fori(0, passes) as it:
                def exp(u):
                    b = u % 3
                    act.wait_ge(reduced.sem, reduced.at(it * n_units + (u + 3)))
                    p = sc[:, b, 0:keys(u)]
                    if sink is not None:
                        nc.scalar.activation(es(b), sink(u), ACT.Exp, bias=nm(b))
                    nc.scalar.activation(p, p, ACT.Exp, bias=nm(b), accum_out=den(b)).then_inc(exped.sem, 1)

                def store(s):
                    act.wait_ge(summed.sem, summed.at(it * n_units + (n_units + (s + 1) * n_group)))
                    for to, source in out(it * 2 + s):
                        nc.scalar.activation(to, source, ACT.Copy).then_inc(stored.sem, 1)

                exp(0)
                exp(1)
                for u in range(n_units):
                    act.wait_ge(turned.sem, turned.at(it * n_units + (u + 4)))
                    act.wait_ge(summed.sem, summed.at(it * n_units + (n_units + u - 1)))
                    n = keys(u)
                    nc.scalar.activation(pT[:, u % 2, 0:n], k.psum[:, 4:6, :].rearrange("p b n -> p (b n)")[:, 0:n], ACT.Copy).then_inc(copied.sem, 1)
                    if u + 2 < n_units:
                        exp(u + 2)
                    if u == n_group:
                        store(0)
                store(1)
    for s in (scored, exped, normed):
        s.base += passes * n_units
    for s, grant in ((reduced, 2), (turned, 3), (summed, n_units), (copied, 1)):
        s.base += passes * n_units + grant
    staged.base += groups * n_stages
    stored.base += (groups + 1) * n_out


def stage_dilated(k, t, f):
    tab = k.place("dil_tab", 28800, DIL_HEADS, SEQ)
    stage_dilated_table(k, t, tab, 32896)
    q, key = f.pT[:, 8:12, :], f.pT[:, 12:16, :]
    pieces = ((0, SEQ),)
    stage_head_norm(k, "dil_norm", [(f.pT, 8, pieces, lambda c: k.par("qn_g", c - 8)), (f.pT, 12, pieces, lambda c: k.par("kn_g", c - 12))], 33000)
    sets = [[k.place(f"dil_{s}{i}", 33000 + (i * 3 + j) * SEQ, SEQ) for j, s in enumerate(("qs", "ks", "vs"))] for i in range(2)]
    by_tile = lambda vs: vs[:, :].rearrange("p (t d) -> p t d", d=P)

    def units(s):
        qs, ks, vs = sets[s]
        made = []
        for half in range(2):
            h = slice(half * HEAD, (half + 1) * HEAD)
            for i in range(TILES):
                n = (i + 1) * P
                made.append((qs[h, i * P:(i + 1) * P], [(ks[h, 0:n], n)],
                             lambda g, half=half, i=i, n=n: one(tab, g * 2 + half, (3 - i) * P, n),
                             lambda j, h=h, v=by_tile(vs): v[:, j, h], k.psum[h, 6, i * P:(i + 1) * P]))
        return made

    def stages(g, s):
        qs, ks, vs = sets[s]
        return [(qs[:, :], one(f.pT, g + 8, 0, SEQ)), (ks[:, :], one(f.pT, g + 12, 0, SEQ)), (by_tile(vs), f.va[:, :, bass.ds(g * P, P)])]

    stage_attention(k, "dil", DIL_HEADS // 2, units, stages, lambda g: [(one(f.mixT, g + 4, 0, SEQ), k.psum[:, 6, :])], 37000, PICKS_AT)


def add_to_x(k, gate, pieces, per=RING):
    def epilogue(dve, it, r, banks):
        for i, ((t0, n), bank) in enumerate(zip(pieces, banks)):
            x = k.xT[:, bass.ds(it * per + r, 1), t0:t0 + n].rearrange("p o y -> p (o y)")
            k.nc.vector.scalar_tensor_tensor(x, bank, gate(it * per + r, i), x, ALU.mult, ALU.add).then_inc(k.bank_read.sem, 1)
    return epilogue


def copy_to(k, place, pieces):
    def epilogue(dve, it, r, banks):
        for i, bank in enumerate(banks):
            k.nc.vector.tensor_copy(place(it, r, i), bank).then_inc(k.bank_read.sem, 1)
    return epilogue


def one(buf, c, t0, n):
    return buf[:, bass.ds(c, 1), t0:t0 + n].rearrange("p o y -> p (o y)")


LATENT = ((0, SEQ),)


def first_block(k, t, upto=99):
    stage_norm(k, LATENT, lambda i, c: k.par("norm1_g", c), None)
    f = First(k)
    with k.nc.Block() as block:
        product(k, block, t["w_projT"], 16, KD, LATENT, k.h_high, k.h_low, 28800,
                copy_to(k, lambda it, r, i: one(f.pT, it * RING + r, 0, SEQ), LATENT))
    stage_rows(k, t["w_projV"], 2, BANK, TILES, lambda b, i: (f.vm, f.va)[b][:, i, :], 28800,
               (t["w_gates"], 2 * M_HEADS, lambda i: f.gates[:, i, :]))
    stage_conv(k, t, f)
    stage_mlstm(k, t, f)
    stage_dilated(k, t, f)
    with k.nc.Block() as block:
        high, low = k.place("mix_high", BIG, KD, SEQ, dtype=FR), k.place("mix_low", BIG + KD * SEQ, KD, SEQ, dtype=FR)
        product(k, block, t["w_out"], KD, KD, LATENT, high, low, BIG + 2 * KD * SEQ, add_to_x(k, lambda c, i: 1.0, LATENT), full=f.mixT)
    return f


class Peer:

    def __init__(self, k):
        self.qT = k.place("peer_qT", BIG, 2 * PEER_HEADS, SEQ)
        self.picks = k.place("picks", PICKS_AT, 3, SEQ)
        self.gelu = k.nc.dram_tensor("gelu_dram", (N_KEYS, N_KEYS, SEQ), F32).ap()
        self.gates = k.nc.dram_tensor("gates_dram", (N_KEYS, N_KEYS, SEQ), F32).ap()


MOD_RING = 4
EIGHT = range(8)


def stage_pick(k, t, f):
    nc = k.nc
    V = k.dve
    H2 = 2 * PEER_HEADS
    at = BIG + H2 * SEQ

    def take(name, *shape, dtype=F32):
        nonlocal at
        b = k.place("pick_" + name, at, *shape, dtype=dtype)
        at += int(np.prod(shape))
        return b

    keys = take("keys", H2, N_KEYS)
    qs = take("qs", H2, P)
    rest = take("rest", N_KEYS)
    best = take("best", H2, TOPK)
    best_at = take("best_at", H2, TOPK, dtype=U32)
    best_f = take("best_f", H2, TOPK)
    cand = take("cand", TOPK, TOPK)
    cand_rest = take("cand_rest", TOPK * TOPK)
    top = take("top", PEER_HEADS, TOPK)
    top_at = take("top_at", PEER_HEADS, TOPK, dtype=U32)
    half_at = [take(f"half_at{i}", PICKS, dtype=U32) for i in range(2)]
    half_f = [take(f"half_f{i}", PICKS) for i in range(2)]
    equal = take("equal", PICKS // 2, TOPK)
    out = [take(f"out{i}", PICKS) for i in range(3)]
    total = take("total", PEER_HEADS)
    share = LAYERS * MODS // TILES
    cond = take("cond", 2, D)
    w_mod = [take(f"w_mod{r}", D) for r in range(MOD_RING)]
    mod_sum = take("mod_sum", share, 2)
    u_raw, u_high, u_low = ([take(f"u_{x}{r}", KD, N_KEYS, dtype=d) for r in range(2)] for x, d in (("raw", F32), ("high", FR), ("low", FR)))
    gelu = [take(f"gelu{r}", SEQ) for r in range(2)]
    products = k.place("pick_products", at, D, dtype=mybir.dt.bfloat16)
    assert at + D // 2 <= H_LOW, at
    scores = k.psum[:, 0:4, :].rearrange("p b (h n) -> p (b h) n", n=N_KEYS)
    (keys_in, cond_in, cond_ready, staged, scored, shifted, exped, picked, turned, stored, mod_used, u_high_ready, u_split, pre_done, gelu_done) = (
        k.sem("pick_" + x) for x in ("keys_in", "cond_in", "cond_ready", "staged", "scored", "shifted", "exped", "picked", "turned", "stored",
                                     "mod_used", "u_high_ready", "u_split", "pre_done", "gelu_done"))
    u_in, gelu_out = ([k.sem(f"pick_{x}{r}") for r in range(2)] for x in ("u_in", "gelu_out"))
    w_mod_in = [k.sem(f"pick_w_mod_in{r}") for r in range(MOD_RING)]
    per_tile = N_KEYS // TILES
    inner = per_tile // 8 - 1
    assert share == inner * 8

    def loop_eights(eng, it, eight):
        with eng.Fori(0, inner) as jt:
            eight(it * per_tile + jt * 8, jt)
        eight(it * per_tile + inner * 8, None)

    with nc.Block() as block:
        @block.sync
        def _(sp):
            sp.dma_start(keys[:, :, :], t["keys"].rearrange("p (h n) -> p h n", n=N_KEYS)).then_inc(keys_in, 16)
            sp.dma_start(cond[:, :, :], t["cond"].rearrange("p (c d) -> p c d", d=D)).then_inc(cond_in, 16)
            for r in range(2):
                sp.sem_inc(gelu_out[r], 16)
            sp.sem_inc(scored, 1)
            with sp.Fori(0, TILES) as it:
                sp.wait_ge(scored, it + 1)
                sp.dma_start(qs[:, :, :], f.qT[:, :, bass.ds(it * P, P)]).then_inc(staged, 16)

                def eight(c0, jt):
                    for r in EIGHT:
                        sp.wait_ge(u_split, c0 + (r + 1))
                        sp.dma_start(u_raw[r % 2][:, :, :], t["expert_uT"][c0 + r].rearrange("p (k e) -> p k e", e=N_KEYS)).then_inc(u_in[r % 2], 16)
                        if jt is not None:
                            j = it * share + jt * 8 + r
                            sp.wait_ge(mod_used, j + 1)
                            sp.dma_start(w_mod[r % MOD_RING][:, :], t["w_mod"][j]).then_inc(w_mod_in[r % MOD_RING], 16)

                loop_eights(sp, it, eight)
            for r in range(2):
                sp.wait_ge(gelu_out[r], 16 + 16 * (N_KEYS // 2))

        @block.gpsimd
        def _(pool):
            pool.sem_inc(u_split, 2)
            with pool.Fori(0, TILES) as it:
                def eight(c0, jt):
                    for r in EIGHT:
                        pool.wait_ge(u_high_ready, c0 + (r + 1))
                        nc.gpsimd.tensor_tensor(u_low[r % 2][:, :, :], u_raw[r % 2][:, :, :], u_high[r % 2][:, :, :].bitcast(F32), ALU.subtract
                                                ).then_inc(u_split, 1)

                loop_eights(pool, it, eight)

        @block.tensor
        def _(pe):
            pe.wait_ge(keys_in, 16)
            pe.sem_inc(pre_done, 2)
            with pe.Fori(0, TILES) as it:
                pe.wait_ge(staged, it * 16 + 16)
                pe.wait_ge(stored, it + 1)
                for i in range(H2):
                    mm = nc.tensor.matmul(scores[:, i, :], qs[:, i, :], keys[:, i, :], start=True, stop=True)
                mm.then_inc(scored, 1)

                def eight(c0, jt):
                    for r in EIGHT:
                        pe.wait_ge(u_split, c0 + (2 + r + 1))
                        pe.wait_ge(gelu_done, c0 + (r + 1))
                        for c in range(KD):
                            mm = split_product(nc, k.psum[:, 5 + r % 2, :], u_high[r % 2][:, c, :], u_low[r % 2][:, c, :],
                                               k.h_high[:, c, 0:SEQ], k.h_low[:, c, 0:SEQ], c == 0, c == KD - 1)
                        mm.then_inc(pre_done, 1)

                loop_eights(pe, it, eight)
                pe.wait_ge(picked, it + 1)
                for i in range(3):
                    mm = nc.tensor.transpose(k.psum[:, 4, i * P:(i + 1) * P], out[i][:, :], k.const("ident"))
                mm.then_inc(turned, 1)

        @block.scalar
        def _(act):
            act.wait_ge(cond_in, 16)
            nc.scalar.activation(cond[:, :, :], cond[:, :, :], ACT.Silu).then_inc(cond_ready, 1)
            act.sem_inc(gelu_done, 2)

            def round_u(c0, r):
                act.wait_ge(u_in[r % 2], c0 * 8 + 16 * (r // 2 + 1))
                if not (isinstance(c0, int) and c0 + r < 2):
                    act.wait_ge(pre_done, c0 + (r + 1))
                nc.scalar.activation(u_high[r % 2][:, :, :], u_raw[r % 2][:, :, :], ACT.Copy).then_inc(u_high_ready, 1)

            def tile(it, last):
                def eight(c0, jt):
                    for r in EIGHT:
                        if not (last and jt is None and r >= 6):
                            round_u(c0, r + 2)
                        act.wait_ge(pre_done, c0 + (2 + r + 1))
                        act.wait_ge(gelu_out[r % 2], c0 * 8 + 16 * (r // 2 + 1))
                        nc.scalar.activation(gelu[r % 2][:, :], k.psum[:, 5 + r % 2, :], ACT.Gelu).then_inc(gelu_done, 1)
                        act.wait_ge(gelu_done, c0 + (2 + r + 1))
                        act.dma_start(f.gelu[c0 + r], gelu[r % 2][:, :]).then_inc(gelu_out[r % 2], 16)
                        if jt is None and r == 5:
                            act.wait_ge(shifted, it + 1)
                            nc.scalar.activation(out[2][:, :], out[2][:, :], ACT.Exp).then_inc(exped, 1)

                loop_eights(act, it, eight)

            round_u(0, 0)
            round_u(0, 1)
            with act.Fori(0, TILES - 1) as it:
                tile(it, False)
            tile(TILES - 1, True)

        @block.vector
        def _(dve):
            dve.sem_inc(stored, 1)
            dve.sem_inc(mod_used, MOD_RING)
            dve.wait_ge(cond_ready, 1)
            with dve.Fori(0, TILES) as it:
                V.restart(dve)

                def modulate(j):
                    dve.wait_ge(w_mod_in[j % MOD_RING], it * (16 * share // MOD_RING) + 16 * (j // MOD_RING + 1))
                    dve.wait_ge(mod_used, it * share + (MOD_RING + j))
                    for c in range(2):
                        ins = nc.vector.scalar_tensor_tensor(products[:, :], w_mod[j % MOD_RING][:, :], 1.0, cond[:, c, :], ALU.mult, ALU.mult,
                                                             accum_out=mod_sum[:, j, c:c + 1])
                        if c == 0:
                            V(dve, ins)
                    ins.then_inc(mod_used, 1)

                def best16(values, left, best, where):
                    V(dve, nc.vector.max(best[:, 0:8], values))
                    V(dve, nc.vector.max_index(where[:, 0:8], best[:, 0:8], values))
                    V(dve, nc.vector.match_replace(left, best[:, 0:8], values, -3e38))
                    V(dve, nc.vector.max(best[:, 8:16], left))
                    V(dve, nc.vector.max_index(where[:, 8:16], best[:, 8:16], left))

                dve.wait_ge(scored, it + 2)
                for i in range(H2):
                    modulate(i)
                    best16(scores[:, i, :], rest[:, :], best[:, i, :], best_at[:, i, :])
                for h in range(PEER_HEADS):
                    modulate(H2 + h)
                    first = best[:, 2 * h, :].unsqueeze(2).to_broadcast([P, TOPK, TOPK])
                    second = best[:, 2 * h + 1, :].unsqueeze(1).to_broadcast([P, TOPK, TOPK])
                    V(dve, nc.vector.tensor_tensor(cand[:, :, :], first, second, ALU.add))
                    best16(cand[:, :, :].rearrange("p a b -> p (a b)"), cand_rest[:, :], top[:, h, :], top_at[:, h, :])
                weight = out[2][:, :].rearrange("p (h s) -> p h s", s=TOPK)
                nc.vector.tensor_tensor(weight, top[:, :, :], top[:, :, 0:1].to_broadcast([P, PEER_HEADS, TOPK]), ALU.subtract).then_inc(shifted, 1)
                where = top_at[:, :, :].rearrange("p h s -> p (h s)")
                V(dve, nc.vector.tensor_scalar(half_at[0][:, :], where, 4, None, ALU.logical_shift_right))
                V(dve, nc.vector.tensor_scalar(half_at[1][:, :], where, TOPK - 1, None, ALU.bitwise_and))
                V(dve, nc.vector.tensor_copy(best_f[:, :, :], best_at[:, :, :]))
                for i in range(2):
                    V(dve, nc.vector.tensor_copy(half_f[i][:, :], half_at[i][:, :]))
                heads = PEER_HEADS // 2
                for i in range(2):
                    for part in range(2):
                        p = slice(part * PICKS // 2, (part + 1) * PICKS // 2)
                        V(dve, nc.vector.tensor_tensor(equal[:, :, :], half_f[i][:, p].unsqueeze(2).to_broadcast([P, PICKS // 2, TOPK]),
                                                       k.const("iota16").unsqueeze(1).to_broadcast([P, PICKS // 2, TOPK]), ALU.is_equal))
                        eq = equal[:, :, :].rearrange("p (h s) a -> p h s a", s=TOPK)
                        number = best_f[:, :, :].rearrange("p (h i) a -> p h i a", i=2)[:, part * heads:(part + 1) * heads, i, :]
                        V(dve, nc.vector.tensor_tensor(eq, eq, number.unsqueeze(2).to_broadcast([P, heads, TOPK, TOPK]), ALU.mult))
                        V(dve, nc.vector.tensor_reduce(out[i][:, p], equal[:, :, :], AX_X, ALU.add))
                b = k.par("b_mod", it * share, share).unsqueeze(2).to_broadcast([P, share, 2])
                V(dve, nc.vector.tensor_tensor(k.modT[:, bass.ds(it * share, share), :], mod_sum[:, :, :], b, ALU.add))
                dve.wait_ge(exped, it + 1)
                V(dve, nc.vector.tensor_reduce(total[:, :], weight, AX_X, ALU.add))
                V(dve, nc.vector.reciprocal(total[:, :], total[:, :]))
                nc.vector.tensor_tensor(weight, weight, total[:, :].unsqueeze(2).to_broadcast([P, PEER_HEADS, TOPK]), ALU.mult).then_inc(picked, 1)
                dve.wait_ge(turned, it + 1)
                nc.vector.tensor_copy(f.picks[:, :, bass.ds(it * P, P)], k.psum[:, 4, 0:3 * P].rearrange("p (i n) -> p i n", n=P)).then_inc(stored, 1)
            for layer in range(LAYERS):
                for which in (1, 4):
                    j = layer * MODS + which * KD
                    V(dve, nc.vector.tensor_scalar(k.modT[:, j:j + KD, :], k.modT[:, j:j + KD, :], 1.0, None, ALU.add))


GATE_TOK = 128
GROUP = 8


def stage_gates(k, f):
    nc = k.nc
    hot1 = k.place("hot1", H_HIGH, 2, GROUP, N_KEYS)
    hot2 = k.place("hot2", H_HIGH + 2 * GROUP * N_KEYS, 2, GROUP, N_KEYS)
    plane = k.place("gate_plane", H_HIGH + 4 * GROUP * N_KEYS, 2, N_KEYS, GATE_TOK)
    groups = GATE_TOK // GROUP
    hot1_ready, same, pool_gated, scalar_gated, summed, taken = (
        k.sem("gates_" + x) for x in ("hot1_ready", "same", "pool_gated", "scalar_gated", "summed", "taken"))
    stored = [k.sem(f"gates_stored{b}") for b in range(2)]
    times = SEQ // (2 * GATE_TOK)
    n_body = 2 * groups
    by_pool = 5
    own = k.place("gate_own", H_HIGH + 4 * GROUP * N_KEYS + 2 * N_KEYS * GATE_TOK, 2, GROUP)
    iota = k.const("iota").unsqueeze(1)

    def tokens(it, g):
        return bass.ds(it * (2 * GATE_TOK) + g * GROUP, GROUP)

    with nc.Block() as block:
        @block.vector
        def _(dve):
            dve.sem_inc(summed, 2)
            with dve.Fori(0, times) as it:
                for g in range(n_body):
                    b = g % 2
                    dve.wait_ge(summed, it * n_body + (g + 1))
                    for i, (hot, ready) in enumerate(((hot2, same), (hot1, hot1_ready))):
                        pick = f.picks[:, 1 - i, tokens(it, g)].unsqueeze(2).to_broadcast([P, GROUP, N_KEYS])
                        nc.vector.tensor_tensor(hot[:, b, :, :], pick, iota.to_broadcast([P, GROUP, N_KEYS]), ALU.is_equal).then_inc(ready, 1)

        @block.gpsimd
        def _(pool):
            with pool.Fori(0, times) as it:
                for g in range(n_body):
                    rows = hot2[:, g % 2, 0:by_pool, :]
                    pool.wait_ge(same, it * n_body + (g + 1))
                    gate = f.picks[:, 2, bass.ds(it * (2 * GATE_TOK) + g * GROUP, by_pool)].unsqueeze(2).to_broadcast([P, by_pool, N_KEYS])
                    nc.gpsimd.tensor_tensor(rows, rows, gate, ALU.mult).then_inc(pool_gated, 1)

        @block.tensor
        def _(pe):
            with pe.Fori(0, times) as it:
                for g in range(n_body):
                    pe.wait_ge(hot1_ready, it * n_body + (g + 1))
                    pe.wait_ge(pool_gated, it * n_body + (g + 1))
                    pe.wait_ge(scalar_gated, it * n_body + (g + 1))
                    pe.wait_ge(taken, it * n_body + (g + 1))
                    for j in range(GROUP):
                        mm = nc.tensor.matmul(k.psum[:, 2 * (g % 4) + j // 4, (j % 4) * P:(j % 4 + 1) * P], hot1[:, g % 2, j, :], hot2[:, g % 2, j, :],
                                              start=True, stop=True)
                    mm.then_inc(summed, 1)

        @block.scalar
        def _(act):
            act.sem_inc(taken, 4)
            with act.Fori(0, times) as it:
                k.act.restart(act)

                def gate(g):
                    act.wait_ge(same, it * n_body + (g + 1))
                    k.act(act, nc.scalar.activation(own[:, g % 2, :], f.picks[:, 2, tokens(it, g)], ACT.Copy))
                    for j in range(by_pool, GROUP):
                        row = hot2[:, g % 2, j, :]
                        ins = nc.scalar.activation(row, row, ACT.Copy, scale=own[:, g % 2, j:j + 1])
                    ins.then_inc(scalar_gated, 1)

                def take(g):
                    b = g // groups
                    act.wait_ge(summed, it * n_body + (g + 3))
                    if g % groups == 0:
                        act.wait_ge(stored[b], it * 16 + 16)
                    o = plane[:, b, :, (g % groups) * GROUP:(g % groups + 1) * GROUP].rearrange("p e t -> p t e")
                    nc.scalar.activation(o, k.psum[:, 2 * (g % 4):2 * (g % 4) + 2, :].rearrange("p b (t e) -> p (b t) e", e=N_KEYS), ACT.Copy).then_inc(taken, 1)

                gate(0)
                for g in range(n_body):
                    if g + 1 < n_body:
                        gate(g + 1)
                    take(g)

        @block.sync
        def _(sp):
            for b in range(2):
                sp.sem_inc(stored[b], 16)
            with sp.Fori(0, times) as it:
                for b in range(2):
                    sp.wait_ge(taken, it * n_body + (4 + (b + 1) * groups))
                    o = f.gates.rearrange("c e t -> e c t")[:, :, bass.ds(it * (2 * GATE_TOK) + b * GATE_TOK, GATE_TOK)]
                    sp.dma_start(o, plane[:, b, :, :]).then_inc(stored[b], 16)
            for b in range(2):
                sp.wait_ge(stored[b], 16 + times * 16)


def stage_values(k, t, f):
    nc = k.nc
    pair, quads = 2, 4
    at = BIG

    def take(name, n, *shape, dtype=F32):
        nonlocal at
        size = int(np.prod(shape))
        at += n * size
        return [k.place(f"{name}{r}", at + (r - n) * size, *shape, dtype=dtype) for r in range(n)]

    v_raw, g_slot, p_slot = take("v_raw", 4, D), take("g", 4, SEQ), take("p", 4, SEQ)
    v_high, v_low = take("v_high", 4, D, dtype=FR), take("v_low", 4, D, dtype=FR)
    a_full, a_high, a_low = take("a_full", 4, SEQ), take("a_high", 4, SEQ, dtype=FR), take("a_low", 4, SEQ, dtype=FR)
    assert at <= H_LOW
    v_in, g_in, p_in = ([k.sem(f"{x}_in{r}") for r in range(4)] for x in "vgp")
    v_high_ready, v_split, gated, a_high_ready, a_split, out_summed, x_added = (
        k.sem("value_" + x) for x in ("v_high_ready", "v_split", "gated", "a_high_ready", "a_split", "out_summed", "x_added"))
    times = N_KEYS // 8
    v_rows = t["expert_v"].rearrange("(e c) d -> c e d", c=N_KEYS)

    def loaded(it, r):
        return it * 32 + 16 * (r // 4 + 1)

    with nc.Block() as block:
        @block.sync
        def _(sp):
            with sp.Fori(0, times) as it:
                for r in EIGHT:
                    c = it * 8 + r
                    sp.wait_ge(gated, it * 8 + (r + 1))
                    sp.dma_start(g_slot[r % 4][:, :], f.gates[c]).then_inc(g_in[r % 4], 16)
                    sp.dma_start(p_slot[r % 4][:, :], f.gelu[c]).then_inc(p_in[r % 4], 16)
                    sp.wait_ge(v_split, it * 8 + (r + 1))
                    sp.dma_start(v_raw[r % 4][:, :], v_rows[c]).then_inc(v_in[r % 4], 16)

        @block.scalar
        def _(act):
            with act.Fori(0, times) as it:
                for r in EIGHT:
                    act.wait_ge(v_in[r % 4], loaded(it, r))
                    act.wait_ge(out_summed, it * 32 + (r // pair * KD + KD))
                    nc.scalar.activation(v_high[r % 4][:, :], v_raw[r % 4][:, :], ACT.Copy).then_inc(v_high_ready, 1)
                    act.wait_ge(gated, it * 8 + (4 + r + 1))
                    nc.scalar.activation(a_high[r % 4][:, :], a_full[r % 4][:, :], ACT.Copy).then_inc(a_high_ready, 1)

        @block.gpsimd
        def _(pool):
            pool.sem_inc(v_split, 4)
            with pool.Fori(0, times) as it:
                for r in EIGHT:
                    pool.wait_ge(v_high_ready, it * 8 + (r + 1))
                    nc.gpsimd.tensor_tensor(v_low[r % 4][:, :], v_raw[r % 4][:, :], v_high[r % 4][:, :].bitcast(F32), ALU.subtract).then_inc(v_split, 1)

        @block.tensor
        def _(pe):
            pe.sem_inc(out_summed, 2 * KD)
            with pe.Fori(0, times) as it:
                for q in range(quads):
                    pe.wait_ge(v_split, it * 8 + (4 + (q + 1) * pair))
                    pe.wait_ge(a_split, it * 8 + (q + 1) * pair)
                    for d in range(KD):
                        pe.wait_ge(x_added, it * 32 + (q * KD + d + 1))
                        for j in range(pair):
                            r = (q * pair + j) % 4
                            s = slice(d * P, (d + 1) * P)
                            mm = split_product(nc, k.psum[:, d, :], v_high[r][:, s], v_low[r][:, s], a_high[r][:, :], a_low[r][:, :],
                                               j == 0, j == pair - 1)
                        mm.then_inc(out_summed, 1)

        @block.vector
        def _(dve):
            dve.sem_inc(gated, 4)
            dve.sem_inc(x_added, KD)

            def prepare(it, q):
                for r in range(q * pair, (q + 1) * pair):
                    dve.wait_ge(p_in[r % 4], loaded(it, r))
                    dve.wait_ge(g_in[r % 4], loaded(it, r))
                    nc.vector.tensor_tensor(a_full[r % 4][:, :], p_slot[r % 4][:, :], g_slot[r % 4][:, :], ALU.mult).then_inc(gated, 1)
                for r in range(q * pair, (q + 1) * pair):
                    dve.wait_ge(a_high_ready, it * 8 + (r + 1))
                    nc.vector.tensor_tensor(a_low[r % 4][:, :], a_full[r % 4][:, :], a_high[r % 4][:, :].bitcast(F32), ALU.subtract).then_inc(a_split, 1)

            def add(it, q):
                for d in range(KD):
                    dve.wait_ge(out_summed, it * 32 + (2 * KD + q * KD + d + 1))
                    x = k.xT[:, d, 0:SEQ]
                    nc.vector.tensor_tensor(x, x, k.psum[:, d, :], ALU.add).then_inc(x_added, 1)

            prepare(0, 0)
            prepare(0, 1)
            with dve.Fori(0, times - 1) as it:
                for q in range(quads):
                    add(it, q)
                    prepare(it, q + 2)
            for q in range(quads):
                add(times - 1, q)
                if q + 2 < quads:
                    prepare(times - 1, q + 2)


def peer(k, t):
    f = Peer(k)
    stage_norm(k, LATENT, lambda i, c: k.par("norm2_g", c), None)
    with k.nc.Block() as block:
        product(k, block, t["w_query"], 2 * PEER_HEADS, KD, LATENT, k.h_high, k.h_low, BIG + 2 * PEER_HEADS * SEQ,
                copy_to(k, lambda it, r, i: one(f.qT, it * RING + r, 0, SEQ), LATENT))
    stage_pick(k, t, f)
    stage_gates(k, f)
    stage_values(k, t, f)
    return f


class Layer:

    def __init__(self, k, i):
        self.q = k.place(f"q{i}", BIG, KD, TOK)
        self.key = k.place(f"k{i}", BIG + KD * TOK, KD, TOK)
        self.v = k.place(f"v_rows{i}", BIG + 2 * KD * TOK, ALL_TILES, D)


FREE = BIG + 3 * KD * TOK


def mod_col(k, layer, which, c, piece):
    return k.modT[:, bass.ds(c + (layer * MODS + which * KD), 1), piece]


def stage_gain(k, layer, name, which):
    with k.nc.Block() as block:
        @block.vector
        def _(dve):
            j = layer * MODS + which * KD
            for i in range(2):
                k.dve(dve, k.nc.vector.tensor_tensor(k.gain[:, i, :], k.par(name, layer * KD, KD), k.modT[:, j:j + KD, i], ALU.mult))


def modulated_norm(k, layer, name, first, pieces):
    stage_gain(k, layer, name, first + 1)
    stage_norm(k, pieces, lambda i, c: k.gain[:, i, c:c + 1], lambda i, c: mod_col(k, layer, first, c, i))


def stage_na_table(k, t, tab):
    nc = k.nc
    half_cols = GRID_W // 2
    shift = k.place("na_shift", 10240, half_cols, P, rows=RPB_W + 1)
    rpb = k.place("na_rpb", 10240 + half_cols * P, NA_HEADS * RPB_H, rows=RPB_W + 1)
    tables_in, summed, taken = (k.sem("na_table_" + s) for s in ("in", "summed", "taken"))
    wide = NA_HEADS * RPB_H
    n_pairs = GRID_W // 2
    with nc.Block() as block:
        @block.sync
        def _(sp):
            sp.dma_start(rpb[:, :], t["rpbT"]).then_inc(tables_in, 16)
            s = t["shift"].rearrange("x (c p) -> x c p", p=P)
            sp.dma_start(shift[:, :, :], s[:, 0:half_cols, :]).then_inc(tables_in, 16)
            sp.wait_ge(summed, n_pairs // 2)
            sp.dma_start(shift[:, :, :], s[:, half_cols:GRID_W, :]).then_inc(tables_in, 16)

        @block.tensor
        def _(pe):
            for j in range(n_pairs):
                if j == 0:
                    pe.wait_ge(tables_in, 32)
                if j == n_pairs // 2:
                    pe.wait_ge(tables_in, 48)
                if j >= 8:
                    pe.wait_ge(taken, 2 * (j - 7))
                for i in range(2):
                    mm = nc.tensor.matmul(k.psum[:, j % 8, i * wide:(i + 1) * wide], shift[:, (2 * j + i) % half_cols, :], rpb[:, :], start=True, stop=True)
                mm.then_inc(summed, 1)

        @block.vector
        def _(dve):
            for j in range(n_pairs):
                dve.wait_ge(summed, j + 1)
                for half in range(2):
                    p = slice(half * HEAD, (half + 1) * HEAD)
                    o = tab[p, :, half:half + RPB_H, 2 * j:2 * j + 2]
                    nc.vector.tensor_copy(o, k.psum[p, j % 8, 0:2 * wide].rearrange("p (c h s) -> p h s c", c=2, s=RPB_H)).then_inc(taken, 1)


def na_layer(k, t, layer):
    b = Layer(k, layer)
    both = PIECES
    modulated_norm(k, layer, "g_attn", 0, both)
    with k.nc.Block() as block:
        product(k, block, t["na_qk"][0:KD], KD, KD, both, k.h_high, k.h_low, FREE,
                copy_to(k, lambda it, r, i: one(b.q, it * RING + r, *both[i]), both))
    with k.nc.Block() as block:
        product(k, block, t["na_qk"][KD:2 * KD], KD, KD, both, k.h_high, k.h_low, FREE,
                copy_to(k, lambda it, r, i: one(b.key, it * RING + r, *both[i]), both))
    stage_rows(k, t["na_v"], 2, BANK, ALL_TILES, lambda n, i: b.v[:, i, n * BANK:(n + 1) * BANK], FREE)
    stage_head_norm(k, "na_norm", [(x, c0, both, lambda c, g=g: k.par(g)) for x, g in ((b.q, "na_gq"), (b.key, "na_gk")) for c0 in (0, 4)], FREE)
    tab = k.place("na_tab", FREE, NA_HEADS, RPB_H + 1, GRID_W)
    stage_na_table(k, t, tab)
    behind = FREE + NA_HEADS * (RPB_H + 1) * GRID_W
    sets = [[k.place(f"na_{s}{i}", set_at[j], TOK) for j, s in enumerate(("qs", "ks", "vs"))]
            for i, set_at in enumerate(((H_HIGH, H_HIGH + TOK, H_HIGH + 2 * TOK), (behind, behind + TOK, PICKS_AT)))]
    by_tile = lambda vs: vs[:, :].rearrange("p (t d) -> p t d", d=P)

    def units(s):
        qs, ks, vs = sets[s]
        v = by_tile(vs)
        made = []
        for half in range(2):
            h = slice(half * HEAD, (half + 1) * HEAD)
            context = (ks[h, SEQ:TOK], CTX)
            for i in range(TILES):
                made.append((qs[h, i * P:(i + 1) * P], [(ks[h, 0:SEQ], SEQ), context],
                             lambda g, half=half, i=i: tab[:, bass.ds(g * 2 + half, 1), 7 - 2 * i:15 - 2 * i, :].rearrange("p o s c -> p (o s c)"),
                             lambda j, h=h: v[:, j, h], k.psum[h, 6, i * P:(i + 1) * P]))
            for i in range(CTX // P):
                made.append((qs[h, SEQ + i * P:SEQ + (i + 1) * P], [context], None,
                             lambda j, h=h: v[:, TILES + j, h], k.psum[h, 7, i * P:(i + 1) * P]))
        return made

    def stages(g, s):
        qs, ks, vs = sets[s]
        return [(qs[:, :], one(b.q, g, 0, TOK)), (ks[:, :], one(b.key, g, 0, TOK)), (by_tile(vs), b.v[:, :, bass.ds(g * P, P)])]

    stage_attention(k, "na", NA_HEADS // 2, units, stages,
                    lambda g: [(one(b.q, g, t0, n), k.psum[:, 6 + i, 0:n]) for i, (t0, n) in enumerate(both)], H_HIGH + 3 * TOK, PICKS_AT + TOK)
    with k.nc.Block() as block:
        high, low = split_of_q(k, "na", layer)
        product(k, block, t["na_o"], KD, KD, both, high, low, FREE, add_to_x(k, lambda c, i: mod_col(k, layer, 2, c, i), both), full=b.q)


def split_of_q(k, name, layer):
    return k.place(f"{name}_o_high", H_HIGH, KD, TOK, dtype=FR), k.place(f"{name}_o_low", BIG, KD, TOK, dtype=FR)


def stage_rope(k, t, jobs, at):
    nc = k.nc
    rope = k.place("rope", at, 2, SEQ)
    part = k.place("rope_part", at + 2 * SEQ, 2, SEQ)
    rope_in, swapped, turned = (k.sem("rope_" + s) for s in ("in", "swapped", "turned"))
    with nc.Block() as block:
        @block.sync
        def _(sp):
            sp.dma_start(rope[:, :, :], t["rope"]).then_inc(rope_in, 16)

        @block.tensor
        def _(pe):
            for j, x in enumerate(jobs):
                if j >= 8:
                    pe.wait_ge(turned, j - 7)
                nc.tensor.matmul(k.psum[:, j % 8, :], k.const("swap"), x, start=True, stop=True).then_inc(swapped, 1)

        @block.vector
        def _(dve):
            dve.wait_ge(rope_in, 16)
            for j, x in enumerate(jobs):
                dve.wait_ge(swapped, j + 1)
                k.dve(dve, nc.vector.tensor_tensor(part[:, j % 2, :], k.psum[:, j % 8, :], rope[:, 1, :], ALU.mult))
                k.dve(dve, nc.vector.tensor_tensor(x, x, rope[:, 0, :], ALU.mult))
                nc.vector.tensor_tensor(x, x, part[:, j % 2, :], ALU.add).then_inc(turned, 1)


def swa_layer(k, t, layer):
    b = Layer(k, layer)
    both = PIECES
    modulated_norm(k, layer, "g_attn", 0, both)
    with k.nc.Block() as block:
        product(k, block, t["swa_q"], KD, KD, LATENT, k.h_high, k.h_low, FREE, copy_to(k, lambda it, r, i: one(b.q, it * RING + r, 0, SEQ), LATENT))
    with k.nc.Block() as block:
        product(k, block, t["swa_k"], KV_HEADS, KD, both, k.h_high, k.h_low, FREE, copy_to(k, lambda it, r, i: one(b.key, it * RING + r, *both[i]), both))
    width = KV_HEADS * HEAD
    stage_rows(k, t["swa_v"], 1, width, ALL_TILES, lambda n, i: b.v[:, i, 0:width], FREE)
    stage_head_norm(k, "swa_norm", [(b.q, 0, LATENT, lambda c: k.par("swa_gq")), (b.q, 4, LATENT, lambda c: k.par("swa_gq")),
                                    (b.key, 0, both, lambda c: k.par("swa_gk"))], FREE)
    stage_rope(k, t, [b.q[:, c, 0:SEQ] for c in range(KD)] + [b.key[:, c, 0:SEQ] for c in range(KV_HEADS)], FREE)
    per = 2
    set_size = per * SEQ + TOK + ALL_TILES * HEAD + 2 * per + 4
    sets = []
    for i in range(2):
        o = FREE + i * set_size
        sets.append((k.place(f"swa_qs{i}", o, per, SEQ), k.place(f"swa_ks{i}", o + per * SEQ, TOK),
                     k.place(f"swa_vs{i}", o + per * SEQ + TOK, ALL_TILES, HEAD),
                     k.place(f"swa_sinks{i}", o + per * SEQ + TOK + ALL_TILES * HEAD, 2 * per)))

    def units(s):
        qs, ks, vs, _ = sets[s]
        made = []
        for qc in range(per):
            for half in range(2):
                h = slice(half * HEAD, (half + 1) * HEAD)
                for i in range(TILES):
                    lo, hi = max(0, i - 1), min(TILES, i + 2)
                    n = (hi - lo) * P
                    y = (lo - (i - 1)) * P
                    made.append((qs[h, qc, i * P:(i + 1) * P], [(ks[h, lo * P:hi * P], n), (ks[h, SEQ:TOK], CTX)],
                                 lambda g, y=y, n=n: k.const("band")[:, y:y + n],
                                 lambda j, lo=lo, hi=hi: vs[:, lo + j if j < hi - lo else TILES + j - (hi - lo), :],
                                 k.psum[h, 6 + qc, i * P:(i + 1) * P]))
        return made

    def sink(u):
        s, head = u // (2 * per * TILES), u // TILES % (2 * per)
        return sets[s][3][:, head:head + 1]

    def stages(g, s):
        qs, ks, vs, sinks = sets[s]
        return [(qs[:, :, :], b.q[:, bass.ds(g * per, per), 0:SEQ]), (ks[:, :], one(b.key, g, 0, TOK)),
                (vs[:, :, :], b.v[:, :, bass.ds(g * HEAD, HEAD)]), (sinks[:, :], k.par("sink", g * (2 * per), 2 * per))]

    stage_attention(k, "swa", KV_HEADS, units, stages,
                    lambda g: [(one(b.q, g * per + c, 0, SEQ), k.psum[:, 6 + c, :]) for c in range(per)], FREE + 2 * set_size, PICKS_AT, sink)
    with k.nc.Block() as block:
        high, low = split_of_q(k, "swa", layer)
        product(k, block, t["swa_o"], KD, KD, LATENT, high, low, FREE, add_to_x(k, lambda c, i: mod_col(k, layer, 2, c, i), LATENT), full=b.q)


def conv_ffn(k, t, layer, pieces):
    nc = k.nc
    modulated_norm(k, layer, "g_ffn", 3, pieces)
    act_T = k.place(f"ffn_act{layer}", BIG, FF_CHUNKS, TOK)
    at = BIG + FF_CHUNKS * TOK
    conv = k.place(f"ffn_conv{layer}", at, 2, 2, TOK)
    conv_done, silu_done = k.sem(f"ffn_conv_done{layer}"), k.sem(f"ffn_silu_done{layer}")
    width = sum(n for _, n in pieces)
    np_ = len(pieces)

    def epilogue(dve, it, r, banks):
        pair, gate = r // 2, r % 2
        j = it * RING + (layer * 2 * FF_CHUNKS + r)
        tap = lambda i: k.par("ffn_w", j * 3 + i)
        o = conv[:, pair, gate, :]
        for (t0, n), bank in zip(pieces, banks):
            k.dve(dve, nc.vector.tensor_scalar(o[:, t0:t0 + n], bank, tap(1), k.par("ffn_b", j), ALU.mult, ALU.add))
        for (t0, n), bank in zip(pieces, banks):
            k.dve(dve, nc.vector.scalar_tensor_tensor(o[:, t0 + 1:t0 + n], bank[:, 0:n - 1], tap(0), o[:, t0 + 1:t0 + n], ALU.mult, ALU.add))
        for (t0, n), bank in zip(pieces, banks):
            nc.vector.scalar_tensor_tensor(o[:, t0:t0 + n - 1], bank[:, 1:n], tap(2), o[:, t0:t0 + n - 1], ALU.mult, ALU.add).then_inc(k.bank_read.sem, 1)
        dve.wait_ge(k.bank_read.sem, k.bank_read.at((it * RING + (RING + r + 1)) * np_))
        if gate:
            dve.sem_inc(conv_done, 1)
            dve.wait_ge(silu_done, it * 2 + (pair + 1))
            k.dve(dve, nc.vector.tensor_tensor(act_T[:, bass.ds(it * 2 + pair, 1), 0:width].rearrange("p o y -> p (o y)"),
                                               conv[:, pair, 0, 0:width], conv[:, pair, 1, 0:width], ALU.mult))

    def silu(act, it, r):
        if r % 2:
            g = conv[:, r // 2, 1, 0:width]
            act.wait_ge(conv_done, it * 2 + (r // 2 + 1))
            nc.scalar.activation(g, g, ACT.Silu).then_inc(silu_done, 1)

    with nc.Block() as block:
        product(k, block, t[f"ffn_up{layer}"], 2 * FF_CHUNKS, KD, pieces, k.h_high, k.h_low, at + 4 * TOK, epilogue, silu)
    high, low = k.place(f"ffn_high{layer}", at, FF_CHUNKS, TOK, dtype=FR), k.place(f"ffn_low{layer}", BIG, FF_CHUNKS, TOK, dtype=FR)
    with nc.Block() as block:
        product(k, block, t[f"ffn_down{layer}"], KD, FF_CHUNKS, pieces, high, low, at + FF_CHUNKS * TOK,
                add_to_x(k, lambda c, i: mod_col(k, layer, 5, c, i), pieces, RING // 2), full=act_T, parts=2, split_at=H_HIGH)


def stage_store(k, out):
    stored = k.sem("stored")
    with k.nc.Block() as block:
        @block.sync
        def _(sp):
            sp.dma_start(out, k.xT[:, :, 0:SEQ]).then_inc(stored, 16)
            sp.wait_ge(stored, 16)


def build(nc, t, out):
    k = Core(nc)
    stage_load(k, t)
    first_block(k, t)
    peer(k, t)
    na_layer(k, t, 0)
    conv_ffn(k, t, 0, PIECES)
    swa_layer(k, t, 1)
    conv_ffn(k, t, 1, LATENT)
    stage_store(k, out)


def constants():
    f = np.float32
    p, x = np.arange(P)[:, None], np.arange(P)[None, :]
    parts = dict(
        ident=p == x, tri=p <= x, ones=np.ones((P, P)), iota=np.broadcast_to(x, (P, P)),
        blocks=p // HEAD == x // HEAD, swap=p == (x // HEAD) * HEAD + (x % HEAD + HEAD // 2) % HEAD,
        causal=np.where(x <= p, 0, NEG), iota16=np.broadcast_to(np.arange(TOPK)[None], (P, TOPK)),
        band=np.where(np.abs(p + P - np.arange(3 * P)[None]) <= RADIUS, 0, NEG))
    consts = np.concatenate([np.asarray(parts[n], f) for n in CONST_SIZES], 1)
    pick = np.zeros((UNITS, UNITS, P), f)
    pick[np.arange(UNITS), np.arange(UNITS)] = 1
    dist = SEQ - 1 - np.arange(SEQ + P)
    exact = N_BUCKETS // 2
    ratio = np.log(np.maximum(dist, 1).astype(f) / f(exact)) / np.log(2048 / exact)
    large = np.minimum(exact + (ratio * (N_BUCKETS - exact)).astype(np.int32), N_BUCKETS - 1)
    bucket = np.where(dist < exact, dist, large)
    hot = np.zeros((N_BUCKETS + 1, SEQ + P), f)
    ok = dist >= 0
    hot[bucket[ok], np.nonzero(ok)[0]] = 1
    count = (dist <= 128).astype(int) + (dist % 4 == 0) + (dist % 16 == 0)
    hot[N_BUCKETS] = np.where(ok & (count > 0), np.log(np.maximum(count, 1)), NEG)
    shift = np.zeros((RPB_W + 1, GRID_W, 2, GRID_W), f)
    for kc in range(GRID_W):
        for qc in range(GRID_W):
            start = min(max(qc - 8, 0), GRID_W - 16)
            if start <= kc < start + 16:
                shift[kc - qc + 15, kc, :, qc] = 1
            else:
                shift[RPB_W, kc, :, qc] = 1
    tok = np.arange(SEQ)
    inv = (10000.0 ** (-np.arange(16, dtype=f) / f(16))).astype(f)
    ang = np.concatenate([(tok // GRID_W).astype(f)[:, None] * inv, (tok % GRID_W).astype(f)[:, None] * inv], 1)
    d = np.arange(P) % HEAD
    cos = np.cos(ang)[:, d % 32].T.astype(f)
    sin = (np.sin(ang)[:, d % 32] * np.where(d < 32, -1, 1)).T.astype(f)
    return dict(consts=consts, pick=pick, bucket_hot=hot, shift=shift.reshape(RPB_W + 1, -1), rope=np.stack([cos, sin], 1))


def layouts(a):
    cc = np.ascontiguousarray

    def chunks(w):
        kk, n = w.shape
        return cc(w.reshape(kk // P, P, n // P, P).transpose(2, 1, 0, 3)).reshape(n // P, P, -1)

    def blocks(w, width):
        kk, n = w.shape
        return cc(w.reshape(kk // P, P, n // width, width).transpose(2, 1, 0, 3)).reshape(n // width, P, -1)

    def cols(v):
        return v.reshape(-1, P).T

    def rows(v):
        return np.broadcast_to(v.reshape(1, -1), (P, v.size))

    def ff(v):
        return v.reshape(*v.shape[:-1], 2, FF_CHUNKS, P).swapaxes(-3, -2)

    w_in = a["w_in"][0]
    mw, aw = M_HEADS * P, DIL_HEADS * HEAD
    u, vm, z, gates = w_in[:, 0:mw], w_in[:, mw:2 * mw], w_in[:, 2 * mw:3 * mw], w_in[:, 3 * mw:3 * mw + 2 * M_HEADS]
    at = 3 * mw + 2 * M_HEADS
    qa, ka, va = (w_in[:, at + i * aw:at + (i + 1) * aw] for i in range(3))
    qkv = a["swa_w_qkv_2"][0]
    swa_k = qkv[:, D:D + KV_HEADS * HEAD].reshape(D, KV_HEADS, 1, HEAD)
    swa_k = np.broadcast_to(swa_k, (D, KV_HEADS, 2, HEAD)).reshape(D, -1)
    na = a["na_w_qkv_2"][0]
    rpb = a["na_rpb_2"][0]
    rpbT = np.concatenate([rpb.transpose(2, 0, 1), np.full((1, NA_HEADS, RPB_H), NEG, np.float32)], 0)
    parts = dict(
        norm1_g=cols(a["norm1_g"][0]), conv_w=a["conv_w"][0].reshape(4, M_HEADS, P).transpose(2, 1, 0).reshape(P, -1),
        conv_b=cols(a["conv_b"][0]), mh_g=cols(a["mh_norm_g"][0]), skip=cols(a["skip_m"][0]), qn_g=cols(a["qn_g"][0]),
        kn_g=cols(a["kn_g"][0]), norm2_g=cols(a["norm2_g"][0]), gate_b=rows(np.concatenate([a["ig_b"][0], a["fg_b"][0]])),
        g_attn=cols(a["g_attn_2"]), g_ffn=cols(a["g_ffn_2"]), b_mod=cols(a["b_mod_2"]),
        na_gq=np.tile(a["na_g_q_2"][0], 2)[:, None], na_gk=np.tile(a["na_g_k_2"][0], 2)[:, None],
        swa_gq=np.tile(a["swa_g_q_2"][0], 2)[:, None], swa_gk=np.tile(a["swa_g_k_2"][0], 2)[:, None],
        sink=rows(a["swa_sink_2"][0]),
        ffn_w=ff(a["ffn_conv_w_2"]).transpose(4, 0, 2, 3, 1).reshape(P, -1),
        ffn_b=ff(a["ffn_conv_b_2"]).transpose(3, 0, 1, 2).reshape(P, -1))
    out = dict(constants())
    out.update(
        xT=cc(a["x"][0].T.reshape(KD, P, SEQ).transpose(1, 0, 2)), ctxT=cc(a["ctx_2"][0].T.reshape(KD, P, CTX).transpose(1, 0, 2)),
        params=cc(np.concatenate([parts[n] for n in PARAM_SIZES], 1)),
        w_mod=cc(np.concatenate(list(a["w_mod_2"]), 1).T).reshape(LAYERS * MODS, P, D), cond=cc(rows(np.stack([a["c_2"][0], a["c_ctx_2"]]))),
        w_projT=chunks(np.concatenate([u, z, qa, ka], 1)), w_projV=blocks(np.concatenate([vm, va], 1), BANK),
        w_gates=blocks(gates, 2 * M_HEADS)[0],
        w_qk=cc(np.stack([a["wq_m"][0], a["wk_m"][0]]).transpose(2, 0, 1, 3)),
        rel_bias=a["rel_bias"], w_out=chunks(a["w_out"][0]), w_query=chunks(a["w_query"][0]),
        keys=cc(np.stack([a["sub_keys1"][0], a["sub_keys2"][0]]).transpose(3, 1, 0, 2)).reshape(P, -1),
        expert_uT=cc(a["expert_u"][0].reshape(N_KEYS, N_KEYS, KD, P).transpose(1, 3, 2, 0)).reshape(N_KEYS, P, -1),
        expert_v=a["expert_v"][0],
        na_qk=chunks(na[:, 0:2 * D]), na_v=blocks(na[:, 2 * D:], BANK), na_o=chunks(a["na_w_o_2"][0]), rpbT=cc(rpbT).reshape(RPB_W + 1, -1),
        swa_q=chunks(qkv[:, 0:D]), swa_k=chunks(swa_k), swa_v=blocks(qkv[:, D + KV_HEADS * HEAD:], KV_HEADS * HEAD),
        swa_o=chunks(a["swa_w_o_2"][0]))
    for i in range(LAYERS):
        out[f"ffn_up{i}"] = chunks(ff(a["ffn_w_up_2"][i]).reshape(D, -1))
        out[f"ffn_down{i}"] = chunks(a["ffn_w_down_2"][i])
    return {n: cc(v) for n, v in out.items()}


def kernel(**inputs):
    import concourse.bacc as bacc
    from concourse.bass_utils import run_bass_kernel_spmd as run

    arrays = layouts({n: np.asarray(v) for n, v in inputs.items()})
    nc = bacc.Bacc("TRN2", target_bir_lowering=False, num_devices=1)
    t = {n: nc.dram_tensor(f"in_{n}", v.shape, mybir.dt.from_np(v.dtype), kind="ExternalInput").ap() for n, v in arrays.items()}
    out = nc.dram_tensor("out_xT", (P, KD, SEQ), F32, kind="ExternalOutput").ap()
    build(nc, t, out)
    got = run(nc, [{f"in_{n}": v for n, v in arrays.items()}], core_ids=[0]).results[0]["out_xT"]
    return np.ascontiguousarray(np.asarray(got).transpose(1, 0, 2).reshape(D, SEQ).T)[None]
```

```python
import numpy as np

import concourse.bass as bass
from concourse import mybir

F32 = mybir.dt.float32
U32 = mybir.dt.uint32
FR = mybir.dt.float32r
ALU = mybir.AluOpType
ACT = mybir.ActivationFunctionType
AX_X = mybir.AxisListType.X

P = 128
BANK = 512
D = 1024
KD = D // P
SEQ = 512
CTX = 256
TOK = SEQ + CTX
TILES = SEQ // P
ALL_TILES = TOK // P
EPS = 1e-6
NEG = -1e30
RING = 4

M_HEADS = 4
CHUNKS = SEQ // P
UNITS = CHUNKS * M_HEADS
DIL_HEADS = 8
HEAD = 64
N_BUCKETS = 32
PEER_HEADS = 8
TOPK = 16
N_KEYS = 128
PICKS = PEER_HEADS * TOPK
NA_HEADS = 16
KV_HEADS = 4
GRID_W = 64
ROWS = SEQ // GRID_W
RPB_H = 15
RPB_W = 31
D_FF = 2816
FF_CHUNKS = D_FF // P
RADIUS = 128
LAYERS = 2
MODS = 6 * KD

PARAM_SIZES = dict(
    norm1_g=KD, conv_w=4 * M_HEADS, conv_b=M_HEADS, mh_g=M_HEADS, skip=M_HEADS, qn_g=4, kn_g=4, norm2_g=KD,
    gate_b=2 * M_HEADS, g_attn=LAYERS * KD, g_ffn=LAYERS * KD, b_mod=LAYERS * MODS,
    na_gq=1, na_gk=1, swa_gq=1, swa_gk=1, sink=NA_HEADS,
    ffn_w=LAYERS * 2 * FF_CHUNKS * 3, ffn_b=LAYERS * 2 * FF_CHUNKS,
)
CONST_SIZES = dict(ident=P, tri=P, ones=P, iota=P, heads=HEAD, window=GRID_W, swap=P, causal=P, iota16=TOPK, band=3 * P)


def offsets(sizes):
    out, at = {}, 0
    for name, n in sizes.items():
        out[name] = (at, n)
        at += n
    return out, at


PARAMS, N_PARAMS = offsets(PARAM_SIZES)
CONSTS, N_CONSTS = offsets(CONST_SIZES)

SBUF_START = 16512
SBUF_FLOATS = (229344 - SBUF_START) // 4
PICKS_AT = 8560
H_HIGH = 10240
BIG = H_HIGH + KD * TOK
H_LOW = 47064
FREE = BIG + 3 * KD * TOK


class Chain:

    def __init__(self, sem):
        self.sem, self.n = sem, 0

    def __call__(self, eng, ins):
        self.n += 1
        ins.then_inc(self.sem, 1)
        eng.wait_ge(self.sem, self.n)

    def restart(self, eng):
        eng.sem_clear(self.sem)
        self.n = 0


class Signal:

    def __init__(self, sem):
        self.sem, self.base = sem, 0

    def at(self, n):
        return n + self.base


class Core:

    def __init__(self, nc):
        self.nc = nc
        self.names = 0
        self.signals = {}
        self.psum = nc.alloc_psum_tensor("psum", [P, 8, BANK], F32)
        self.dve = Chain(nc.alloc_semaphore("vector_done"))
        self.act = Chain(nc.alloc_semaphore("scalar_done"))
        self.weights_in = [Signal(nc.alloc_semaphore(f"weights_in{r}")) for r in range(RING)]
        self.product_done = Signal(nc.alloc_semaphore("product_done"))
        self.bank_read = Signal(nc.alloc_semaphore("bank_read"))
        self.xT = self.place("xT", 0, KD, TOK)
        self.params = self.place("params", 6144, N_PARAMS)
        self.consts = self.place("consts", 6144 + 704, N_CONSTS)
        self.modT = self.place("modT", 8304, LAYERS * MODS, 2)
        self.gain = self.place("gain", 8512, 2, KD)
        self.h_high = self.place("h_high", H_HIGH, KD, TOK, dtype=FR)
        self.h_low = self.place("h_low", H_LOW, KD, TOK, dtype=FR)
        self.w_high, self.w_low, self.x_high, self.x_low = (self.shared(s) for s in ("w_high", "w_low", "x_high", "x_low"))

    def place(self, name, at, *shape, dtype=F32, rows=P):
        n = int(np.prod(shape))
        assert at + n <= SBUF_FLOATS, (name, at + n, SBUF_FLOATS)
        return self.nc.alloc_sbuf_tensor_at(name, [rows, *shape], dtype, offset=SBUF_START + 4 * at)

    def sem(self, name):
        return self.nc.alloc_semaphore(name)

    def shared(self, name):
        if name not in self.signals:
            self.signals[name] = Signal(self.nc.alloc_semaphore(name))
        return self.signals[name]

    def par(self, name, i=0, n=1):
        return self.params[:, bass.ds(i + PARAMS[name][0], n)]

    def const(self, name, rows=P):
        at, n = CONSTS[name]
        return self.consts[0:rows, at:at + n]


PIECES = ((0, SEQ), (SEQ, CTX))


def stage_load(k, t):
    loaded = k.sem("loaded")
    with k.nc.Block() as block:
        @block.sync
        def _(sp):
            sp.dma_start(k.xT[:, :, 0:SEQ], t["xT"]).then_inc(loaded, 16)
            sp.dma_start(k.xT[:, :, SEQ:TOK], t["ctxT"]).then_inc(loaded, 16)
            sp.dma_start(k.params[:, :], t["params"]).then_inc(loaded, 16)
            sp.dma_start(k.consts[:, :], t["consts"]).then_inc(loaded, 16)
            sp.wait_ge(loaded, 64)


def split_product(nc, bank, w_high, w_low, x_high, x_low, first, last):
    nc.tensor.matmul(bank, w_high, x_high, start=first, stop=False)
    nc.tensor.matmul(bank, w_high, x_low, start=False, stop=False)
    return nc.tensor.matmul(bank, w_low, x_high, start=False, stop=last)


def product(k, block, w, n_chunks, k_chunks, pieces, high, low, at, epilogue, scalar=None, full=None, norm=None, parts=1,
            split_at=None):
    nc = k.nc
    k.names += 1
    kp = k_chunks // parts
    n_raw = RING // parts
    raw = [k.place(f"w_raw{k.names}_{r}", at + r * kp * P, kp, P) for r in range(n_raw)]
    split_at = at + n_raw * kp * P if split_at is None else split_at
    w_high, w_low = ([k.place(f"w_{s}{k.names}_{r}", split_at + (2 * i + r) * kp * P, kp, P, dtype=FR) for r in range(2)]
                     for i, s in enumerate(("high", "low")))
    per = RING // parts
    passes = n_chunks // per
    n_pieces = len(pieces)
    width = sum(n for _, n in pieces)
    assert passes * per == n_chunks and kp * parts == k_chunks

    def banks(r):
        return [k.psum[:, r // parts * n_pieces + i, 0:n] for i, (_, n) in enumerate(pieces)]

    @block.sync
    def _(sp):
        with sp.Fori(0, passes) as it:
            for r in range(RING):
                sp.wait_ge(k.w_low.sem, k.w_low.at(it * RING + (r + 1)))
                source = w[it * per + r // parts].rearrange("p (k n) -> p k n", n=P)[:, r % parts * kp:(r % parts + 1) * kp, :]
                sp.dma_start(raw[r % n_raw][:, :, :], source).then_inc(k.weights_in[r % n_raw].sem, 16)

    @block.scalar
    def _(act):
        def round_weights(it, r):
            act.wait_ge(k.weights_in[r % n_raw].sem, k.weights_in[r % n_raw].at(it * (16 * parts) + 16 * (r // n_raw + 1)))
            if not (isinstance(it, int) and it * RING + r < 2):
                act.wait_ge(k.product_done.sem, k.product_done.at((it * RING + (r - 1)) * n_pieces))
            nc.scalar.activation(w_high[r % 2][:, :, :], raw[r % n_raw][:, :, :], ACT.Copy).then_inc(k.w_high.sem, 1)

        if norm:
            norm.squares(act)
            round_weights(0, 0)
            round_weights(0, 1)
            norm.scalar(act)
        elif full is not None:
            for c in range(k_chunks):
                if c == 4:
                    round_weights(0, 0)
                    round_weights(0, 1)
                nc.scalar.activation(high[:, c, 0:width], full[:, c, 0:width], ACT.Copy).then_inc(k.x_high.sem, 1)
        else:
            round_weights(0, 0)
            round_weights(0, 1)
        if passes > 1:
            with act.Fori(0, passes - 1) as it:
                for r in range(RING):
                    round_weights(it, r + 2)
                    if scalar:
                        scalar(act, it, r)
        for r in range(RING):
            if r + 2 < RING:
                round_weights(passes - 1, r + 2)
            if scalar:
                scalar(act, passes - 1, r)

    @block.gpsimd
    def _(pool):
        pool.sem_inc(k.w_low.sem, n_raw)
        with pool.Fori(0, passes) as it:
            for r in range(RING):
                pool.wait_ge(k.w_high.sem, k.w_high.at(it * RING + (r + 1)))
                nc.gpsimd.tensor_tensor(w_low[r % 2][:, :, :], raw[r % n_raw][:, :, :], w_high[r % 2][:, :, :].bitcast(F32), ALU.subtract
                                        ).then_inc(k.w_low.sem, 1)

    @block.tensor
    def _(pe):
        if norm:
            norm.tensor(pe)
        with pe.Fori(0, passes) as it:
            for r in range(RING):
                pe.wait_ge(k.w_low.sem, k.w_low.at(it * RING + (n_raw + r + 1)))
                part = r % parts
                if part == 0:
                    pe.wait_ge(k.bank_read.sem, k.bank_read.at((it * per + (r // parts + 1)) * n_pieces))
                for bank, (t0, n) in zip(banks(r), pieces):
                    for c in range(kp):
                        kc = part * kp + c
                        if full is not None or norm:
                            pe.wait_ge(k.x_low.sem, k.x_low.at(kc + 1))
                        mm = split_product(nc, bank, w_high[r % 2][:, c, :], w_low[r % 2][:, c, :], high[:, kc, t0:t0 + n], low[:, kc, t0:t0 + n],
                                           kc == 0, kc == k_chunks - 1)
                    mm.then_inc(k.product_done.sem, 1)

    @block.vector
    def _(dve):
        dve.sem_inc(k.bank_read.sem, per * n_pieces)
        if norm:
            norm.vector(dve)
        elif full is not None:
            for c in range(k_chunks):
                dve.wait_ge(k.x_high.sem, k.x_high.at(c + 1))
                nc.vector.tensor_tensor(low[:, c, 0:width], full[:, c, 0:width], high[:, c, 0:width].bitcast(F32), ALU.subtract
                                        ).then_inc(k.x_low.sem, 1)
        with dve.Fori(0, passes) as it:
            k.dve.restart(dve)
            for r in range(parts - 1, RING, parts):
                dve.wait_ge(k.product_done.sem, k.product_done.at((it * RING + (r + 1)) * n_pieces))
                epilogue(dve, it, r // parts, banks(r))

    for s in k.weights_in[0:n_raw]:
        s.base += 16 * passes * parts
    k.product_done.base += n_chunks * parts * n_pieces
    k.bank_read.base += (n_chunks + per) * n_pieces
    k.w_high.base += n_chunks * parts
    k.w_low.base += n_chunks * parts + n_raw
    if norm:
        norm.count()
    if full is not None or norm:
        k.x_high.base += k_chunks
        k.x_low.base += k_chunks


def newton(k, dve, y, v, t):
    nc = k.nc
    k.dve(dve, nc.vector.tensor_tensor(t, y, y, ALU.mult))
    k.dve(dve, nc.vector.tensor_tensor(t, t, v, ALU.mult))
    k.dve(dve, nc.vector.tensor_scalar(t, t, -0.5, 1.5, ALU.mult, ALU.add))
    k.dve(dve, nc.vector.tensor_tensor(y, y, t, ALU.mult))


class Norm:

    def __init__(self, k, pieces, gain, shift=None, first=None):
        self.k, self.nc, self.pieces, self.gain, self.shift, self.first = k, k.nc, pieces, gain, shift, first
        k.names += 1
        self.width = sum(n for _, n in pieces)
        self.sq = k.place(f"norm_sq{k.names}", BIG, KD, TOK)
        self.h = k.place(f"norm_h{k.names}", BIG, KD, TOK)
        self.v, self.y, self.u = (k.place(f"norm_{x}{k.names}", BIG + (KD + i) * TOK, TOK) for i, x in enumerate("vyu"))
        self.sq_ready, self.pair_ready, self.sum_ready, self.v_ready, self.y_ready, self.h_ready = (
            k.shared(f"norm_{x}") for x in ("sq_ready", "pair_ready", "sum_ready", "v_ready", "y_ready", "h_ready"))

    def squares(self, act):
        for c in range(KD):
            self.nc.scalar.activation(self.sq[:, c, 0:self.width], self.k.xT[:, c, 0:self.width], ACT.Square).then_inc(self.sq_ready.sem, 1)

    def scalar(self, act):
        k, nc = self.k, self.nc
        v, y = self.v[:, 0:self.width], self.y[:, 0:self.width]
        act.wait_ge(self.v_ready.sem, self.v_ready.at(1))
        k.act(act, nc.scalar.activation(y, v, ACT.Ln))
        nc.scalar.activation(y, y, ACT.Exp, scale=-0.5).then_inc(self.y_ready.sem, 1)
        for c in range(KD):
            act.wait_ge(self.h_ready.sem, self.h_ready.at(c + 1))
            for i, (t0, n) in enumerate(self.pieces):
                h, high = self.h[:, c, t0:t0 + n], k.h_high[:, c, t0:t0 + n]
                if self.shift is None:
                    ins = nc.scalar.activation(high, h, ACT.Copy)
                else:
                    ins = nc.scalar.activation(high, h, ACT.Identity, bias=self.shift(i, c))
            ins.then_inc(k.x_high.sem, 1)

    def tensor(self, pe):
        k = self.k
        for c in range(0, KD, 2):
            pe.wait_ge(self.pair_ready.sem, self.pair_ready.at(c // 2 + 1))
            for i, (t0, n) in enumerate(self.pieces):
                mm = self.nc.tensor.matmul(k.psum[:, i, 0:n], k.const("ones"), self.sq[:, c, t0:t0 + n], start=(c == 0), stop=(c == KD - 2))
        mm.then_inc(self.sum_ready.sem, 1)

    def vector(self, dve):
        k, nc, pieces = self.k, self.nc, self.pieces
        w = self.width
        if self.first:
            self.first(dve)
        for c in range(0, KD, 2):
            dve.wait_ge(self.sq_ready.sem, self.sq_ready.at(c + 2))
            nc.vector.tensor_tensor(self.sq[:, c, 0:w], self.sq[:, c, 0:w], self.sq[:, c + 1, 0:w], ALU.add).then_inc(self.pair_ready.sem, 1)
        dve.wait_ge(self.sum_ready.sem, self.sum_ready.at(1))
        for i, (t0, n) in enumerate(pieces):
            ins = nc.vector.tensor_scalar(self.v[:, t0:t0 + n], k.psum[:, i, 0:n], 1.0 / D, EPS, ALU.mult, ALU.add)
        ins.then_inc(self.v_ready.sem, 1)
        dve.wait_ge(self.y_ready.sem, self.y_ready.at(1))
        newton(k, dve, self.y[:, 0:w], self.v[:, 0:w], self.u[:, 0:w])

        def scaled(c):
            for i, (t0, n) in enumerate(pieces):
                ins = nc.vector.scalar_tensor_tensor(self.h[:, c, t0:t0 + n], k.xT[:, c, t0:t0 + n], self.gain(i, c), self.y[:, t0:t0 + n], ALU.mult, ALU.mult)
            ins.then_inc(self.h_ready.sem, 1)

        def low(c):
            dve.wait_ge(k.x_high.sem, k.x_high.at(c + 1))
            for i, (t0, n) in enumerate(pieces):
                h, o, high = self.h[:, c, t0:t0 + n], k.h_low[:, c, t0:t0 + n], k.h_high[:, c, t0:t0 + n].bitcast(F32)
                if self.shift is None:
                    ins = nc.vector.tensor_tensor(o, h, high, ALU.subtract)
                else:
                    ins = nc.vector.scalar_tensor_tensor(o, h, self.shift(i, c), high, ALU.add, ALU.subtract)
            ins.then_inc(k.x_low.sem, 1)

        for c in range(KD + 2):
            if c < KD:
                scaled(c)
            if c >= 2:
                low(c - 2)

    def count(self):
        for s, n in ((self.sq_ready, KD), (self.pair_ready, KD // 2), (self.sum_ready, 1), (self.v_ready, 1), (self.y_ready, 1), (self.h_ready, KD)):
            s.base += n


def stage_rows(k, w, n_blocks, width, tiles, out, at):
    nc = k.nc
    k.names += 1
    assert width <= BANK
    raw = [k.place(f"rows_w{k.names}_{r}", at + r * BANK, BANK) for r in range(RING)]
    high, low = ([k.place(f"rows_{s}{k.names}_{r}", at + (RING * i + r) * BANK, BANK, dtype=FR) for r in range(RING)]
                 for i, s in ((1, "high"), (2, "low")))
    taken = k.shared("rows_taken")
    steps = [(b, c) for b in range(n_blocks) for c in range(KD)]
    with nc.Block() as block:
        @block.sync
        def _(sp):
            for s, (b, c) in enumerate(steps):
                if s >= RING:
                    sp.wait_ge(k.w_low.sem, k.w_low.at(s - RING + 1))
                sp.dma_start(raw[s % RING][:, 0:width], w[b][:, c * width:(c + 1) * width]).then_inc(k.weights_in[s % RING].sem, 16)

        @block.scalar
        def _(act):
            def round_rows(s):
                act.wait_ge(k.weights_in[s % RING].sem, k.weights_in[s % RING].at(16 * (s // RING + 1)))
                if s >= RING:
                    act.wait_ge(k.product_done.sem, k.product_done.at((s - RING + 1) * tiles))
                nc.scalar.activation(high[s % RING][:, 0:width], raw[s % RING][:, 0:width], ACT.Copy).then_inc(k.w_high.sem, 1)

            for s in range(RING - 1):
                round_rows(s)
            for s, (b, c) in enumerate(steps):
                if s + RING - 1 < len(steps):
                    round_rows(s + RING - 1)
                if c == KD - 1:
                    for i in range(tiles):
                        act.wait_ge(k.product_done.sem, k.product_done.at(s * tiles + i + 1))
                        for place, n0, n in out(b, i):
                            ins = nc.scalar.activation(place, k.psum[:, (b * tiles + i) % 8, n0:n0 + n], ACT.Copy)
                        ins.then_inc(taken.sem, 1)

        @block.vector
        def _(dve):
            for s, (b, c) in enumerate(steps):
                dve.wait_ge(k.w_high.sem, k.w_high.at(s + 1))
                nc.vector.tensor_tensor(low[s % RING][:, 0:width], raw[s % RING][:, 0:width], high[s % RING][:, 0:width].bitcast(F32), ALU.subtract
                                        ).then_inc(k.w_low.sem, 1)

        @block.tensor
        def _(pe):
            for s, (b, c) in enumerate(steps):
                pe.wait_ge(k.w_low.sem, k.w_low.at(s + 1))
                for i in range(tiles):
                    job = b * tiles + i
                    if c == 0 and job >= 8:
                        pe.wait_ge(taken.sem, taken.at(job - 7))
                    t = slice(i * P, (i + 1) * P)
                    split_product(nc, k.psum[:, job % 8, 0:width], k.h_high[:, c, t], k.h_low[:, c, t], high[s % RING][:, 0:width], low[s % RING][:, 0:width],
                                  c == 0, c == KD - 1).then_inc(k.product_done.sem, 1)
    for r in range(RING):
        k.weights_in[r].base += 16 * len(range(r, len(steps), RING))
    k.product_done.base += len(steps) * tiles
    k.w_high.base += len(steps)
    k.w_low.base += len(steps)
    taken.base += n_blocks * tiles


class First:

    def __init__(self, k):
        self.pT = k.place("projT", BIG, 16, SEQ)
        self.vm = k.place("vm", 24576, CHUNKS, BANK)
        self.va = k.place("va", 26624, CHUNKS, BANK)
        self.gates = k.place("gates", 28672, CHUNKS, 2 * M_HEADS)
        self.cT = k.place("convT", 28800, M_HEADS, SEQ)
        self.w_qk = k.place("w_qk", 30848, 2, M_HEADS, P)
        self.qT = k.place("m_qT", 31872, M_HEADS, SEQ)
        self.kT = k.place("m_kT", 33920, M_HEADS, SEQ)
        self.k_rows = k.place("m_k_rows", 35968, CHUNKS, M_HEADS, P)
        self.mixT = k.place("mixT", H_HIGH, KD, SEQ)


M_SCALE = P ** -0.5


def stage_conv(k, t, f):
    nc = k.nc
    w_in, conv_done, c_ready, qk_summed, qk_taken, rows_summed = (
        k.sem(s) for s in ("w_qk_in", "conv_done", "c_ready", "qk_summed", "qk_taken", "k_rows_summed"))
    with nc.Block() as block:
        @block.sync
        def _(sp):
            sp.dma_start(f.w_qk[:, :, :, :], t["w_qk"]).then_inc(w_in, 16)

        @block.vector
        def _(dve):
            for h in range(M_HEADS):
                u, c = f.pT[:, h, :], f.cT[:, h, :]
                tap = lambda j: k.par("conv_w", h * 4 + j)
                k.dve(dve, nc.vector.tensor_scalar(c, u, tap(3), k.par("conv_b", h), ALU.mult, ALU.add))
                for back in (1, 2, 3):
                    ins = nc.vector.scalar_tensor_tensor(c[:, back:SEQ], u[:, 0:SEQ - back], tap(3 - back),
                                                         c[:, back:SEQ], ALU.mult, ALU.add)
                    if back < 3:
                        k.dve(dve, ins)
                    else:
                        ins.then_inc(conv_done, 1)
            for i in range(2 * M_HEADS):
                dve.wait_ge(qk_summed, i + 1)
                o, scale = (f.qT[:, i, :], 1.0) if i < M_HEADS else (f.kT[:, i - M_HEADS, :], M_SCALE)
                nc.vector.tensor_scalar(o, k.psum[:, i, :], scale, None, ALU.mult).then_inc(qk_taken, 1)
            for n in range(CHUNKS):
                dve.wait_ge(rows_summed, n + 1)
                nc.vector.tensor_scalar(f.k_rows[:, n, :, :].rearrange("p h d -> p (h d)"), k.psum[:, n, :], M_SCALE, None, ALU.mult)

        @block.scalar
        def _(act):
            for h in range(M_HEADS):
                act.wait_ge(conv_done, h + 1)
                nc.scalar.activation(f.cT[:, h, :], f.cT[:, h, :], ACT.Silu).then_inc(c_ready, 1)
            nc.scalar.activation(f.pT[:, 4:8, :], f.pT[:, 4:8, :], ACT.Sigmoid)

        @block.tensor
        def _(pe):
            pe.wait_ge(w_in, 16)
            for i in range(2 * M_HEADS):
                h = i % M_HEADS
                if i < M_HEADS:
                    pe.wait_ge(c_ready, h + 1)
                nc.tensor.matmul(k.psum[:, i, :], f.w_qk[:, i // M_HEADS, h, :], f.cT[:, h, :], start=True, stop=True).then_inc(qk_summed, 1)
            for n in range(CHUNKS):
                pe.wait_ge(qk_taken, n + 1)
                for h in range(M_HEADS):
                    mm = nc.tensor.matmul(k.psum[:, n, h * P:(h + 1) * P], f.cT[:, h, n * P:(n + 1) * P], f.w_qk[:, 1, h, :],
                                          start=True, stop=True)
                mm.then_inc(rows_summed, 1)


def stage_mlstm(k, t, f):
    nc = k.nc
    V = k.dve
    small = 51904
    v_aug = k.place("v_aug", 38016, UNITS, P + 1)
    dm = k.place("d_mat", 40080, UNITS, P)
    sdT = k.place("sdT", 42128, UNITS, P)
    state = k.place("state", 44176, CHUNKS - 1, M_HEADS, P + 1)
    pick = k.place("pick", 45728, UNITS, P, rows=UNITS)
    num = k.place("num", 47776, UNITS, P + 1)
    tmp = k.place("m_tmp", 49840, UNITS, P + 1)
    col = lambda i, n=UNITS: k.place(f"m_col{i}", small + i * UNITS, n)
    lf, li, b, g, inter, mt, iw, den, wts, bl = (col(i) for i in range(10))
    bcast = k.place("m_bcast", small + 10 * UNITS, 4, UNITS)
    line = k.place("m_line", small + 14 * UNITS, 6, UNITS, rows=1)
    rT = k.place("m_rT", small + 20 * UNITS, P, rows=UNITS)
    bT = k.place("m_bT", small + 20 * UNITS + P, P, rows=UNITS)
    mlT = k.place("m_mlT", small + 20 * UNITS + 2 * P, 1, rows=UNITS)
    gb = k.place("m_gb", small + 20 * UNITS + 2 * P + 32, CHUNKS, 2 * M_HEADS)
    (pick_in, gates_ready, soft_ready, lf_ready, cum_summed, r_ready, ml_ready, ml_turned, scan_ready, scan_exp, pack_ready,
     packed, g_ready, wts_ready, kw_ready, carried, rows_spread, d_ready, d_exp, scored, taken, sd_ready, turned, sdT_ready,
     state_ready, num_summed, num_taken, rms_ready, rms_done, h_ready, h_turned, h_taken) = (k.sem("m_" + s) for s in (
         "pick_in", "gates_ready", "soft_ready", "lf_ready", "cum_summed", "r_ready", "ml_ready", "ml_turned", "scan_ready",
         "scan_exp", "pack_ready", "packed", "g_ready", "wts_ready", "kw_ready", "carried", "rows_spread", "d_ready", "d_exp",
         "scored", "taken", "sd_ready", "turned", "sdT_ready", "state_ready", "num_summed", "num_taken", "rms_ready",
         "rms_done", "h_ready", "h_turned", "h_taken"))
    ps = k.psum
    flat4 = lambda bank: ps[:, bank:bank + 4, :].rearrange("p b (h l) -> p (b h) l", l=P)
    over = lambda c: c.unsqueeze(2).to_broadcast([P, UNITS, P])
    W1 = P + 1

    with nc.Block() as block:
        @block.sync
        def _(sp):
            sp.dma_start(pick[:, :, :], t["pick"]).then_inc(pick_in, 16)

        @block.vector
        def _(dve):
            bias = k.par("gate_b", 0, 2 * M_HEADS).unsqueeze(1).to_broadcast([P, CHUNKS, 2 * M_HEADS])
            V(dve, nc.vector.tensor_tensor(gb[:, :, :], f.gates[:, :, :], bias, ALU.add))
            by_unit = lambda c: c[:, :].rearrange("p (n h) -> p n h", h=M_HEADS)
            V(dve, nc.vector.tensor_copy(by_unit(li), gb[:, :, 0:M_HEADS]))
            V(dve, nc.vector.tensor_copy(by_unit(lf), gb[:, :, M_HEADS:2 * M_HEADS]))
            nc.vector.scalar_tensor_tensor(g[:, :], lf[:, :], -1.0, lf[:, :], ALU.mult, ALU.min).then_inc(gates_ready, 1)
            V(dve, nc.vector.tensor_scalar(lf[:, :], lf[:, :], 0.0, None, ALU.min))
            dve.wait_ge(soft_ready, 1)
            nc.vector.tensor_tensor(lf[:, :], lf[:, :], g[:, :], ALU.subtract).then_inc(lf_ready, 1)
            V(dve, nc.vector.memset(v_aug[:, :, P:W1], 1.0))
            V(dve, nc.vector.tensor_copy(v_aug[:, :, 0:P], f.vm[:, :, :].rearrange("p n (h d) -> p (n h) d", d=P)))
            dve.wait_ge(cum_summed, 1)
            V(dve, nc.vector.tensor_copy(b[:, :], ps[:, 0, 0:UNITS]))
            V(dve, nc.vector.tensor_copy(bl[:, :], ps[:, 0, UNITS:2 * UNITS]))
            V(dve, nc.vector.tensor_copy(line[0:1, 0, :], ps[0:1, 3, 0:UNITS]))
            V(dve, nc.vector.tensor_copy(bT[:, :], ps[0:UNITS, 1, 0:P]))
            nc.vector.tensor_tensor(rT[:, :], ps[0:UNITS, 2, 0:P], bT[:, :], ALU.subtract).then_inc(r_ready, 1)
            dve.wait_ge(r_ready, 1)
            V(dve, nc.vector.tensor_reduce(mlT[:, :], rT[:, :], AX_X, ALU.max))
            nc.vector.tensor_tensor(mlT[:, :], mlT[:, :], bT[:, P - 1:P], ALU.add).then_inc(ml_ready, 1)
            dve.wait_ge(ml_turned, 1)
            V(dve, nc.vector.tensor_copy(line[0:1, 4, :], ps[0:1, 3, UNITS:2 * UNITS]))
            V(dve, nc.vector.memset(line[0:1, 1, 0:M_HEADS], 0.0))
            for n in range(CHUNKS):
                s = slice(n * M_HEADS, (n + 1) * M_HEADS)
                V(dve, nc.vector.tensor_tensor(line[0:1, 2, s], line[0:1, 0, s], line[0:1, 1, s], ALU.add))
                m_new = line[0:1, 1, (n + 1) * M_HEADS:(n + 2) * M_HEADS] if n < CHUNKS - 1 else line[0:1, 5, 0:M_HEADS]
                V(dve, nc.vector.tensor_tensor(m_new, line[0:1, 2, s], line[0:1, 4, s], ALU.max))
                V(dve, nc.vector.tensor_tensor(line[0:1, 2, s], line[0:1, 2, s], m_new, ALU.subtract))
                last = nc.vector.tensor_tensor(line[0:1, 3, s], line[0:1, 4, s], m_new, ALU.subtract)
                if n < CHUNKS - 1:
                    V(dve, last)
            last.then_inc(scan_ready, 1)
            dve.wait_ge(packed, 1)
            V(dve, nc.vector.tensor_copy(bcast[:, :, :].rearrange("p a u -> p (a u)"), ps[:, 3, 64:64 + 4 * UNITS]))
            V(dve, nc.vector.tensor_tensor(g[:, :], bl[:, :], b[:, :], ALU.subtract))
            V(dve, nc.vector.tensor_tensor(g[:, :], g[:, :], li[:, :], ALU.add))
            nc.vector.tensor_tensor(g[:, :], g[:, :], bcast[:, 3, :], ALU.subtract).then_inc(g_ready, 1)
            V(dve, nc.vector.tensor_tensor(inter[:, :], b[:, :], bcast[:, 0, :], ALU.add))
            dve.wait_ge(wts_ready, 1)
            kr = f.k_rows[:, :, :, :].rearrange("p n h d -> p (n h) d")
            nc.vector.tensor_tensor(kr, kr, over(wts[:, :]), ALU.mult).then_inc(kw_ready, 1)
            dve.wait_ge(rows_spread, 1)
            V(dve, nc.vector.tensor_tensor(dm[:, :, :], flat4(4), over(b[:, :]), ALU.add))
            V(dve, nc.vector.tensor_tensor(dm[:, :, :], dm[:, :, :],
                                           k.const("causal").unsqueeze(1).to_broadcast([P, UNITS, P]), ALU.add))
            V(dve, nc.vector.tensor_reduce(mt[:, :], dm[:, :, :], AX_X, ALU.max))
            V(dve, nc.vector.tensor_tensor(mt[:, :], mt[:, :], inter[:, :], ALU.max))
            V(dve, nc.vector.tensor_tensor(iw[:, :], inter[:, :], mt[:, :], ALU.subtract))
            nc.vector.tensor_tensor(dm[:, :, :], dm[:, :, :], over(mt[:, :]), ALU.subtract).then_inc(d_ready, 1)
            dve.wait_ge(carried, 1)
            for n in range(CHUNKS - 1):
                for h in range(M_HEADS):
                    u = n * M_HEADS + h
                    cc = ps[:, u // 3, (u % 3) * W1:(u % 3 + 1) * W1]
                    own = nc.vector.tensor_scalar(state[:, n, h, :], cc, bcast[:, 2, u:u + 1], None, ALU.mult)
                    if n == 0:
                        own.then_inc(state_ready, 1)
                        continue
                    V(dve, own)
                    if h == 0:
                        dve.wait_ge(state_ready, n * M_HEADS)
                    nc.vector.scalar_tensor_tensor(state[:, n, h, :], state[:, n - 1, h, :], bcast[:, 1, u:u + 1],
                                                   state[:, n, h, :], ALU.mult, ALU.add).then_inc(state_ready, 1)
            dve.wait_ge(d_exp, 1)
            dve.wait_ge(scored, 1)
            nc.vector.tensor_tensor(dm[:, :, :], flat4(4), dm[:, :, :], ALU.mult).then_inc(sd_ready, 1)
            dve.wait_ge(turned, 1)
            nc.vector.tensor_copy(sdT[:, :, :], flat4(0)).then_inc(sdT_ready, 1)
            for n in range(CHUNKS):
                dve.wait_ge(num_summed, n + 1)
                for h in range(M_HEADS):
                    u = n * M_HEADS + h
                    own = ps[:, 4 + h // 2, (h % 2) * W1:(h % 2 + 1) * W1]
                    ins = nc.vector.tensor_copy(num[:, u, :], own)
                    if n:
                        V(dve, ins)
                        past = ps[:, 6 + h // 2, (h % 2) * W1:(h % 2 + 1) * W1]
                        ins = nc.vector.scalar_tensor_tensor(num[:, u, :], past, iw[:, u:u + 1], num[:, u, :], ALU.mult, ALU.add)
                    if h < M_HEADS - 1:
                        V(dve, ins)
                ins.then_inc(num_taken, 1)
            dve.wait_ge(num_taken, CHUNKS)
            row_sum = num[:, :, P:W1].rearrange("p u o -> p (u o)")
            V(dve, nc.vector.scalar_tensor_tensor(den[:, :], row_sum, -1.0, row_sum, ALU.mult, ALU.max))
            V(dve, nc.vector.tensor_tensor(den[:, :], den[:, :], mt[:, :], ALU.max))
            V(dve, nc.vector.reciprocal(den[:, :], den[:, :]))
            hn = num[:, :, 0:P]
            V(dve, nc.vector.tensor_tensor(hn, hn, over(den[:, :]), ALU.mult))
            V(dve, nc.vector.tensor_tensor(tmp[:, :, 0:P], hn, hn, ALU.mult))
            V(dve, nc.vector.tensor_reduce(wts[:, :], tmp[:, :, 0:P], AX_X, ALU.add))
            nc.vector.tensor_scalar(wts[:, :], wts[:, :], 1.0 / P, EPS, ALU.mult, ALU.add).then_inc(rms_ready, 1)
            dve.wait_ge(rms_done, 1)
            newton(k, dve, g[:, :], wts[:, :], den[:, :])
            nc.vector.tensor_tensor(hn, hn, over(g[:, :]), ALU.mult).then_inc(h_ready, 1)
            for h in range(M_HEADS):
                dve.wait_ge(h_turned, h + 1)
                c = f.cT[:, h, :]
                V(dve, nc.vector.tensor_scalar(c, c, k.par("skip", h), None, ALU.mult))
                V(dve, nc.vector.scalar_tensor_tensor(c, ps[:, h, :], k.par("mh_g", h), c, ALU.mult, ALU.add))
                V(dve, nc.vector.tensor_tensor(f.mixT[:, h, :], c, f.pT[:, M_HEADS + h, :], ALU.mult))

        @block.scalar
        def _(act):
            act.wait_ge(gates_ready, 1)
            k.act(act, nc.scalar.activation(g[:, :], g[:, :], ACT.Exp))
            nc.scalar.activation(g[:, :], g[:, :], ACT.Ln, bias=1.0).then_inc(soft_ready, 1)
            act.wait_ge(scan_ready, 1)
            nc.scalar.activation(line[0:1, 2:4, :], line[0:1, 2:4, :], ACT.Exp).then_inc(scan_exp, 1)
            act.wait_ge(g_ready, 1)
            nc.scalar.activation(wts[:, :], g[:, :], ACT.Exp).then_inc(wts_ready, 1)
            act.wait_ge(d_ready, 1)
            k.act(act, nc.scalar.activation(iw[:, :], iw[:, :], ACT.Exp))
            k.act(act, nc.scalar.activation(mt[:, :], mt[:, :], ACT.Exp, scale=-1.0))
            nc.scalar.activation(dm[:, :, :], dm[:, :, :], ACT.Exp).then_inc(d_exp, 1)
            act.wait_ge(rms_ready, 1)
            k.act(act, nc.scalar.activation(g[:, :], wts[:, :], ACT.Ln))
            nc.scalar.activation(g[:, :], g[:, :], ACT.Exp, scale=-0.5).then_inc(rms_done, 1)

        @block.tensor
        def _(pe):
            pe.wait_ge(lf_ready, 1)
            nc.tensor.matmul(ps[:, 0, 0:UNITS], k.const("tri"), lf[:, :], start=True, stop=True)
            nc.tensor.matmul(ps[:, 0, UNITS:2 * UNITS], k.const("ones"), lf[:, :], start=True, stop=True)
            nc.tensor.matmul(ps[0:UNITS, 1, 0:P], lf[:, :], k.const("tri"), start=True, stop=True)
            nc.tensor.matmul(ps[0:1, 3, 0:UNITS], k.const("ones")[:, 0:1], lf[:, :], start=True, stop=True)
            nc.tensor.matmul(ps[0:UNITS, 2, 0:P], li[:, :], k.const("ident"), start=True, stop=True).then_inc(cum_summed, 1)
            pe.wait_ge(ml_ready, 1)
            nc.tensor.matmul(ps[0:1, 3, UNITS:2 * UNITS], mlT[:, :], k.const("ident", UNITS)[:, 0:UNITS], start=True, stop=True).then_inc(ml_turned, 1)
            pe.wait_ge(pick_in, 16)
            for u in range(UNITS):
                mm = nc.tensor.matmul(flat4(4)[:, u, :], pick[:, u, :], rT[:, :], start=True, stop=True)
            mm.then_inc(rows_spread, 1)
            pe.wait_ge(scan_exp, 1)
            nc.tensor.matmul(ps[:, 3, 64:64 + 4 * UNITS], k.const("ones", 1), line[0:1, 1:5, :], start=True, stop=True).then_inc(packed, 1)
            pe.wait_ge(kw_ready, 1)
            for u in range(UNITS - M_HEADS):
                mm = nc.tensor.matmul(ps[:, u // 3, (u % 3) * W1:(u % 3 + 1) * W1], f.k_rows[:, u // M_HEADS, u % M_HEADS, :],
                                      v_aug[:, u, :], start=True, stop=True)
            mm.then_inc(carried, 1)
            pe.wait_ge(d_ready, 1)
            for n in range(CHUNKS):
                s = slice(n * P, (n + 1) * P)
                for h in range(M_HEADS):
                    mm = nc.tensor.matmul(flat4(4)[:, n * M_HEADS + h, :], f.qT[:, h, s], f.kT[:, h, s], start=True, stop=True)
            mm.then_inc(scored, 1)
            pe.wait_ge(sd_ready, 1)
            pe.wait_ge(state_ready, (CHUNKS - 1) * M_HEADS)
            for u in range(UNITS):
                mm = nc.tensor.transpose(flat4(0)[:, u, :], dm[:, u, :], k.const("ident"))
            mm.then_inc(turned, 1)
            pe.wait_ge(sdT_ready, 1)
            for n in range(CHUNKS):
                if n:
                    pe.wait_ge(num_taken, n)
                for h in range(M_HEADS):
                    o = slice((h % 2) * W1, (h % 2 + 1) * W1)
                    mm = nc.tensor.matmul(ps[:, 4 + h // 2, o], sdT[:, n * M_HEADS + h, :], v_aug[:, n * M_HEADS + h, :], start=True, stop=True)
                    if n:
                        mm = nc.tensor.matmul(ps[:, 6 + h // 2, o], f.qT[:, h, n * P:(n + 1) * P], state[:, n - 1, h, :], start=True, stop=True)
                mm.then_inc(num_summed, 1)
            pe.wait_ge(h_ready, 1)
            for h in range(M_HEADS):
                for n in range(CHUNKS):
                    mm = nc.tensor.transpose(ps[:, h, n * P:(n + 1) * P], num[:, n * M_HEADS + h, 0:P], k.const("ident"))
                mm.then_inc(h_turned, 1)


HEADS_AT_ONCE = 32


def stage_head_norm(k, t, name, jobs, at, small_at, table=None):
    nc = k.nc
    H = HEADS_AT_ONCE
    n_jobs = len(jobs)
    n_sq = 2
    sq = k.place(f"{name}_sq", at, n_sq, TOK)
    spread = k.place(f"{name}_spread", at + n_sq * TOK, H // 2, P, dtype=FR, rows=H)
    v, y, u = (k.place(f"{name}_{x}", at + n_sq * TOK + H // 2 * P + i * TOK, TOK, rows=H) for i, x in enumerate(("v", "y", "u")))
    spread_in = k.place(f"{name}_spread_in", at + n_sq * TOK + H // 2 * P, H // 2, P, rows=H)
    y_high, y_low = (k.place(f"{name}_y_{x}", small_at + i * TOK, TOK, dtype=FR, rows=H) for i, x in enumerate(("high", "low")))
    counts = dict(spread_loaded=16, spread_ready=1, squared=n_jobs, summed=n_jobs, v_ready=1, y_ready=1, y_split=1, y_rounded=1, y_spread=n_jobs, scaled=n_jobs)
    sig = {x: k.shared("head_norm_" + x) for x in counts}
    wait = lambda eng, x, n: eng.wait_ge(sig[x].sem, sig[x].at(n))
    widest = max(jobs, key=lambda job: len(job[1]))[1]
    width = sum(n for _, n in widest)
    sum_of = lambda j: k.const("heads")[:, H - 2 - 2 * j:2 * H - 2 - 2 * j]
    bank = lambda j, i, n: k.psum[:, 2 + 2 * (j % 3) + i, 0:n]
    with k.nc.Block() as block:
        @block.sync
        def _(sp):
            sp.dma_start(spread_in[:, :, :], t["spread"].rearrange("h (j p) -> h j p", p=P)).then_inc(sig["spread_loaded"].sem, 16)
            if table:
                table.load(sp)

        @block.scalar
        def _(act):
            for j, (x, pieces, _) in enumerate(jobs):
                w = sum(n for _, n in pieces)
                if j >= n_sq:
                    wait(act, "summed", j - n_sq + 1)
                nc.scalar.activation(sq[:, j % n_sq, 0:w], x[:, 0:w], ACT.Square).then_inc(sig["squared"].sem, 1)
                if j == n_jobs // 2:
                    wait(act, "spread_loaded", 16)
                    nc.scalar.activation(spread[:, :, :], spread_in[:, :, :], ACT.Copy).then_inc(sig["spread_ready"].sem, 1)
            wait(act, "v_ready", 1)
            k.act(act, nc.scalar.activation(y[:, 0:width], v[:, 0:width], ACT.Ln))
            nc.scalar.activation(y[:, 0:width], y[:, 0:width], ACT.Exp, scale=-0.5).then_inc(sig["y_ready"].sem, 1)
            wait(act, "y_rounded", 1)
            nc.scalar.activation(y_high[:, 0:width], y[:, 0:width], ACT.Copy).then_inc(sig["y_split"].sem, 1)

        if table:
            @block.gpsimd
            def _(pool):
                table.gpsimd(pool)

        @block.tensor
        def _(pe):
            if table:
                table.tensor(pe)
            for j, (_, pieces, _) in enumerate(jobs):
                wait(pe, "squared", j + 1)
                for i, (t0, n) in enumerate(pieces):
                    with_piece = [m for m, job in enumerate(jobs) if len(job[1]) > i]
                    mm = nc.tensor.matmul(k.psum[0:H, i, 0:n], sum_of(j), sq[:, j % n_sq, t0:t0 + n], start=(j == with_piece[0]), stop=(j == with_piece[-1]))
                mm.then_inc(sig["summed"].sem, 1)
            wait(pe, "spread_ready", 1)
            wait(pe, "y_split", 2)
            for j, (_, pieces, _) in enumerate(jobs):
                if j >= 3:
                    wait(pe, "scaled", j - 2)
                for i, (t0, n) in enumerate(pieces):
                    nc.tensor.matmul(bank(j, i, n), spread[:, j, :], y_high[:, t0:t0 + n], start=True, stop=False)
                    mm = nc.tensor.matmul(bank(j, i, n), spread[:, j, :], y_low[:, t0:t0 + n], start=False, stop=True)
                mm.then_inc(sig["y_spread"].sem, 1)

        @block.vector
        def _(dve):
            if table:
                table.vector_first(dve)
            wait(dve, "summed", n_jobs)
            wait(dve, "spread_ready", 1)
            for i, (t0, n) in enumerate(widest):
                ins = nc.vector.tensor_scalar(v[:, t0:t0 + n], k.psum[0:H, i, 0:n], 1.0 / HEAD, EPS, ALU.mult, ALU.add)
            ins.then_inc(sig["v_ready"].sem, 1)
            wait(dve, "y_ready", 1)
            newton(k, dve, y[:, 0:width], v[:, 0:width], u[:, 0:width])
            dve.sem_inc(sig["y_rounded"].sem, 1)
            wait(dve, "y_split", 1)
            nc.vector.tensor_tensor(y_low[:, 0:width], y[:, 0:width], y_high[:, 0:width].bitcast(F32), ALU.subtract).then_inc(sig["y_split"].sem, 1)
            for j, (x, pieces, gain) in enumerate(jobs):
                wait(dve, "y_spread", j + 1)
                for i, (t0, n) in enumerate(pieces):
                    o = x[:, t0:t0 + n]
                    ins = nc.vector.scalar_tensor_tensor(o, o, gain, bank(j, i, n), ALU.mult, ALU.mult)
                ins.then_inc(sig["scaled"].sem, 1)
            if table:
                table.vector_last(dve)
    counts["y_split"] = 2
    for x, n in counts.items():
        sig[x].base += n


class DilatedTable:
    LENGTH = SEQ + P

    def __init__(self, k, t, tab, at):
        self.k, self.nc, self.t, self.tab = k, k.nc, t, tab
        z = self.LENGTH
        self.rel = k.place("rel_bias", at, DIL_HEADS, rows=N_BUCKETS + 1)
        self.spread = k.place("rel_spread", at + 16, DIL_HEADS, P, rows=N_BUCKETS + 1)
        self.hot = k.place("bucket_hot", at + 16 + DIL_HEADS * P, z, rows=N_BUCKETS + 1)
        self.line = k.place("bias_line", at + 16 + DIL_HEADS * P + z, DIL_HEADS, z)
        self.tables_in, self.spread_ready, self.line_summed, self.line_ready, self.skew_out, self.skew_in = (k.sem("dil_" + s) for s in (
            "tables_in", "spread_ready", "line_summed", "line_ready", "skew_out", "skew_in"))
        self.skew = self.nc.dram_tensor("skew", (DIL_HEADS, P, z), F32)
        self.steps = [(h, z0, n, 6 + i) for h in range(DIL_HEADS) for i, (z0, n) in enumerate(((0, SEQ), (SEQ, P)))]

    def load(self, sp):
        z = self.LENGTH
        sp.dma_start(self.rel[0:N_BUCKETS, :], self.t["rel_bias"]).then_inc(self.tables_in, 16)
        sp.dma_start(self.hot[:, :], self.t["bucket_hot"]).then_inc(self.tables_in, 16)
        for h in range(DIL_HEADS):
            sp.wait_ge(self.line_ready, 2 * h + 2)
            sp.dma_start(self.skew.ap()[h], self.line[:, h, :]).then_inc(self.skew_out, 16)
        sp.wait_ge(self.skew_out, 16 * DIL_HEADS)
        for h in range(DIL_HEADS):
            back = bass.AP(self.skew, h * P * z + P - 1, [[z - 1, P], [1, SEQ]])
            sp.dma_start(self.tab[:, h, :], back).then_inc(self.skew_in, 16)
        sp.wait_ge(self.skew_in, 16 * DIL_HEADS)

    def gpsimd(self, pool):
        pass

    def tensor(self, pe):
        pe.wait_ge(self.spread_ready, 1)
        for j, (h, z0, n, bank) in enumerate(self.steps):
            if j >= 2:
                pe.wait_ge(self.line_ready, j - 1)
            self.nc.tensor.matmul(self.k.psum[:, bank, 0:n], self.spread[:, h, :], self.hot[:, z0:z0 + n], start=True, stop=True
                                  ).then_inc(self.line_summed, 1)
        pe.wait_ge(self.line_ready, len(self.steps))

    def vector_first(self, dve):
        k, nc = self.k, self.nc
        dve.wait_ge(self.tables_in, 32)
        k.dve(dve, nc.vector.memset(self.spread[N_BUCKETS:N_BUCKETS + 1, :, :], 1.0))
        nc.vector.tensor_copy(self.spread[0:N_BUCKETS, :, :], self.rel[0:N_BUCKETS, :].unsqueeze(2).to_broadcast([N_BUCKETS, DIL_HEADS, P])
                              ).then_inc(self.spread_ready, 1)
        for j, (h, z0, n, bank) in enumerate(self.steps):
            dve.wait_ge(self.line_summed, j + 1)
            nc.vector.tensor_copy(self.line[:, h, z0:z0 + n], k.psum[:, bank, 0:n]).then_inc(self.line_ready, 1)

    def vector_last(self, dve):
        pass


def stage_attention(k, name, groups, units, stages, out, at, stat_at, sink=None):
    nc = k.nc
    V = k.dve
    units = [units(s) for s in range(2)]
    n_group = len(units[0])
    n_units = 2 * n_group
    units = units[0] + units[1]
    n_sc = 3 if n_units % 3 == 0 else 4
    sc = k.place(f"{name}_scores", at, n_sc, TOK)
    pT = k.place(f"{name}_probsT", at + n_sc * TOK, 2, TOK)
    stat = k.place(f"{name}_stat", stat_at, 2 * n_sc)
    staged, scored, reduced, exped, normed, turned, copied, summed, stored = (k.shared(f"attention_{s}") for s in (
        "staged", "scored", "reduced", "exped", "normed", "turned", "copied", "summed", "stored"))
    passes = groups // 2
    n_stages = len(stages(0, 0))
    n_out = len(out(0))
    scale = HEAD ** -0.5
    unit = lambda u: units[u % n_units]
    keys = lambda u: sum(n for _, n in unit(u)[1])
    nm = lambda b: stat[:, b:b + 1]
    den = lambda b: stat[:, n_sc + b:n_sc + b + 1]
    columns = lambda u: keys(u) + (sink is not None)

    def all_passes(eng, run):
        if passes > 1:
            with eng.Fori(0, passes - 1) as it:
                run(it, False)
        run(passes - 1, True)

    with nc.Block() as block:
        @block.gpsimd
        def _(pool):
            with pool.Fori(0, passes) as it:
                for s in range(2):
                    pool.wait_ge(summed.sem, summed.at(it * n_units + (s + 1) * n_group))
                    for to, source in stages(it * 2 + s, s):
                        nc.gpsimd.tensor_copy(to, source).then_inc(staged.sem, 1)

        @block.tensor
        def _(pe):
            pe.sem_inc(turned.sem, n_sc)
            pe.sem_inc(summed.sem, n_units)

            def score(it, u):
                if u % n_group == 0:
                    pe.wait_ge(staged.sem, staged.at(it * (2 * n_stages) + (u // n_group + 1) * n_stages))
                pe.wait_ge(reduced.sem, reduced.at(it * n_units + (u + 1)))
                for i, (kk, n) in enumerate(unit(u)[1]):
                    mm = nc.tensor.matmul(k.psum[:, (u % 2) * 2 + i, 0:n], unit(u)[0], kk, start=True, stop=True)
                mm.then_inc(scored.sem, 1)

            def multiply(it, u):
                _, _, _, values, o = unit(u)
                pe.wait_ge(copied.sem, copied.at(it * n_units + (u + 2)))
                if u % n_group == 0:
                    pe.wait_ge(stored.sem, stored.at(it * (2 * n_out) + (u // n_group + 1) * n_out))
                tiles = keys(u) // P
                for j in range(tiles):
                    mm = nc.tensor.matmul(o, values(j), pT[:, u % 2, j * P:(j + 1) * P], start=(j == 0), stop=(j == tiles - 1))
                mm.then_inc(summed.sem, 1)

            def run(it, last):
                for u in range(n_units):
                    pe.wait_ge(normed.sem, normed.at(it * n_units + (u + 1)))
                    pe.wait_ge(copied.sem, copied.at(it * n_units + (u + 1)))
                    for j in range(keys(u) // P):
                        mm = nc.tensor.transpose(k.psum[:, 4 + j // 4, (j % 4) * P:(j % 4 + 1) * P], sc[:, u % n_sc, j * P:(j + 1) * P], k.const("ident"))
                    mm.then_inc(turned.sem, 1)
                    if u + 3 < n_units or not last:
                        score(it, u + 3)
                    if u:
                        multiply(it, u - 1)
                multiply(it, n_units - 1)

            for u in range(3):
                score(0, u)
            all_passes(pe, run)

        @block.vector
        def _(dve):
            dve.sem_inc(reduced.sem, 2)

            def gather(it, u):
                b = u % n_units % n_sc
                dve.wait_ge(scored.sem, scored.at(it * n_units + (u + 1)))
                dve.wait_ge(turned.sem, turned.at(it * n_units + (u + 1)))
                at_key = 0
                if sink is not None:
                    nc.vector.tensor_copy(sc[:, b, keys(u):columns(u)], sink(u % n_units))
                for i, (_, n) in enumerate(unit(u)[1]):
                    o, s = sc[:, b, at_key:at_key + n], k.psum[:, u % 2 * 2 + i, 0:n]
                    if i == 0 and unit(u)[2] is not None:
                        ins = nc.vector.scalar_tensor_tensor(o, s, scale, unit(u)[2](it * 2 + u // n_group), ALU.mult, ALU.add)
                    else:
                        ins = nc.vector.tensor_scalar(o, s, scale, None, ALU.mult)
                    at_key += n
                V(dve, ins)
                nc.vector.tensor_reduce(nm(b), sc[:, b, 0:columns(u)], AX_X, ALU.max, negate=True).then_inc(reduced.sem, 1)

            def norm(it, u):
                b = u % n_sc
                dve.wait_ge(exped.sem, exped.at(it * n_units + (u + 1)))
                V(dve, nc.vector.reciprocal(den(b), den(b)))
                p = sc[:, b, 0:keys(u)]
                nc.vector.tensor_scalar(p, p, den(b), None, ALU.mult).then_inc(normed.sem, 1)

            def run(it, last):
                V.restart(dve)
                for u in range(n_units):
                    norm(it, u)
                    if u + 2 < n_units or not last:
                        gather(it, u + 2)

            V.restart(dve)
            gather(0, 0)
            gather(0, 1)
            all_passes(dve, run)

        @block.scalar
        def _(act):
            act.sem_inc(copied.sem, 1)
            act.sem_inc(stored.sem, n_out)

            def exp(it, u):
                b = u % n_units % n_sc
                act.wait_ge(reduced.sem, reduced.at(it * n_units + (u + 3)))
                p = sc[:, b, 0:columns(u)]
                nc.scalar.activation(p, p, ACT.Exp, bias=nm(b), accum_out=den(b)).then_inc(exped.sem, 1)

            def store(it, s):
                act.wait_ge(summed.sem, summed.at(it * n_units + (n_units + (s + 1) * n_group)))
                for to, source in out(it * 2 + s):
                    nc.scalar.activation(to, source, ACT.Copy).then_inc(stored.sem, 1)

            def run(it, last):
                for u in range(n_units):
                    act.wait_ge(turned.sem, turned.at(it * n_units + (u + 1 + n_sc)))
                    act.wait_ge(summed.sem, summed.at(it * n_units + (n_units + u - 1)))
                    n = keys(u)
                    nc.scalar.activation(pT[:, u % 2, 0:n], k.psum[:, 4:6, :].rearrange("p b n -> p (b n)")[:, 0:n], ACT.Copy).then_inc(copied.sem, 1)
                    if u + 2 < n_units or not last:
                        exp(it, u + 2)
                    if u == n_group:
                        store(it, 0)
                store(it, 1)

            exp(0, 0)
            exp(0, 1)
            all_passes(act, run)
    for s in (scored, exped, normed):
        s.base += passes * n_units
    for s, grant in ((reduced, 2), (turned, n_sc), (summed, n_units), (copied, 1)):
        s.base += passes * n_units + grant
    staged.base += groups * n_stages
    stored.base += (groups + 1) * n_out


def stage_dilated(k, t, f):
    tab = k.place("dil_tab", 28800, DIL_HEADS, SEQ)
    q, key = f.pT[:, 8:12, :], f.pT[:, 12:16, :]
    stage_head_norm(k, t, "dil_norm", [(f.pT[:, c, :], LATENT, k.par("qn_g" if c < 12 else "kn_g", c % 4)) for c in range(8, 16)], 40000, 46000,
                    DilatedTable(k, t, tab, 32896))
    sets = [[k.place(f"dil_{s}{i}", 33000 + (i * 3 + j) * SEQ, SEQ) for j, s in enumerate(("qs", "ks", "vs"))] for i in range(2)]
    by_tile = lambda vs: vs[:, :].rearrange("p (t d) -> p t d", d=P)

    def units(s):
        qs, ks, vs = sets[s]
        made = []
        for half in range(2):
            h = slice(half * HEAD, (half + 1) * HEAD)
            for i in range(TILES):
                n = (i + 1) * P
                made.append((qs[h, i * P:(i + 1) * P], [(ks[h, 0:n], n)],
                             lambda g, half=half, i=i, n=n: one(tab, g * 2 + half, (3 - i) * P, n),
                             lambda j, h=h, v=by_tile(vs): v[:, j, h], k.psum[h, 6, i * P:(i + 1) * P]))
        return made

    def stages(g, s):
        qs, ks, vs = sets[s]
        return [(qs[:, :], one(f.pT, g + 8, 0, SEQ)), (ks[:, :], one(f.pT, g + 12, 0, SEQ)), (by_tile(vs), f.va[:, :, bass.ds(g * P, P)])]

    stage_attention(k, "dil", DIL_HEADS // 2, units, stages, lambda g: [(one(f.mixT, g + 4, 0, SEQ), k.psum[:, 6, :])], 37000, PICKS_AT)


def add_to_x(k, gate, pieces, per=RING):
    def epilogue(dve, it, r, banks):
        for i, ((t0, n), bank) in enumerate(zip(pieces, banks)):
            x = k.xT[:, bass.ds(it * per + r, 1), t0:t0 + n].rearrange("p o y -> p (o y)")
            k.nc.vector.scalar_tensor_tensor(x, bank, gate(it * per + r, i), x, ALU.mult, ALU.add).then_inc(k.bank_read.sem, 1)
    return epilogue


def copy_to(k, place, pieces):
    def epilogue(dve, it, r, banks):
        for i, bank in enumerate(banks):
            k.nc.vector.tensor_copy(place(it, r, i), bank).then_inc(k.bank_read.sem, 1)
    return epilogue


def one(buf, c, t0, n):
    return buf[:, bass.ds(c, 1), t0:t0 + n].rearrange("p o y -> p (o y)")


LATENT = ((0, SEQ),)


def first_block(k, t, upto=99):
    f = First(k)
    with k.nc.Block() as block:
        product(k, block, t["w_projT"], 16, KD, LATENT, k.h_high, k.h_low, 28800,
                copy_to(k, lambda it, r, i: one(f.pT, it * RING + r, 0, SEQ), LATENT),
                norm=Norm(k, LATENT, lambda i, c: k.par("norm1_g", c)))
    targets = ((f.vm, 0), (f.va, BANK), (f.gates, 2 * BANK), (None, 2 * BANK + 2 * M_HEADS))
    width = targets[-1][1] // 3

    def parts(b, i):
        for (place, at), (_, end) in zip(targets, targets[1:]):
            lo, hi = max(at, b * width), min(end, (b + 1) * width)
            if lo < hi:
                yield place[:, i, lo - at:hi - at], lo - b * width, hi - lo

    stage_rows(k, t["w_projV"], 3, width, TILES, parts, 28800)
    stage_conv(k, t, f)
    stage_mlstm(k, t, f)
    stage_dilated(k, t, f)
    with k.nc.Block() as block:
        high, low = k.place("mix_high", BIG, KD, SEQ, dtype=FR), k.place("mix_low", BIG + KD * SEQ, KD, SEQ, dtype=FR)
        product(k, block, t["w_out"], KD, KD, LATENT, high, low, BIG + 2 * KD * SEQ, add_to_x(k, lambda c, i: 1.0, LATENT), full=f.mixT)
    return f


class Peer:

    def __init__(self, k):
        self.qT = k.place("peer_qT", BIG, 2 * PEER_HEADS, SEQ)
        self.picks = k.place("picks", PICKS_AT, 3, SEQ)
        self.gelu = k.nc.dram_tensor("gelu_dram", (N_KEYS, N_KEYS, SEQ), F32).ap()
        self.gates = k.nc.dram_tensor("gates_dram", (N_KEYS, N_KEYS, SEQ), F32).ap()


MOD_RING = 4
EIGHT = range(8)


def stage_pick(k, t, f):
    nc = k.nc
    V = k.dve
    H2 = 2 * PEER_HEADS
    at = BIG + H2 * SEQ

    def take(name, *shape, dtype=F32):
        nonlocal at
        b = k.place("pick_" + name, at, *shape, dtype=dtype)
        at += int(np.prod(shape))
        return b

    keys = take("keys", H2, N_KEYS)
    qs = take("qs", H2, P)
    rest = take("rest", N_KEYS)
    best = take("best", H2, TOPK)
    best_at = take("best_at", H2, TOPK, dtype=U32)
    best_f = take("best_f", H2, TOPK)
    cand = take("cand", TOPK, TOPK)
    cand_rest = take("cand_rest", TOPK * TOPK)
    top = take("top", PEER_HEADS, TOPK)
    top_at = take("top_at", PEER_HEADS, TOPK, dtype=U32)
    half_at = [take(f"half_at{i}", PICKS, dtype=U32) for i in range(2)]
    half_f = [take(f"half_f{i}", PICKS) for i in range(2)]
    equal = take("equal", PICKS // 2, TOPK)
    out = [take(f"out{i}", PICKS) for i in range(3)]
    total = take("total", PEER_HEADS)
    share = LAYERS * MODS // TILES
    cond = take("cond", 2, D)
    w_mod = [take(f"w_mod{r}", D) for r in range(MOD_RING)]
    mod_sum = take("mod_sum", share, 2)
    u_raw, u_high, u_low = ([take(f"u_{x}{r}", KD, N_KEYS, dtype=d) for r in range(2)] for x, d in (("raw", F32), ("high", FR), ("low", FR)))
    gelu = [take(f"gelu{r}", SEQ) for r in range(2)]
    products = k.place("pick_products", at, D, dtype=mybir.dt.bfloat16)
    assert at + D // 2 <= H_LOW, at
    scores = k.psum[:, 0:4, :].rearrange("p b (h n) -> p (b h) n", n=N_KEYS)
    (keys_in, cond_in, cond_ready, staged, scored, shifted, exped, picked, turned, stored, mod_used, u_high_ready, u_split, pre_done, gelu_done) = (
        k.sem("pick_" + x) for x in ("keys_in", "cond_in", "cond_ready", "staged", "scored", "shifted", "exped", "picked", "turned", "stored",
                                     "mod_used", "u_high_ready", "u_split", "pre_done", "gelu_done"))
    u_in, gelu_out = ([k.sem(f"pick_{x}{r}") for r in range(2)] for x in ("u_in", "gelu_out"))
    w_mod_in = [k.sem(f"pick_w_mod_in{r}") for r in range(MOD_RING)]
    per_tile = N_KEYS // TILES
    inner = per_tile // 8 - 1
    assert share == inner * 8

    def loop_eights(eng, it, eight):
        with eng.Fori(0, inner) as jt:
            eight(it * per_tile + jt * 8, jt)
        eight(it * per_tile + inner * 8, None)

    with nc.Block() as block:
        @block.sync
        def _(sp):
            sp.dma_start(keys[:, :, :], t["keys"].rearrange("p (h n) -> p h n", n=N_KEYS)).then_inc(keys_in, 16)
            sp.dma_start(cond[:, :, :], t["cond"].rearrange("p (c d) -> p c d", d=D)).then_inc(cond_in, 16)
            for r in range(2):
                sp.sem_inc(gelu_out[r], 16)
            sp.sem_inc(scored, 1)
            with sp.Fori(0, TILES) as it:
                sp.wait_ge(scored, it + 1)
                sp.dma_start(qs[:, :, :], f.qT[:, :, bass.ds(it * P, P)]).then_inc(staged, 16)

                def eight(c0, jt):
                    for r in EIGHT:
                        sp.wait_ge(u_split, c0 + (r + 1))
                        sp.dma_start(u_raw[r % 2][:, :, :], t["expert_uT"][c0 + r].rearrange("p (k e) -> p k e", e=N_KEYS)).then_inc(u_in[r % 2], 16)
                        if jt is not None:
                            j = it * share + jt * 8 + r
                            sp.wait_ge(mod_used, j + 1)
                            sp.dma_start(w_mod[r % MOD_RING][:, :], t["w_mod"][j]).then_inc(w_mod_in[r % MOD_RING], 16)

                loop_eights(sp, it, eight)
            for r in range(2):
                sp.wait_ge(gelu_out[r], 16 + 16 * (N_KEYS // 2))

        @block.gpsimd
        def _(pool):
            pool.sem_inc(u_split, 2)
            with pool.Fori(0, TILES) as it:
                def eight(c0, jt):
                    for r in EIGHT:
                        pool.wait_ge(u_high_ready, c0 + (r + 1))
                        nc.gpsimd.tensor_tensor(u_low[r % 2][:, :, :], u_raw[r % 2][:, :, :], u_high[r % 2][:, :, :].bitcast(F32), ALU.subtract
                                                ).then_inc(u_split, 1)

                loop_eights(pool, it, eight)

        @block.tensor
        def _(pe):
            pe.wait_ge(keys_in, 16)
            pe.sem_inc(pre_done, 2)
            with pe.Fori(0, TILES) as it:
                pe.wait_ge(staged, it * 16 + 16)
                pe.wait_ge(stored, it + 1)
                for i in range(H2):
                    mm = nc.tensor.matmul(scores[:, i, :], qs[:, i, :], keys[:, i, :], start=True, stop=True)
                mm.then_inc(scored, 1)

                def eight(c0, jt):
                    for r in EIGHT:
                        pe.wait_ge(u_split, c0 + (2 + r + 1))
                        pe.wait_ge(gelu_done, c0 + (r + 1))
                        for c in range(KD):
                            mm = split_product(nc, k.psum[:, 5 + r % 2, :], u_high[r % 2][:, c, :], u_low[r % 2][:, c, :],
                                               k.h_high[:, c, 0:SEQ], k.h_low[:, c, 0:SEQ], c == 0, c == KD - 1)
                        mm.then_inc(pre_done, 1)

                loop_eights(pe, it, eight)
                pe.wait_ge(picked, it + 1)
                for i in range(3):
                    mm = nc.tensor.transpose(k.psum[:, 4, i * P:(i + 1) * P], out[i][:, :], k.const("ident"))
                mm.then_inc(turned, 1)

        @block.scalar
        def _(act):
            act.wait_ge(cond_in, 16)
            nc.scalar.activation(cond[:, :, :], cond[:, :, :], ACT.Silu).then_inc(cond_ready, 1)
            act.sem_inc(gelu_done, 2)

            def round_u(c0, r):
                act.wait_ge(u_in[r % 2], c0 * 8 + 16 * (r // 2 + 1))
                if not (isinstance(c0, int) and c0 + r < 2):
                    act.wait_ge(pre_done, c0 + (r + 1))
                nc.scalar.activation(u_high[r % 2][:, :, :], u_raw[r % 2][:, :, :], ACT.Copy).then_inc(u_high_ready, 1)

            def tile(it, last):
                def eight(c0, jt):
                    for r in EIGHT:
                        if not (last and jt is None and r >= 6):
                            round_u(c0, r + 2)
                        act.wait_ge(pre_done, c0 + (2 + r + 1))
                        act.wait_ge(gelu_out[r % 2], c0 * 8 + 16 * (r // 2 + 1))
                        nc.scalar.activation(gelu[r % 2][:, :], k.psum[:, 5 + r % 2, :], ACT.Gelu).then_inc(gelu_done, 1)
                        act.wait_ge(gelu_done, c0 + (2 + r + 1))
                        act.dma_start(f.gelu[c0 + r], gelu[r % 2][:, :]).then_inc(gelu_out[r % 2], 16)
                        if jt is None and r == 5:
                            act.wait_ge(shifted, it + 1)
                            nc.scalar.activation(out[2][:, :], out[2][:, :], ACT.Exp).then_inc(exped, 1)

                loop_eights(act, it, eight)

            round_u(0, 0)
            round_u(0, 1)
            with act.Fori(0, TILES - 1) as it:
                tile(it, False)
            tile(TILES - 1, True)

        @block.vector
        def _(dve):
            dve.sem_inc(stored, 1)
            dve.sem_inc(mod_used, MOD_RING)
            dve.wait_ge(cond_ready, 1)
            with dve.Fori(0, TILES) as it:
                V.restart(dve)

                def modulate(j):
                    dve.wait_ge(w_mod_in[j % MOD_RING], it * (16 * share // MOD_RING) + 16 * (j // MOD_RING + 1))
                    dve.wait_ge(mod_used, it * share + (MOD_RING + j))
                    for c in range(2):
                        ins = nc.vector.scalar_tensor_tensor(products[:, :], w_mod[j % MOD_RING][:, :], 1.0, cond[:, c, :], ALU.mult, ALU.mult,
                                                             accum_out=mod_sum[:, j, c:c + 1])
                        if c == 0:
                            V(dve, ins)
                    ins.then_inc(mod_used, 1)

                def best16(values, left, best, where):
                    V(dve, nc.vector.max(best[:, 0:8], values))
                    V(dve, nc.vector.max_index(where[:, 0:8], best[:, 0:8], values))
                    V(dve, nc.vector.match_replace(left, best[:, 0:8], values, -3e38))
                    V(dve, nc.vector.max(best[:, 8:16], left))
                    V(dve, nc.vector.max_index(where[:, 8:16], best[:, 8:16], left))

                dve.wait_ge(scored, it + 2)
                for i in range(H2):
                    modulate(i)
                    best16(scores[:, i, :], rest[:, :], best[:, i, :], best_at[:, i, :])
                for h in range(PEER_HEADS):
                    modulate(H2 + h)
                    first = best[:, 2 * h, :].unsqueeze(2).to_broadcast([P, TOPK, TOPK])
                    second = best[:, 2 * h + 1, :].unsqueeze(1).to_broadcast([P, TOPK, TOPK])
                    V(dve, nc.vector.tensor_tensor(cand[:, :, :], first, second, ALU.add))
                    best16(cand[:, :, :].rearrange("p a b -> p (a b)"), cand_rest[:, :], top[:, h, :], top_at[:, h, :])
                weight = out[2][:, :].rearrange("p (h s) -> p h s", s=TOPK)
                nc.vector.tensor_tensor(weight, top[:, :, :], top[:, :, 0:1].to_broadcast([P, PEER_HEADS, TOPK]), ALU.subtract).then_inc(shifted, 1)
                where = top_at[:, :, :].rearrange("p h s -> p (h s)")
                V(dve, nc.vector.tensor_scalar(half_at[0][:, :], where, 4, None, ALU.logical_shift_right))
                V(dve, nc.vector.tensor_scalar(half_at[1][:, :], where, TOPK - 1, None, ALU.bitwise_and))
                V(dve, nc.vector.tensor_copy(best_f[:, :, :], best_at[:, :, :]))
                for i in range(2):
                    V(dve, nc.vector.tensor_copy(half_f[i][:, :], half_at[i][:, :]))
                heads = PEER_HEADS // 2
                for i in range(2):
                    for part in range(2):
                        p = slice(part * PICKS // 2, (part + 1) * PICKS // 2)
                        V(dve, nc.vector.tensor_tensor(equal[:, :, :], half_f[i][:, p].unsqueeze(2).to_broadcast([P, PICKS // 2, TOPK]),
                                                       k.const("iota16").unsqueeze(1).to_broadcast([P, PICKS // 2, TOPK]), ALU.is_equal))
                        eq = equal[:, :, :].rearrange("p (h s) a -> p h s a", s=TOPK)
                        number = best_f[:, :, :].rearrange("p (h i) a -> p h i a", i=2)[:, part * heads:(part + 1) * heads, i, :]
                        V(dve, nc.vector.tensor_tensor(eq, eq, number.unsqueeze(2).to_broadcast([P, heads, TOPK, TOPK]), ALU.mult))
                        V(dve, nc.vector.tensor_reduce(out[i][:, p], equal[:, :, :], AX_X, ALU.add))
                b = k.par("b_mod", it * share, share).unsqueeze(2).to_broadcast([P, share, 2])
                V(dve, nc.vector.tensor_tensor(k.modT[:, bass.ds(it * share, share), :], mod_sum[:, :, :], b, ALU.add))
                dve.wait_ge(exped, it + 1)
                V(dve, nc.vector.tensor_reduce(total[:, :], weight, AX_X, ALU.add))
                V(dve, nc.vector.reciprocal(total[:, :], total[:, :]))
                nc.vector.tensor_tensor(weight, weight, total[:, :].unsqueeze(2).to_broadcast([P, PEER_HEADS, TOPK]), ALU.mult).then_inc(picked, 1)
                dve.wait_ge(turned, it + 1)
                nc.vector.tensor_copy(f.picks[:, :, bass.ds(it * P, P)], k.psum[:, 4, 0:3 * P].rearrange("p (i n) -> p i n", n=P)).then_inc(stored, 1)
            for layer in range(LAYERS):
                for which in (1, 4):
                    j = layer * MODS + which * KD
                    V(dve, nc.vector.tensor_scalar(k.modT[:, j:j + KD, :], k.modT[:, j:j + KD, :], 1.0, None, ALU.add))


GATE_TOK = 128
GROUP = 8


def stage_gates(k, f):
    nc = k.nc
    hot1 = k.place("hot1", H_HIGH, 2, GROUP, N_KEYS)
    hot2 = k.place("hot2", H_HIGH + 2 * GROUP * N_KEYS, 2, GROUP, N_KEYS)
    plane = k.place("gate_plane", H_HIGH + 4 * GROUP * N_KEYS, 2, N_KEYS, GATE_TOK)
    groups = GATE_TOK // GROUP
    hot1_ready, same, pool_gated, scalar_gated, summed, taken = (
        k.sem("gates_" + x) for x in ("hot1_ready", "same", "pool_gated", "scalar_gated", "summed", "taken"))
    stored = [k.sem(f"gates_stored{b}") for b in range(2)]
    times = SEQ // (2 * GATE_TOK)
    n_body = 2 * groups
    by_pool = 5
    own = k.place("gate_own", H_HIGH + 4 * GROUP * N_KEYS + 2 * N_KEYS * GATE_TOK, 2, GROUP)
    iota = k.const("iota").unsqueeze(1)

    def tokens(it, g):
        return bass.ds(it * (2 * GATE_TOK) + g * GROUP, GROUP)

    with nc.Block() as block:
        @block.vector
        def _(dve):
            dve.sem_inc(summed, 2)
            with dve.Fori(0, times) as it:
                for g in range(n_body):
                    b = g % 2
                    dve.wait_ge(summed, it * n_body + (g + 1))
                    for i, (hot, ready) in enumerate(((hot2, same), (hot1, hot1_ready))):
                        pick = f.picks[:, 1 - i, tokens(it, g)].unsqueeze(2).to_broadcast([P, GROUP, N_KEYS])
                        nc.vector.tensor_tensor(hot[:, b, :, :], pick, iota.to_broadcast([P, GROUP, N_KEYS]), ALU.is_equal).then_inc(ready, 1)

        @block.gpsimd
        def _(pool):
            with pool.Fori(0, times) as it:
                for g in range(n_body):
                    rows = hot2[:, g % 2, 0:by_pool, :]
                    pool.wait_ge(same, it * n_body + (g + 1))
                    gate = f.picks[:, 2, bass.ds(it * (2 * GATE_TOK) + g * GROUP, by_pool)].unsqueeze(2).to_broadcast([P, by_pool, N_KEYS])
                    nc.gpsimd.tensor_tensor(rows, rows, gate, ALU.mult).then_inc(pool_gated, 1)

        @block.tensor
        def _(pe):
            with pe.Fori(0, times) as it:
                for g in range(n_body):
                    pe.wait_ge(hot1_ready, it * n_body + (g + 1))
                    pe.wait_ge(pool_gated, it * n_body + (g + 1))
                    pe.wait_ge(scalar_gated, it * n_body + (g + 1))
                    pe.wait_ge(taken, it * n_body + (g + 1))
                    for j in range(GROUP):
                        mm = nc.tensor.matmul(k.psum[:, 2 * (g % 4) + j // 4, (j % 4) * P:(j % 4 + 1) * P], hot1[:, g % 2, j, :], hot2[:, g % 2, j, :],
                                              start=True, stop=True)
                    mm.then_inc(summed, 1)

        @block.scalar
        def _(act):
            act.sem_inc(taken, 4)
            with act.Fori(0, times) as it:
                k.act.restart(act)

                def gate(g):
                    act.wait_ge(same, it * n_body + (g + 1))
                    k.act(act, nc.scalar.activation(own[:, g % 2, :], f.picks[:, 2, tokens(it, g)], ACT.Copy))
                    for j in range(by_pool, GROUP):
                        row = hot2[:, g % 2, j, :]
                        ins = nc.scalar.activation(row, row, ACT.Copy, scale=own[:, g % 2, j:j + 1])
                    ins.then_inc(scalar_gated, 1)

                def take(g):
                    b = g // groups
                    act.wait_ge(summed, it * n_body + (g + 3))
                    if g % groups == 0:
                        act.wait_ge(stored[b], it * 16 + 16)
                    o = plane[:, b, :, (g % groups) * GROUP:(g % groups + 1) * GROUP].rearrange("p e t -> p t e")
                    nc.scalar.activation(o, k.psum[:, 2 * (g % 4):2 * (g % 4) + 2, :].rearrange("p b (t e) -> p (b t) e", e=N_KEYS), ACT.Copy).then_inc(taken, 1)

                gate(0)
                for g in range(n_body):
                    if g + 1 < n_body:
                        gate(g + 1)
                    take(g)

        @block.sync
        def _(sp):
            for b in range(2):
                sp.sem_inc(stored[b], 16)
            with sp.Fori(0, times) as it:
                for b in range(2):
                    sp.wait_ge(taken, it * n_body + (4 + (b + 1) * groups))
                    o = f.gates.rearrange("c e t -> e c t")[:, :, bass.ds(it * (2 * GATE_TOK) + b * GATE_TOK, GATE_TOK)]
                    sp.dma_start(o, plane[:, b, :, :]).then_inc(stored[b], 16)
            for b in range(2):
                sp.wait_ge(stored[b], 16 + times * 16)


def stage_values(k, t, f):
    nc = k.nc
    pair, quads = 2, 4
    at = BIG

    def take(name, n, *shape, dtype=F32):
        nonlocal at
        size = int(np.prod(shape))
        at += n * size
        return [k.place(f"{name}{r}", at + (r - n) * size, *shape, dtype=dtype) for r in range(n)]

    v_raw, g_slot, p_slot = take("v_raw", 4, D), take("g", 4, SEQ), take("p", 4, SEQ)
    v_high, v_low = take("v_high", 4, D, dtype=FR), take("v_low", 4, D, dtype=FR)
    a_full, a_high, a_low = take("a_full", 4, SEQ), take("a_high", 4, SEQ, dtype=FR), take("a_low", 4, SEQ, dtype=FR)
    assert at <= H_LOW
    v_in, g_in, p_in = ([k.sem(f"{x}_in{r}") for r in range(4)] for x in "vgp")
    v_high_ready, v_split, gated, a_high_ready, a_split, out_summed, x_added = (
        k.sem("value_" + x) for x in ("v_high_ready", "v_split", "gated", "a_high_ready", "a_split", "out_summed", "x_added"))
    times = N_KEYS // 8
    v_rows = t["expert_v"].rearrange("(e c) d -> c e d", c=N_KEYS)

    def loaded(it, r):
        return it * 32 + 16 * (r // 4 + 1)

    with nc.Block() as block:
        @block.sync
        def _(sp):
            with sp.Fori(0, times) as it:
                for r in EIGHT:
                    c = it * 8 + r
                    sp.wait_ge(v_split, it * 8 + (r + 1))
                    sp.dma_start(v_raw[r % 4][:, :], v_rows[c]).then_inc(v_in[r % 4], 16)
                    sp.wait_ge(gated, it * 8 + (r + 1))
                    sp.dma_start(g_slot[r % 4][:, :], f.gates[c]).then_inc(g_in[r % 4], 16)
                    sp.dma_start(p_slot[r % 4][:, :], f.gelu[c]).then_inc(p_in[r % 4], 16)

        @block.scalar
        def _(act):
            with act.Fori(0, times) as it:
                for r in EIGHT:
                    act.wait_ge(v_in[r % 4], loaded(it, r))
                    act.wait_ge(out_summed, it * 32 + (r // pair * KD + KD))
                    nc.scalar.activation(v_high[r % 4][:, :], v_raw[r % 4][:, :], ACT.Copy).then_inc(v_high_ready, 1)
                    act.wait_ge(gated, it * 8 + (4 + r + 1))
                    nc.scalar.activation(a_high[r % 4][:, :], a_full[r % 4][:, :], ACT.Copy).then_inc(a_high_ready, 1)

        @block.gpsimd
        def _(pool):
            pool.sem_inc(v_split, 4)
            with pool.Fori(0, times) as it:
                for r in EIGHT:
                    pool.wait_ge(v_high_ready, it * 8 + (r + 1))
                    nc.gpsimd.tensor_tensor(v_low[r % 4][:, :], v_raw[r % 4][:, :], v_high[r % 4][:, :].bitcast(F32), ALU.subtract).then_inc(v_split, 1)

        @block.tensor
        def _(pe):
            pe.sem_inc(out_summed, 2 * KD)
            with pe.Fori(0, times) as it:
                for q in range(quads):
                    pe.wait_ge(v_split, it * 8 + (4 + (q + 1) * pair))
                    pe.wait_ge(a_split, it * 8 + (q + 1) * pair)
                    for d in range(KD):
                        pe.wait_ge(x_added, it * 32 + (q * KD + d + 1))
                        for j in range(pair):
                            r = (q * pair + j) % 4
                            s = slice(d * P, (d + 1) * P)
                            mm = split_product(nc, k.psum[:, d, :], v_high[r][:, s], v_low[r][:, s], a_high[r][:, :], a_low[r][:, :],
                                               j == 0, j == pair - 1)
                        mm.then_inc(out_summed, 1)

        @block.vector
        def _(dve):
            dve.sem_inc(gated, 4)
            dve.sem_inc(x_added, KD)

            def prepare(it, q):
                for r in range(q * pair, (q + 1) * pair):
                    dve.wait_ge(p_in[r % 4], loaded(it, r))
                    dve.wait_ge(g_in[r % 4], loaded(it, r))
                    nc.vector.tensor_tensor(a_full[r % 4][:, :], p_slot[r % 4][:, :], g_slot[r % 4][:, :], ALU.mult).then_inc(gated, 1)
                for r in range(q * pair, (q + 1) * pair):
                    dve.wait_ge(a_high_ready, it * 8 + (r + 1))
                    nc.vector.tensor_tensor(a_low[r % 4][:, :], a_full[r % 4][:, :], a_high[r % 4][:, :].bitcast(F32), ALU.subtract).then_inc(a_split, 1)

            def add(it, q):
                for d in range(KD):
                    dve.wait_ge(out_summed, it * 32 + (2 * KD + q * KD + d + 1))
                    x = k.xT[:, d, 0:SEQ]
                    nc.vector.tensor_tensor(x, x, k.psum[:, d, :], ALU.add).then_inc(x_added, 1)

            prepare(0, 0)
            prepare(0, 1)
            with dve.Fori(0, times - 1) as it:
                for q in range(quads):
                    add(it, q)
                    prepare(it, q + 2)
            for q in range(quads):
                add(times - 1, q)
                if q + 2 < quads:
                    prepare(times - 1, q + 2)


def peer(k, t):
    f = Peer(k)
    with k.nc.Block() as block:
        product(k, block, t["w_query"], 2 * PEER_HEADS, KD, LATENT, k.h_high, k.h_low, FREE,
                copy_to(k, lambda it, r, i: one(f.qT, it * RING + r, 0, SEQ), LATENT), norm=Norm(k, LATENT, lambda i, c: k.par("norm2_g", c)))
    stage_pick(k, t, f)
    stage_gates(k, f)
    stage_values(k, t, f)
    return f


class Layer:

    def __init__(self, k, i):
        self.qk = k.place(f"qk{i}", BIG, 2 * KD, TOK)
        self.q = self.qk[:, 0:KD, :]
        self.key = self.qk[:, KD:2 * KD, :]
        self.v = k.place(f"v_rows{i}", BIG + 2 * KD * TOK, ALL_TILES, D)


def mod_col(k, layer, which, c, piece):
    return k.modT[:, bass.ds(c + (layer * MODS + which * KD), 1), piece]


def modulated_norm(k, layer, name, first, pieces):
    def gains(dve):
        j = layer * MODS + (first + 1) * KD
        for i in range(2):
            k.dve(dve, k.nc.vector.tensor_tensor(k.gain[:, i, :], k.par(name, layer * KD, KD), k.modT[:, j:j + KD, i], ALU.mult))

    return Norm(k, pieces, lambda i, c: k.gain[:, i, c:c + 1], lambda i, c: mod_col(k, layer, first, c, i), gains)


class NaTable:
    BY_LOAD = 4

    def __init__(self, k, t, tab):
        self.k, self.nc, self.rows, self.tab = k, k.nc, t["rpb_rows"], tab
        self.loaded = [k.sem(f"na_table_in{i}") for i in range(NA_HEADS // self.BY_LOAD)]
        self.cleared = k.sem("na_table_cleared")
        self.by_vector = (3,)

    def load(self, sp):
        sp.wait_ge(self.cleared, 2)
        for h in range(NA_HEADS):
            for half in range(2):
                row = bass.AP(self.rows.tensor, h * RPB_H * GRID_W * P + GRID_W - 1, [[P - 1, GRID_W], [GRID_W * P, RPB_H], [1, GRID_W]])
                sp.dma_start(self.tab[half * HEAD:(half + 1) * HEAD, h, half:half + RPB_H, :], row).then_inc(self.loaded[h // self.BY_LOAD], 16)

    def mask(self, eng, which, i):
        window = self.k.const("window").unsqueeze(1).to_broadcast([P, RPB_H + 1, GRID_W])
        eng.wait_ge(self.loaded[i], 2 * 16 * self.BY_LOAD)
        for h in range(i * self.BY_LOAD, (i + 1) * self.BY_LOAD):
            which.tensor_tensor(self.tab[:, h, :, :], self.tab[:, h, :, :], window, ALU.add)

    def tensor(self, pe):
        pass

    def vector_first(self, dve):
        pass

    def gpsimd(self, pool):
        for s in (0, RPB_H):
            self.nc.gpsimd.memset(self.tab[:, :, s, :], 0.0).then_inc(self.cleared, 1)
        for i in range(len(self.loaded)):
            if i not in self.by_vector:
                self.mask(pool, self.nc.gpsimd, i)

    def vector_last(self, dve):
        for i in self.by_vector:
            self.mask(dve, self.nc.vector, i)


def na_layer(k, t, layer):
    b = Layer(k, layer)
    both = PIECES
    with k.nc.Block() as block:
        product(k, block, t["na_qk"], 2 * KD, KD, both, k.h_high, k.h_low, FREE,
                copy_to(k, lambda it, r, i: one(b.qk, it * RING + r, *both[i]), both), norm=modulated_norm(k, layer, "g_attn", 0, both))
    stage_rows(k, t["na_v"], 2, BANK, ALL_TILES, lambda n, i: [(b.v[:, i, n * BANK:(n + 1) * BANK], 0, BANK)], FREE)
    tab = k.place("na_tab", FREE, NA_HEADS, RPB_H + 1, GRID_W)
    stage_head_norm(k, t, "na_norm", [(x[:, c, :], both, k.par(g)) for x, g in ((b.q, "na_gq"), (b.key, "na_gk")) for c in range(KD)],
                    H_HIGH, FREE + NA_HEADS * (RPB_H + 1) * GRID_W, NaTable(k, t, tab))
    behind = FREE + NA_HEADS * (RPB_H + 1) * GRID_W
    sets = [[k.place(f"na_{s}{i}", set_at[j], TOK) for j, s in enumerate(("qs", "ks", "vs"))]
            for i, set_at in enumerate(((H_HIGH, H_HIGH + TOK, H_HIGH + 2 * TOK), (behind, behind + TOK, PICKS_AT)))]
    by_tile = lambda vs: vs[:, :].rearrange("p (t d) -> p t d", d=P)

    def units(s):
        qs, ks, vs = sets[s]
        v = by_tile(vs)
        made = []
        for half in range(2):
            h = slice(half * HEAD, (half + 1) * HEAD)
            context = (ks[h, SEQ:TOK], CTX)
            for i in range(TILES):
                made.append((qs[h, i * P:(i + 1) * P], [(ks[h, 0:SEQ], SEQ), context],
                             lambda g, half=half, i=i: tab[:, bass.ds(g * 2 + half, 1), 7 - 2 * i:15 - 2 * i, :].rearrange("p o s c -> p (o s c)"),
                             lambda j, h=h: v[:, j, h], k.psum[h, 6, i * P:(i + 1) * P]))
            for i in range(CTX // P):
                made.append((qs[h, SEQ + i * P:SEQ + (i + 1) * P], [context], None,
                             lambda j, h=h: v[:, TILES + j, h], k.psum[h, 7, i * P:(i + 1) * P]))
        return made

    def stages(g, s):
        qs, ks, vs = sets[s]
        return [(qs[:, :], one(b.q, g, 0, TOK)), (ks[:, :], one(b.key, g, 0, TOK)), (by_tile(vs), b.v[:, :, bass.ds(g * P, P)])]

    stage_attention(k, "na", NA_HEADS // 2, units, stages,
                    lambda g: [(one(b.q, g, t0, n), k.psum[:, 6 + i, 0:n]) for i, (t0, n) in enumerate(both)], H_HIGH + 3 * TOK, PICKS_AT + TOK)
    with k.nc.Block() as block:
        high, low = split_of_q(k, "na", layer)
        product(k, block, t["na_o"], KD, KD, both, high, low, FREE, add_to_x(k, lambda c, i: mod_col(k, layer, 2, c, i), both), full=b.q)


def split_of_q(k, name, layer):
    return k.place(f"{name}_o_high", H_HIGH, KD, TOK, dtype=FR), k.place(f"{name}_o_low", BIG, KD, TOK, dtype=FR)


def stage_rope(k, t, jobs, at):
    nc = k.nc
    rope = k.place("rope", at, 2, SEQ)
    part = k.place("rope_part", at + 2 * SEQ, 2, SEQ)
    rope_in, swapped, turned = (k.sem("rope_" + s) for s in ("in", "swapped", "turned"))
    with nc.Block() as block:
        @block.sync
        def _(sp):
            sp.dma_start(rope[:, :, :], t["rope"]).then_inc(rope_in, 16)

        @block.tensor
        def _(pe):
            for j, x in enumerate(jobs):
                if j >= 8:
                    pe.wait_ge(turned, j - 7)
                nc.tensor.matmul(k.psum[:, j % 8, :], k.const("swap"), x, start=True, stop=True).then_inc(swapped, 1)

        @block.vector
        def _(dve):
            dve.wait_ge(rope_in, 16)
            for j, x in enumerate(jobs):
                dve.wait_ge(swapped, j + 1)
                k.dve(dve, nc.vector.tensor_tensor(part[:, j % 2, :], k.psum[:, j % 8, :], rope[:, 1, :], ALU.mult))
                k.dve(dve, nc.vector.tensor_tensor(x, x, rope[:, 0, :], ALU.mult))
                nc.vector.tensor_tensor(x, x, part[:, j % 2, :], ALU.add).then_inc(turned, 1)


def swa_layer(k, t, layer):
    b = Layer(k, layer)
    both = PIECES
    with k.nc.Block() as block:
        product(k, block, t["swa_q"], KD, KD, LATENT, k.h_high, k.h_low, FREE, copy_to(k, lambda it, r, i: one(b.q, it * RING + r, 0, SEQ), LATENT),
                norm=modulated_norm(k, layer, "g_attn", 0, both))
    with k.nc.Block() as block:
        product(k, block, t["swa_k"], KV_HEADS, KD, both, k.h_high, k.h_low, FREE, copy_to(k, lambda it, r, i: one(b.key, it * RING + r, *both[i]), both))
    width = KV_HEADS * HEAD
    stage_rows(k, t["swa_v"], 1, width, ALL_TILES, lambda n, i: [(b.v[:, i, 0:width], 0, width)], FREE)
    stage_head_norm(k, t, "swa_norm", [(b.q[:, c, :], LATENT, k.par("swa_gq")) for c in range(KD)]
                    + [(b.key[:, c, :], both, k.par("swa_gk")) for c in range(KV_HEADS)], FREE, H_HIGH)
    stage_rope(k, t, [b.q[:, c, 0:SEQ] for c in range(KD)] + [b.key[:, c, 0:SEQ] for c in range(KV_HEADS)], FREE)
    per = 2
    set_size = per * SEQ + TOK + ALL_TILES * HEAD + 2 * per + 4
    sets = []
    for i in range(2):
        o = FREE + i * set_size
        sets.append((k.place(f"swa_qs{i}", o, per, SEQ), k.place(f"swa_ks{i}", o + per * SEQ, TOK),
                     k.place(f"swa_vs{i}", o + per * SEQ + TOK, ALL_TILES, HEAD),
                     k.place(f"swa_sinks{i}", o + per * SEQ + TOK + ALL_TILES * HEAD, 2 * per)))

    def units(s):
        qs, ks, vs, _ = sets[s]
        made = []
        for qc in range(per):
            for half in range(2):
                h = slice(half * HEAD, (half + 1) * HEAD)
                for i in range(TILES):
                    lo, hi = max(0, i - 1), min(TILES, i + 2)
                    n = (hi - lo) * P
                    y = (lo - (i - 1)) * P
                    made.append((qs[h, qc, i * P:(i + 1) * P], [(ks[h, lo * P:hi * P], n), (ks[h, SEQ:TOK], CTX)],
                                 lambda g, y=y, n=n: k.const("band")[:, y:y + n],
                                 lambda j, lo=lo, hi=hi: vs[:, lo + j if j < hi - lo else TILES + j - (hi - lo), :],
                                 k.psum[h, 6 + qc, i * P:(i + 1) * P]))
        return made

    def sink(u):
        s, head = u // (2 * per * TILES), u // TILES % (2 * per)
        return sets[s][3][:, head:head + 1]

    def stages(g, s):
        qs, ks, vs, sinks = sets[s]
        return [(qs[:, :, :], b.q[:, bass.ds(g * per, per), 0:SEQ]), (ks[:, :], one(b.key, g, 0, TOK)),
                (vs[:, :, :], b.v[:, :, bass.ds(g * HEAD, HEAD)]), (sinks[:, :], k.par("sink", g * (2 * per), 2 * per))]

    stage_attention(k, "swa", KV_HEADS, units, stages,
                    lambda g: [(one(b.q, g * per + c, 0, SEQ), k.psum[:, 6 + c, :]) for c in range(per)], FREE + 2 * set_size, PICKS_AT, sink)
    with k.nc.Block() as block:
        high, low = split_of_q(k, "swa", layer)
        product(k, block, t["swa_o"], KD, KD, LATENT, high, low, FREE, add_to_x(k, lambda c, i: mod_col(k, layer, 2, c, i), LATENT), full=b.q)


def conv_ffn(k, t, layer, pieces):
    nc = k.nc
    act_T = k.place(f"ffn_act{layer}", BIG, FF_CHUNKS, TOK)
    at = BIG + FF_CHUNKS * TOK
    conv = k.place(f"ffn_conv{layer}", at, 2, 2, TOK)
    conv_done, silu_done = k.sem(f"ffn_conv_done{layer}"), k.sem(f"ffn_silu_done{layer}")
    width = sum(n for _, n in pieces)
    np_ = len(pieces)

    def epilogue(dve, it, r, banks):
        pair, gate = r // 2, r % 2
        j = it * RING + (layer * 2 * FF_CHUNKS + r)
        tap = lambda i: k.par("ffn_w", j * 3 + i)
        o = conv[:, pair, gate, :]
        for (t0, n), bank in zip(pieces, banks):
            k.dve(dve, nc.vector.tensor_scalar(o[:, t0:t0 + n], bank, tap(1), k.par("ffn_b", j), ALU.mult, ALU.add))
        for (t0, n), bank in zip(pieces, banks):
            k.dve(dve, nc.vector.scalar_tensor_tensor(o[:, t0 + 1:t0 + n], bank[:, 0:n - 1], tap(0), o[:, t0 + 1:t0 + n], ALU.mult, ALU.add))
        for (t0, n), bank in zip(pieces, banks):
            nc.vector.scalar_tensor_tensor(o[:, t0:t0 + n - 1], bank[:, 1:n], tap(2), o[:, t0:t0 + n - 1], ALU.mult, ALU.add).then_inc(k.bank_read.sem, 1)
        dve.wait_ge(k.bank_read.sem, k.bank_read.at((it * RING + (RING + r + 1)) * np_))
        if gate:
            dve.sem_inc(conv_done, 1)
            dve.wait_ge(silu_done, it * 2 + (pair + 1))
            k.dve(dve, nc.vector.tensor_tensor(act_T[:, bass.ds(it * 2 + pair, 1), 0:width].rearrange("p o y -> p (o y)"),
                                               conv[:, pair, 0, 0:width], conv[:, pair, 1, 0:width], ALU.mult))

    def silu(act, it, r):
        if r % 2:
            g = conv[:, r // 2, 1, 0:width]
            act.wait_ge(conv_done, it * 2 + (r // 2 + 1))
            nc.scalar.activation(g, g, ACT.Silu).then_inc(silu_done, 1)

    with nc.Block() as block:
        product(k, block, t[f"ffn_up{layer}"], 2 * FF_CHUNKS, KD, pieces, k.h_high, k.h_low, at + 4 * TOK, epilogue, silu,
                norm=modulated_norm(k, layer, "g_ffn", 3, pieces))
    high, low = k.place(f"ffn_high{layer}", at, FF_CHUNKS, TOK, dtype=FR), k.place(f"ffn_low{layer}", BIG, FF_CHUNKS, TOK, dtype=FR)
    with nc.Block() as block:
        product(k, block, t[f"ffn_down{layer}"], KD, FF_CHUNKS, pieces, high, low, at + FF_CHUNKS * TOK,
                add_to_x(k, lambda c, i: mod_col(k, layer, 5, c, i), pieces, RING // 2), full=act_T, parts=2, split_at=H_HIGH)


def stage_store(k, out):
    stored = k.sem("stored")
    with k.nc.Block() as block:
        @block.sync
        def _(sp):
            sp.dma_start(out, k.xT[:, :, 0:SEQ]).then_inc(stored, 16)
            sp.wait_ge(stored, 16)


def build(nc, t, out):
    k = Core(nc)
    stage_load(k, t)
    first_block(k, t)
    peer(k, t)
    na_layer(k, t, 0)
    conv_ffn(k, t, 0, PIECES)
    swa_layer(k, t, 1)
    conv_ffn(k, t, 1, LATENT)
    stage_store(k, out)


def outside_window():
    qc, kc = np.arange(P)[:, None] % GRID_W, np.arange(GRID_W)[None]
    start = np.clip(qc - 8, 0, GRID_W - 16)
    return np.where((kc >= start) & (kc < start + 16), 0, NEG)


def constants():
    f = np.float32
    p, x = np.arange(P)[:, None], np.arange(P)[None, :]
    parts = dict(
        ident=p == x, tri=p <= x, ones=np.ones((P, P)), iota=np.broadcast_to(x, (P, P)),
        heads=np.arange(HEAD)[None] == HEADS_AT_ONCE - 2 + p // HEAD, window=outside_window(), swap=p == (x // HEAD) * HEAD + (x % HEAD + HEAD // 2) % HEAD,
        causal=np.where(x <= p, 0, NEG), iota16=np.broadcast_to(np.arange(TOPK)[None], (P, TOPK)),
        band=np.where(np.abs(p + P - np.arange(3 * P)[None]) <= RADIUS, 0, NEG))
    consts = np.concatenate([np.asarray(parts[n], f) for n in CONST_SIZES], 1)
    pick = np.zeros((UNITS, UNITS, P), f)
    pick[np.arange(UNITS), np.arange(UNITS)] = 1
    dist = SEQ - 1 - np.arange(SEQ + P)
    exact = N_BUCKETS // 2
    ratio = np.log(np.maximum(dist, 1).astype(f) / f(exact)) / np.log(2048 / exact)
    large = np.minimum(exact + (ratio * (N_BUCKETS - exact)).astype(np.int32), N_BUCKETS - 1)
    bucket = np.where(dist < exact, dist, large)
    hot = np.zeros((N_BUCKETS + 1, SEQ + P), f)
    ok = dist >= 0
    hot[bucket[ok], np.nonzero(ok)[0]] = 1
    count = (dist <= 128).astype(int) + (dist % 4 == 0) + (dist % 16 == 0)
    hot[N_BUCKETS] = np.where(ok & (count > 0), np.log(np.maximum(count, 1)), NEG)
    spread = np.arange(HEADS_AT_ONCE)[:, None, None] == 2 * np.arange(HEADS_AT_ONCE // 2)[None, :, None] + p.T[None] // HEAD
    tok = np.arange(SEQ)
    inv = (10000.0 ** (-np.arange(16, dtype=f) / f(16))).astype(f)
    ang = np.concatenate([(tok // GRID_W).astype(f)[:, None] * inv, (tok % GRID_W).astype(f)[:, None] * inv], 1)
    d = np.arange(P) % HEAD
    cos = np.cos(ang)[:, d % 32].T.astype(f)
    sin = (np.sin(ang)[:, d % 32] * np.where(d < 32, -1, 1)).T.astype(f)
    return dict(consts=consts, pick=pick, bucket_hot=hot, spread=spread.astype(f).reshape(HEADS_AT_ONCE, -1), rope=np.stack([cos, sin], 1))


def layouts(a):
    cc = np.ascontiguousarray

    def chunks(w):
        kk, n = w.shape
        return cc(w.reshape(kk // P, P, n // P, P).transpose(2, 1, 0, 3)).reshape(n // P, P, -1)

    def blocks(w, width):
        kk, n = w.shape
        return cc(w.reshape(kk // P, P, n // width, width).transpose(2, 1, 0, 3)).reshape(n // width, P, -1)

    def cols(v):
        return v.reshape(-1, P).T

    def rows(v):
        return np.broadcast_to(v.reshape(1, -1), (P, v.size))

    def ff(v):
        return v.reshape(*v.shape[:-1], 2, FF_CHUNKS, P).swapaxes(-3, -2)

    w_in = a["w_in"][0]
    mw, aw = M_HEADS * P, DIL_HEADS * HEAD
    u, vm, z, gates = w_in[:, 0:mw], w_in[:, mw:2 * mw], w_in[:, 2 * mw:3 * mw], w_in[:, 3 * mw:3 * mw + 2 * M_HEADS]
    at = 3 * mw + 2 * M_HEADS
    qa, ka, va = (w_in[:, at + i * aw:at + (i + 1) * aw] for i in range(3))
    qkv = a["swa_w_qkv_2"][0]
    swa_k = qkv[:, D:D + KV_HEADS * HEAD].reshape(D, KV_HEADS, 1, HEAD)
    swa_k = np.broadcast_to(swa_k, (D, KV_HEADS, 2, HEAD)).reshape(D, -1)
    na = a["na_w_qkv_2"][0]
    rpb = a["na_rpb_2"][0]
    rpb_rows = np.pad(rpb, ((0, 0), (0, 0), (GRID_W - 16, P - RPB_W - (GRID_W - 16))))
    rpb_rows = np.broadcast_to(rpb_rows[:, :, None], (NA_HEADS, RPB_H, GRID_W, P))
    parts = dict(
        norm1_g=cols(a["norm1_g"][0]), conv_w=a["conv_w"][0].reshape(4, M_HEADS, P).transpose(2, 1, 0).reshape(P, -1),
        conv_b=cols(a["conv_b"][0]), mh_g=cols(a["mh_norm_g"][0]), skip=cols(a["skip_m"][0]), qn_g=cols(a["qn_g"][0]),
        kn_g=cols(a["kn_g"][0]), norm2_g=cols(a["norm2_g"][0]), gate_b=rows(np.concatenate([a["ig_b"][0], a["fg_b"][0]])),
        g_attn=cols(a["g_attn_2"]), g_ffn=cols(a["g_ffn_2"]), b_mod=cols(a["b_mod_2"]),
        na_gq=np.tile(a["na_g_q_2"][0], 2)[:, None], na_gk=np.tile(a["na_g_k_2"][0], 2)[:, None],
        swa_gq=np.tile(a["swa_g_q_2"][0], 2)[:, None], swa_gk=np.tile(a["swa_g_k_2"][0], 2)[:, None],
        sink=rows(a["swa_sink_2"][0]),
        ffn_w=ff(a["ffn_conv_w_2"]).transpose(4, 0, 2, 3, 1).reshape(P, -1),
        ffn_b=ff(a["ffn_conv_b_2"]).transpose(3, 0, 1, 2).reshape(P, -1))
    out = dict(constants())
    out.update(
        xT=cc(a["x"][0].T.reshape(KD, P, SEQ).transpose(1, 0, 2)), ctxT=cc(a["ctx_2"][0].T.reshape(KD, P, CTX).transpose(1, 0, 2)),
        params=cc(np.concatenate([parts[n] for n in PARAM_SIZES], 1)),
        w_mod=cc(np.concatenate(list(a["w_mod_2"]), 1).T).reshape(LAYERS * MODS, P, D), cond=cc(rows(np.stack([a["c_2"][0], a["c_ctx_2"]]))),
        w_projT=chunks(np.concatenate([u, z, qa, ka], 1)), w_projV=blocks(np.concatenate([vm, va, gates], 1), (2 * BANK + 2 * M_HEADS) // 3),
        w_qk=cc(np.stack([a["wq_m"][0], a["wk_m"][0]]).transpose(2, 0, 1, 3)),
        rel_bias=a["rel_bias"], w_out=chunks(a["w_out"][0]), w_query=chunks(a["w_query"][0]),
        keys=cc(np.stack([a["sub_keys1"][0], a["sub_keys2"][0]]).transpose(3, 1, 0, 2)).reshape(P, -1),
        expert_uT=cc(a["expert_u"][0].reshape(N_KEYS, N_KEYS, KD, P).transpose(1, 3, 2, 0)).reshape(N_KEYS, P, -1),
        expert_v=a["expert_v"][0],
        na_qk=chunks(na[:, 0:2 * D]), na_v=blocks(na[:, 2 * D:], BANK), na_o=chunks(a["na_w_o_2"][0]), rpb_rows=rpb_rows,
        swa_q=chunks(qkv[:, 0:D]), swa_k=chunks(swa_k), swa_v=blocks(qkv[:, D + KV_HEADS * HEAD:], KV_HEADS * HEAD),
        swa_o=chunks(a["swa_w_o_2"][0]))
    for i in range(LAYERS):
        out[f"ffn_up{i}"] = chunks(ff(a["ffn_w_up_2"][i]).reshape(D, -1))
        out[f"ffn_down{i}"] = chunks(a["ffn_w_down_2"][i])
    return {n: cc(v) for n, v in out.items()}


def kernel(**inputs):
    import concourse.bacc as bacc
    from concourse.bass_utils import run_bass_kernel_spmd as run

    arrays = layouts({n: np.asarray(v) for n, v in inputs.items()})
    nc = bacc.Bacc("TRN2", target_bir_lowering=False, num_devices=1)
    t = {n: nc.dram_tensor(f"in_{n}", v.shape, mybir.dt.from_np(v.dtype), kind="ExternalInput").ap() for n, v in arrays.items()}
    out = nc.dram_tensor("out_xT", (P, KD, SEQ), F32, kind="ExternalOutput").ap()
    build(nc, t, out)
    got = run(nc, [{f"in_{n}": v for n, v in arrays.items()}], core_ids=[0]).results[0]["out_xT"]
    return np.ascontiguousarray(np.asarray(got).transpose(1, 0, 2).reshape(D, SEQ).T)[None]
```
